# Optimizing a Trainium2 kernel written in Bass

```python
import jax, jax.numpy as jnp
from jax import lax
import numpy as np

D_MODEL = 1024
BATCH = 1
SEQ = 2048
DEPTH = 2

HEAD_DIM = 64
NORM_EPS = 1e-6
GM_HEADS = 4
GM_WIDTH = GM_HEADS * HEAD_DIM
GM_CHUNK = 128
GLA_HEADS = 4
GLA_DV = HEAD_DIM
GLA_DK = HEAD_DIM // 2
GLA_WIDTH = GLA_HEADS * GLA_DV
GLA_KEY_WIDTH = GLA_HEADS * GLA_DK
GLA_GATE_RANK = 16
GLA_TAU = 16.0
GLA_CHUNK = 16
SWA_Q_HEADS = 8
SWA_KV_HEADS = 2
SWA_GROUP = SWA_Q_HEADS // SWA_KV_HEADS
SWA_WIDTH = SWA_Q_HEADS * HEAD_DIM
SWA_KV_WIDTH = SWA_KV_HEADS * HEAD_DIM
SWA_WINDOW = 128
SWA_BLOCK = 128
ROPE_THETA = 10000.0
D_MIX = GM_WIDTH + GLA_WIDTH + SWA_WIDTH
IN_SPLITS = (GM_WIDTH, GM_WIDTH, GM_WIDTH,
             GLA_KEY_WIDTH, GLA_KEY_WIDTH, GLA_WIDTH,
             GLA_GATE_RANK, GLA_WIDTH,
             SWA_WIDTH, SWA_KV_WIDTH, SWA_KV_WIDTH, SWA_WIDTH)
D_IN = 3 * GM_WIDTH + 2 * GLA_KEY_WIDTH + 2 * GLA_WIDTH + GLA_GATE_RANK + 2 * SWA_WIDTH + 2 * SWA_KV_WIDTH

kernel_name = "hybrid_sgu_gla_swa_sink_block"

def rms_norm(x, g):
    xf = x.astype(jnp.float32)
    y = xf * lax.rsqrt(jnp.mean(xf * xf, axis=-1, keepdims=True) + NORM_EPS)
    return (y * g.astype(jnp.float32)).astype(x.dtype)

def layer_norm(x, g, b):
    xf = x.astype(jnp.float32)
    mu = jnp.mean(xf, axis=-1, keepdims=True)
    xc = xf - mu
    y = xc * lax.rsqrt(jnp.mean(xc * xc, axis=-1, keepdims=True) + NORM_EPS)
    return (y * g.astype(jnp.float32) + b.astype(jnp.float32)).astype(x.dtype)

def rope(x, positions):
    d = x.shape[-1]
    half = d // 2
    inv_freq = jnp.power(ROPE_THETA, -jnp.arange(half, dtype=jnp.float32) * 2.0 / d)
    ang = positions.astype(jnp.float32)[..., None] * inv_freq
    cos = jnp.cos(ang)[:, :, None, :]
    sin = jnp.sin(ang)[:, :, None, :]
    xf = x.astype(jnp.float32)
    x1, x2 = xf[..., :half], xf[..., half:]
    return jnp.concatenate([x1 * cos - x2 * sin, x2 * cos + x1 * sin], axis=-1).astype(x.dtype)

def spatial_gating(u, v, ln_g, ln_b, ws, bs):
    b, s, _ = u.shape
    nc = s // GM_CHUNK
    v = layer_norm(v, ln_g, ln_b)
    vc = v.reshape(b, nc, GM_CHUNK, GM_HEADS, HEAD_DIM)
    causal = jnp.tril(jnp.ones((GM_CHUNK, GM_CHUNK), dtype=bool))
    w = jnp.where(causal[None], ws, 0.0).astype(vc.dtype)
    sv = jnp.einsum('htc,bnchd->bnthd', w, vc) + bs.T.astype(vc.dtype)[:, :, None]
    return u * sv.reshape(b, s, GM_WIDTH)

def gated_linear_attention(q, k, v, g_low, wg2, bg, norm_g):
    b, s, _ = q.shape
    nc, L = s // GLA_CHUNK, GLA_CHUNK
    f32 = jnp.float32
    q = q.astype(f32).reshape(b, nc, L, GLA_HEADS, GLA_DK) * (GLA_DK ** -0.5)
    k = k.astype(f32).reshape(b, nc, L, GLA_HEADS, GLA_DK)
    v = v.astype(f32).reshape(b, nc, L, GLA_HEADS, GLA_DV)
    logit = jnp.einsum('bsr,rc->bsc', g_low.astype(f32), wg2.astype(f32)) + bg.astype(f32)
    log_a = jax.nn.log_sigmoid(logit) / GLA_TAU
    G = jnp.cumsum(log_a.reshape(b, nc, L, GLA_HEADS, GLA_DK), axis=2)
    causal = jnp.tril(jnp.ones((L, L), dtype=bool))[:, :, None, None]
    diff = G[:, :, :, None] - G[:, :, None, :]
    decay = jnp.where(causal, jnp.exp(jnp.where(causal, diff, 0.0)), 0.0)
    attn = jnp.einsum('bnthk,bnshk,bntshk->bnhts', q, k, decay)
    o_intra = jnp.einsum('bnhts,bnshv->bnthv', attn, v)
    G_last = G[:, :, -1]
    k_dec = k * jnp.exp(G_last[:, :, None] - G)
    U = jnp.einsum('bnshk,bnshv->bnhkv', k_dec, v)
    chunk_decay = jnp.exp(G_last)

    def step(state, inp):
        a, u_n = inp
        return a[..., None] * state + u_n, state

    s0 = jnp.zeros((b, GLA_HEADS, GLA_DK, GLA_DV), f32)
    _, s_prev = lax.scan(step, s0, (jnp.moveaxis(chunk_decay, 1, 0), jnp.moveaxis(U, 1, 0)))
    s_prev = jnp.moveaxis(s_prev, 0, 1)
    o_inter = jnp.einsum('bnthk,bnhkv->bnthv', q * jnp.exp(G), s_prev)
    o = (o_intra + o_inter).reshape(b, s, GLA_HEADS, GLA_DV)
    o = rms_norm(o, norm_g)
    return o.reshape(b, s, GLA_WIDTH)

def sliding_window_attention(q, k, v, sinks, positions):
    b, s, _ = q.shape
    T = SWA_BLOCK
    nb = s // T
    q = rope(q.reshape(b, s, SWA_Q_HEADS, HEAD_DIM), positions)
    k = rope(k.reshape(b, s, SWA_KV_HEADS, HEAD_DIM), positions)
    v = v.reshape(b, s, SWA_KV_HEADS, HEAD_DIM)
    qb = q.reshape(b, nb, T, SWA_KV_HEADS, SWA_GROUP, HEAD_DIM)

    def band(t):
        tp = jnp.pad(t, ((0, 0), (T, 0), (0, 0), (0, 0))).reshape(b, nb + 1, T, SWA_KV_HEADS, HEAD_DIM)
        return jnp.concatenate([tp[:, :-1], tp[:, 1:]], axis=2)

    kb, vb = band(k), band(v)
    scores = jnp.einsum('bnqhgd,bnkhd->bnhgqk', qb, kb).astype(jnp.float32) * (HEAD_DIM ** -0.5)
    qpos = jnp.arange(nb)[:, None] * T + jnp.arange(T)[None, :]
    kpos = (jnp.arange(nb)[:, None] - 1) * T + jnp.arange(2 * T)[None, :]
    rel = qpos[:, :, None] - kpos[:, None, :]
    mask = (rel >= 0) & (rel < SWA_WINDOW) & (kpos[:, None, :] >= 0)
    scores = jnp.where(mask[None, :, None, None], scores, -jnp.inf)
    sink = jnp.broadcast_to(sinks.astype(jnp.float32).reshape(1, 1, SWA_KV_HEADS, SWA_GROUP, 1, 1),
                            scores.shape[:-1] + (1,))
    probs = jax.nn.softmax(jnp.concatenate([scores, sink], axis=-1), axis=-1)[..., :-1]
    out = jnp.einsum('bnhgqk,bnkhd->bnqhgd', probs.astype(vb.dtype), vb)
    return out.reshape(b, s, SWA_WIDTH)

def hybrid_layer(x, positions, pre_g, w_in, gm_ln_g, gm_ln_b, gm_ws, gm_bs,
                 gla_wg2, gla_bg, gla_norm_g, swa_sinks, w_out, post_g):
    h = rms_norm(x, pre_g)
    proj = jnp.einsum('bsd,dc->bsc', h, w_in)
    split_points = np.cumsum(IN_SPLITS)[:-1].tolist()
    (gm_u, gm_v, gm_z, gla_q, gla_k, gla_v, gla_glr, gla_z,
     swa_q, swa_k, swa_v, swa_z) = jnp.split(proj, split_points, axis=-1)
    y_a = spatial_gating(gm_u, gm_v, gm_ln_g, gm_ln_b, gm_ws, gm_bs) * jax.nn.silu(gm_z)
    y_b = gated_linear_attention(gla_q, gla_k, gla_v, gla_glr, gla_wg2, gla_bg,
                                 gla_norm_g).astype(x.dtype) * jax.nn.silu(gla_z)
    y_c = sliding_window_attention(swa_q, swa_k, swa_v, swa_sinks, positions) * jax.nn.silu(swa_z)
    y = jnp.einsum('bsc,cd->bsd', jnp.concatenate([y_a, y_b, y_c], axis=-1), w_out)
    return x + rms_norm(y, post_g)

def setup_inputs(seed: int = 0) -> dict:
    key = jax.random.key(seed)
    ks = jax.random.split(key, 16)
    f32 = jnp.float32
    x = jax.random.normal(ks[0], (BATCH, SEQ, D_MODEL), f32)
    positions = jnp.broadcast_to(jnp.arange(SEQ, dtype=jnp.int32)[None, :], (BATCH, SEQ))
    pre_g = 1.0 + 0.1 * jax.random.normal(ks[1], (DEPTH, D_MODEL), f32)
    w_in = jax.random.normal(ks[2], (DEPTH, D_MODEL, D_IN), f32) * (D_MODEL ** -0.5)
    gm_ln_g = 1.0 + 0.1 * jax.random.normal(ks[3], (DEPTH, GM_WIDTH), f32)
    gm_ln_b = 0.02 * jax.random.normal(ks[4], (DEPTH, GM_WIDTH), f32)
    gm_ws = jax.random.normal(ks[5], (DEPTH, GM_HEADS, GM_CHUNK, GM_CHUNK), f32) * (GM_CHUNK ** -0.5)
    gm_bs = 1.0 + 0.1 * jax.random.normal(ks[6], (DEPTH, GM_HEADS, GM_CHUNK), f32)
    gla_wg2 = jax.random.normal(ks[7], (DEPTH, GLA_GATE_RANK, GLA_KEY_WIDTH), f32) * (GLA_GATE_RANK ** -0.5)
    gla_bg = 0.1 * jax.random.normal(ks[8], (DEPTH, GLA_KEY_WIDTH), f32)
    gla_norm_g = 1.0 + 0.1 * jax.random.normal(ks[9], (DEPTH, GLA_DV), f32)
    swa_sinks = 0.5 * jax.random.normal(ks[10], (DEPTH, SWA_Q_HEADS), f32)
    w_out = jax.random.normal(ks[11], (DEPTH, D_MIX, D_MODEL), f32) * (D_MIX ** -0.5)
    post_g = 1.0 + 0.1 * jax.random.normal(ks[12], (DEPTH, D_MODEL), f32)
    return {"x": x, "positions": positions, "pre_g": pre_g, "w_in": w_in,
            "gm_ln_g": gm_ln_g, "gm_ln_b": gm_ln_b, "gm_ws": gm_ws, "gm_bs": gm_bs,
            "gla_wg2": gla_wg2, "gla_bg": gla_bg, "gla_norm_g": gla_norm_g,
            "swa_sinks": swa_sinks, "w_out": w_out, "post_g": post_g}

def reference(x, positions, pre_g, w_in, gm_ln_g, gm_ln_b, gm_ws, gm_bs,
              gla_wg2, gla_bg, gla_norm_g, swa_sinks, w_out, post_g):
    h = x
    for l in range(DEPTH):
        h = hybrid_layer(h, positions, pre_g[l], w_in[l], gm_ln_g[l], gm_ln_b[l], gm_ws[l], gm_bs[l],
                         gla_wg2[l], gla_bg[l], gla_norm_g[l], swa_sinks[l], w_out[l], post_g[l])
    return h


_drawn_inputs = setup_inputs


def setup_inputs(seed=0):
    import zlib

    import numpy as np

    out = dict(_drawn_inputs(seed))
    spreads = {}
    factors = {'gm_ln_b': 6.582, 'swa_sinks': 8.0}
    for name, (base, spread) in spreads.items():
        noise = np.random.default_rng([zlib.crc32(name.encode()), seed]).standard_normal(out[name].shape)
        drawn = base * np.exp(spread * noise) if base else spread * noise
        out[name] = __import__('jax').numpy.asarray(drawn.astype(out[name].dtype))
    for name, factor in factors.items():
        out[name] = (out[name] * factor).astype(out[name].dtype)
    return out
```

```python
from contextlib import ExitStack

import numpy as np

import concourse.bass as bass
from concourse import mybir

F32 = mybir.dt.float32
F16 = mybir.dt.float16
I32 = mybir.dt.int32
U32 = mybir.dt.uint32
ALU = mybir.AluOpType
ACT = mybir.ActivationFunctionType
AX = mybir.AxisListType
ABSMAX = bass.bass_isa.ReduceOp.max

P = 128
D_MODEL, SEQ, DEPTH = 1024, 2048, 2
NT = SEQ // P
KC = D_MODEL // P
HEAD = 64
EPS = 1e-6
GM, GLA, SWA = 256, 256, 512
GH, GK = 4, 32
GATE_TAU = 16.0
NSUB, SUB = 4, 32
ROPE_THETA = 10000.0

C_U, C_V, C_Z = 0, 256, 512
C_GQ, C_GK, C_GV, C_GL, C_GZ = 768, 896, 1024, 1280, 1296
C_SQ, C_SK, C_SV, C_SZ = 1552, 2064, 2192, 2320
D_IN = 2832
RANK = C_GZ - C_GL
N_CHUNK = 6
CH = D_IN // N_CHUNK
WG = CH // 2
N_WIN = D_IN // WG
OG = 256
N_WOUT = D_MODEL // OG
RAW_W = max(WG, OG)

H_SCALE = 2.0 ** 10
TOP = 2.0 ** 14
NEG = -1.0e30
TINY = 1.0e-30
EXP_BITS = 0x7F800000
ROUND = 12582912.0
TWO_PI_HI, TWO_PI_LO = 6.28125, 0.0019353071795864769
PI_SAFE = 3.1415925


class Stage:

    def __init__(self, sem, steps):
        self.sem = sem
        self.steps = steps.split()
        assert len(set(self.steps)) == len(self.steps)

    def count(self, n, step):
        return n * len(self.steps) + (self.steps.index(step) + 1)


def wait(engine, stage, n, step):
    if isinstance(n, int) and n < 0:
        return
    engine.wait_ge(stage.sem, stage.count(n, step))


def hybrid_trunk(nc, x, positions, pre_g, w_in, gm_ln_g, gm_ln_b, gm_ws, gm_bs, gla_wg2, gla_bg,
                 gla_norm_g, swa_sinks, w_out, post_g, inv_freq, out):
    with ExitStack() as ctx:
        def sb(name, shape, dt=F32):
            return ctx.enter_context(nc.sbuf_tensor(name, shape, dt))

        def bank(name):
            return ctx.enter_context(nc.psum_tensor(name, [P, 512], F32))

        def sem(name):
            return ctx.enter_context(nc.semaphore(name))

        rope_dram = nc.dram_tensor("rope_tables", (NT, P, HEAD), F32, kind="Internal").ap()

        columns = sb("columns", [P, 200])
        used = [0]

        def col(n, *shape):
            at = used[0]
            used[0] += n
            ap = columns[:, at:at + n]
            return ap if not shape else ap.rearrange("p (a b) -> p a b", a=shape[0])

        w_hi = sb("w_hi", [P, KC, D_IN], F16)
        w_lo = sb("w_lo", [P, KC, D_IN], F16)
        wo_hi = sb("wo_hi", [P, KC, D_MODEL], F16)
        wo_lo = sb("wo_lo", [P, KC, D_MODEL], F16)
        raw = sb("raw", [P, 2, KC, RAW_W])
        kmax = col(KC)
        bmax = col(1)
        gmax = col(1)
        wpow = col(2)
        wscale = col(2 * KC, 2)
        unscale_in = col(N_WIN)
        unscale_out = col(N_WOUT)
        preg = col(KC)
        preg_abs = col(KC)
        postg = sb("postg", [P, D_MODEL])
        ln_g = sb("ln_g", [P, GM])
        ln_b = sb("ln_b", [P, GM])
        gm_wT = sb("gm_wT", [P, GH, P])
        gm_bias = col(GH)
        wg2 = sb("wg2", [RANK, P])
        gate_b = col(1)
        norm_g = sb("norm_g", [P, HEAD])
        sinks = col(8)
        ident = sb("ident", [P, P])
        causal = sb("causal", [P, P])
        band = sb("band", [P, 2, 2 * P])
        head_mask = col(GH)
        one = col(1)
        unused = col(1)
        pool_one = col(1)
        neg_half = col(GH)
        xt = sb("xt", [P, D_MODEL])
        h_hi = sb("h_hi", [P, KC, P], F16)
        h_lo = sb("h_lo", [P, KC, P], F16)
        x_stats = col(2 * 6, 2)
        x_mv = col(2)
        x_r = col(1)
        pj = sb("pj", [P, D_IN])
        y = sb("y", [P, D_MODEL])
        s_buf = sb("s_buf", [P, 8 * 2 * P])
        pt = sb("pt", [P, 2 * 4 * P])
        qT = sb("qT", [P, 4, P])
        kT = sb("kT", [P, 2, P])
        vv = sb("vv", [P, 2, P])
        rope = sb("rope", [P, HEAD])
        row_max = col(8)
        neg_max = col(8)
        row_sum = col(8)
        sink_e = col(8)
        denom = col(8)
        g_v = sb("g_v", [P, GLA])
        g_qk = sb("g_qk", [P, 2, P])
        g_low = sb("g_low", [RANK, P])
        gate_a = sb("gate_a", [P, P])
        gate_m = sb("gate_m", [P, P])
        cum = sb("cum", [P, P])
        ref_p = col(NSUB + 1)
        ref_n = col(NSUB)
        k_ref = sb("k_ref", [P, NSUB, P])
        q_ref = gate_m
        q_bd = sb("q_bd", [P, NSUB * GH * SUB])
        decay = sb("decay", [P, P])
        q_dec = decay
        tile_decay = col(1)
        k_dec = sb("k_dec", [P, P])
        k_decN = gate_a
        state = sb("state", [P, GLA])
        update = q_bd[:, 0:GLA]
        mix = sb("mix", [P, GLA])
        o_sum = col(GH)
        o_r = col(GH)
        v_stats = col(6)
        v_mv = col(2)
        v_r = col(1)
        y_max = col(1)
        y_scale = col(1)
        y_unscale = col(1)
        y_parts = pt[:].bitcast(F16).rearrange("p (s k t) -> p s k t", s=2, k=KC)
        y_hi, y_lo = y_parts[:, 0], y_parts[:, 1]
        fac = col(N_WOUT)
        ot = sb("ot", [P, D_MODEL])
        res = sb("res", [P, D_MODEL])
        o_stats = col(2 * 6, 2)
        o_mv = col(2)
        out_r = col(1)

        PJ = [bank("PJ0"), bank("PJ1")]
        TR = [bank("TR0"), bank("TR1")]
        SC = [bank("SC0"), bank("SC1")]
        MX = bank("MX")
        GL = bank("GL")

        s4 = s_buf[:].rearrange("p (g r k) -> p g r k", g=2, r=4)
        xc, xs = s_buf[:, 0:640], s_buf[:, 640:1280]
        roped = s_buf[:, 1280:1920]
        att = s_buf[:, 0:512]
        pt4 = pt[:].rearrange("p (g c q) -> p g c q", g=2, c=4)
        a_mask = q_bd[:].rearrange("p (h t) -> p h t", h=GH)

        def halves(ap, n):
            return ap.rearrange("p (n e d) -> p n e d", n=n, e=2)

        params = sem("params_loaded")
        raw_loaded = [sem("raw_even_loaded"), sem("raw_odd_loaded")]
        x_loaded = sem("x_loaded")
        rope_loaded = sem("rope_loaded")
        rope_stored = sem("rope_stored")
        res_loaded = sem("res_loaded")
        out_stored = sem("out_stored")
        const_ready = sem("const_ready")
        pos_loaded = sem("pos_loaded")
        table_v = sem("rope_table_vector_steps")
        table_a = sem("rope_table_sines")
        layer_state = sem("layer_state_cleared")
        gmw_t = sem("gm_weights_transposed")
        gmw_ready = sem("gm_weights_ready")
        preg_ready = sem("preg_ready")

        NB = N_WIN + N_WOUT
        v_w = Stage(sem("v_w"), "kmax gmul bmax guard bits recip scale unscale mult lo")
        a_w = Stage(sem("a_w"), "hi")
        p_w = Stage(sem("p_w"), "all")

        t_x = Stage(sem("t_x"), "x0 x1")
        a_x = Stage(sem("a_x"), "scale hi0 hi1")
        v_x = Stage(sem("v_x"), "stats aggr msq eps lo0 lo1")
        p_x = Stage(sem("p_x"), "pow")

        t_a = Stage(sem("t_a"), "c0 c1 c2 c3 c4 c5")
        a_a = Stage(sem("a_a"), "c0 c1 c2 c3 c4 c5")

        t_b = Stage(sem("t_b"), "gla gm logit ropeq ropek sc0 at kd sc1 o u pt0a pt0b pv0 pt1a pt1b pv1")
        a_b = Stage(sem("a_b"), "qk low gv vv silu_a silu_b silu_c abs exp ln qT kT kref qref decay kdec kdn"
                                " exp0 sq exp1 sink pt0 pt1 yscale")
        v_b = Stage(sem("v_b"), "ln_stats ln_aggr ln_eps ln_norm ln_g ln_b xc xs rq1 rq2 rk1 rk2 gate_u gate_g"
                                " min la cum refs refn sv ya kref qref qbd dlast qdec kdec am"
                                " mask0 max0 neg0 negm0 mask1 max1 neg1 negm1 sinkd um state ored oeps o1 yb"
                                " pt0 pt1 den recip att yc ymax yguard ybits yrecip yscale yun")
        p_b = Stage(sem("p_b"), "ln_pow o_pow kcopy vcopy")

        t_c = Stage(sem("t_c"), "y0 y1 out0 out1")
        a_c = Stage(sem("a_c"), "hi0 hi1 ev0 ev1")
        v_c = Stage(sem("v_c"), "lo0 lo1 fac stats aggr msq eps post add")
        p_c = Stage(sem("p_c"), "pow")

        N_PARAMS = 11

        def run_layer(engine, layer, iteration):
            base = layer * NT
            iteration(base, a=True, b=False, c=False, x=True)
            yield
            iteration(base + 1, a=True, b=True, c=False, x=True)
            first = 2
            if layer == 0:
                iteration(2, a=True, b=True, c=True, x=True)
                first = 3
            with engine.Fori(first, NT - 1) as i:
                iteration(i + base, a=True, b=True, c=True, x=True)
            iteration(base + NT - 1, a=True, b=True, c=True, x=False)
            iteration(base + NT, a=False, b=True, c=True, x=False)
            iteration(base + NT + 1, a=False, b=False, c=True, x=False)

        def before_aggregate(dve):
            dve.memset(unused[:], 0.0)

        block = ctx.enter_context(nc.Block())

        @block.sync
        def _(sp):
            def rows(t):
                return bass.ts(t, P)

            sp.dma_start(s_buf[:, 512:528].bitcast(I32), positions.rearrange("b (t p) -> p (b t)", p=P),
                         allow_slow_non_contiguous=True).then_inc(pos_loaded, 16)
            sp.dma_start(s_buf[:, 528:560], inv_freq.broadcast_to([P, HEAD // 2])).then_inc(pos_loaded, 16)
            sp.wait_ge(table_a, 2)
            sp.dma_start(rope_dram.rearrange("t p c -> p t c"),
                         pt[:].rearrange("p (t c) -> p t c", t=NT)).then_inc(rope_stored, 16)
            sp.wait_ge(rope_stored, 16)

            for layer in range(DEPTH):
                base = layer * NT
                wait(sp, t_b, base - 1, "pv1")
                wait(sp, v_b, base - 1, "yun")
                wait(sp, a_b, base - 1, "yscale")
                wait(sp, v_c, base - 1, "add")
                wait(sp, v_w, layer * NB - 1, "lo")
                wait(sp, a_w, layer * NB - 1, "hi")
                sp.dma_start(preg[:], pre_g[layer].rearrange("(k p) -> p k", p=P),
                         allow_slow_non_contiguous=True).then_inc(params, 16)
                sp.dma_start(postg[:], post_g[layer:layer + 1].broadcast_to([P, D_MODEL])).then_inc(params, 16)
                sp.dma_start(ln_g[:], gm_ln_g[layer:layer + 1].broadcast_to([P, GM])).then_inc(params, 16)
                sp.dma_start(ln_b[:], gm_ln_b[layer:layer + 1].broadcast_to([P, GM])).then_inc(params, 16)
                sp.dma_start(gm_bias[:], gm_bs[layer].rearrange("h t -> t h"),
                         allow_slow_non_contiguous=True).then_inc(params, 16)
                sp.dma_start(wg2[:], gla_wg2[layer]).then_inc(params, 16)
                sp.dma_start(gate_b[:], gla_bg[layer].rearrange("(c o) -> c o", o=1),
                         allow_slow_non_contiguous=True).then_inc(params, 16)
                sp.dma_start(norm_g[:], gla_norm_g[layer:layer + 1].broadcast_to([P, HEAD])).then_inc(params, 16)
                sp.dma_start(sinks[:], swa_sinks[layer:layer + 1].broadcast_to([P, 8])).then_inc(params, 16)
                sp.dma_start(s_buf[:, 0:512].rearrange("p (h c) -> p h c", h=GH),
                             gm_ws[layer].rearrange("h t c -> t h c")).then_inc(params, 16)
                stream = x if layer == 0 else out
                if layer:
                    sp.wait_ge(out_stored, 16 * base)

                def load_x(n, t):
                    wait(sp, t_x, n - 1, "x1")
                    sp.dma_start(xt[:], stream[rows(t), :]).then_inc(x_loaded, 16)

                def load_block(b):
                    n = layer * NB + b
                    wait(sp, v_w, n - 2, "lo")
                    wait(sp, a_w, n - 2, "hi")
                    w, src = ((WG, w_in[layer][:, b * WG:(b + 1) * WG]) if b < N_WIN else
                              (OG, w_out[layer][:, (b - N_WIN) * OG:(b - N_WIN + 1) * OG]))
                    sp.dma_start(raw[:, n % 2, :, 0:w],
                                 src.rearrange("(k p) c -> p k c", p=P)).then_inc(raw_loaded[n % 2], 16)

                load_x(base, 0)
                for b in range(N_WIN):
                    load_block(b)
                wait(sp, v_x, base, "lo1")
                sp.dma_start(s_buf[0:1, 2047:2048], pre_g[layer:layer + 1, 0:1]).then_inc(params, 16)

                def iteration(n, a, b, c, x):
                    if x:
                        load_x(n + 1, n + 1 - base)
                    if b:
                        j = n - 1
                        wait(sp, v_b, j - 1, "xs")
                        sp.dma_start(rope[:], rope_dram[j - base] if isinstance(j, int) else
                                     rope_dram[bass.ds(j - base, 1)].rearrange("o p c -> (o p) c")).then_inc(rope_loaded, 16)
                    if c:
                        k = n - 2
                        wait(sp, v_c, k - 1, "add")
                        sp.dma_start(res[:], stream[rows(k - base), :]).then_inc(res_loaded, 16)
                        wait(sp, v_c, k, "add")
                        sp.dma_start(out[rows(k - base), :], ot[:]).then_inc(out_stored, 16)

                steps = run_layer(sp, layer, iteration)
                next(steps)
                for b in range(N_WIN, NB):
                    load_block(b)
                for _ in steps:
                    pass
            sp.wait_ge(out_stored, 16 * NT * DEPTH)

        @block.tensor
        def _(pe):
            pe.wait_ge(const_ready, 1)

            def transpose_x(n):
                wait(pe, a_x, n, "scale")
                for half in range(2):
                    for q in range(4):
                        k = 4 * half + q
                        mm = pe.transpose(TR[half][:, q * P:(q + 1) * P], xt[:, k * P:(k + 1) * P], ident[:])
                    mm.then_inc(t_x.sem, 1)

            def chunk(n, c):
                if c == 0:
                    wait(pe, a_x, n, "hi1")
                    wait(pe, v_x, n, "lo1")
                for k in range(KC):
                    for part, (h, w) in enumerate(((h_hi, w_hi), (h_hi, w_lo), (h_lo, w_hi))):
                        mm = pe.matmul(PJ[c % 2][:, 0:CH], h[:, k, :], w[:, k, c * CH:(c + 1) * CH],
                                       start=(k == 0 and part == 0), stop=(k == KC - 1 and part == 2))
                mm.then_inc(t_a.sem, 1)

            def out_half(n, half):
                for k in range(KC):
                    for part, (h, w) in enumerate(((y_hi, wo_hi), (y_hi, wo_lo), (y_lo, wo_hi))):
                        mm = pe.matmul(PJ[half][:, :], h[:, k, :], w[:, k, half * 512:(half + 1) * 512],
                                       start=(k == 0 and part == 0), stop=(k == KC - 1 and part == 2))
                mm.then_inc(t_c.sem, 1)

            def scores(half):
                for r in range(2 * half, 2 * half + 2):
                    for g in range(2):
                        rows = slice(g * HEAD, (g + 1) * HEAD)
                        mm = pe.matmul(SC[g][:, (r % 2) * 2 * P:(r % 2 + 1) * 2 * P], qT[rows, r, :], kT[rows, :, :],
                                       start=True, stop=True)
                mm.then_inc(t_b.sem, 1)

            def prob_transposes(half):
                for g in range(2):
                    for c in range(4):
                        r, blk = 2 * half + c // 2, c % 2
                        mm = pe.transpose(TR[g][:, c * P:(c + 1) * P], s4[:, g, r, blk * P:(blk + 1) * P], ident[:])
                    mm.then_inc(t_b.sem, 1)

            def attend(half):
                for g in range(2):
                    for r2 in range(2):
                        head = 4 * g + 2 * half + r2
                        for blk in range(2):
                            mm = pe.matmul(GL[:, head * HEAD:(head + 1) * HEAD], pt4[:, g, 2 * r2 + blk, :],
                                           vv[:, blk, g * HEAD:(g + 1) * HEAD], start=(blk == 0), stop=(blk == 1))
                mm.then_inc(t_b.sem, 1)

            for layer in range(DEPTH):
                base = layer * NT
                pe.wait_ge(params, 16 * (N_PARAMS * layer + N_PARAMS - 1))
                wait(pe, a_b, base - 1, "pt1")
                wait(pe, v_c, base - 1, "lo1")
                for h in range(GH):
                    mm = pe.transpose(TR[0][:, h * P:(h + 1) * P], s_buf[:, h * P:(h + 1) * P], ident[:])
                mm.then_inc(gmw_t, 1)
                pe.wait_ge(gmw_ready, layer + 1)
                transpose_x(base)

                def iteration(n, a, b, c, x):
                    j, k = n - 1, n - 2
                    ramp = isinstance(n, int) and n == base

                    def wait_block(blk):
                        if ramp:
                            wait(pe, a_w, layer * NB + blk, "hi")
                            wait(pe, v_w, layer * NB + blk, "lo")

                    if b:
                        wait(pe, a_a, j, "c5")
                        wait(pe, v_x, j + 1 if a else j, "lo0")
                        wait(pe, a_x, j + 1 if a else j, "hi0")
                        pe.transpose(TR[0][:, 0:P], pj[:, C_GQ:C_GQ + P], ident[:])
                        pe.transpose(TR[0][:, P:2 * P], pj[:, C_GK:C_GK + P], ident[:])
                        pe.transpose(TR[0][0:RANK, 2 * P:3 * P], pj[:, C_GL:C_GL + RANK], ident[:]).then_inc(t_b.sem, 1)
                    if a:
                        wait(pe, a_a, n - 1, "c4")
                        wait_block(0)
                        wait_block(1)
                        chunk(n, 0)
                    if c:
                        wait(pe, a_b, k, "yscale")
                        if a:
                            wait(pe, v_x, n, "lo1")
                            wait(pe, a_x, n, "hi1")
                        if not b:
                            wait(pe, v_b, k, "pt1")
                            wait(pe, a_b, k, "pt1")
                        wait(pe, v_b, k, "pt1")
                        for q in range(4):
                            mm = pe.transpose(TR[1][:, q * P:(q + 1) * P], y[:, q * P:(q + 1) * P], ident[:])
                        mm.then_inc(t_c.sem, 1)
                        if b:
                            wait(pe, a_b, j, "low")
                        for q in range(4):
                            mm = pe.transpose(TR[0][:, q * P:(q + 1) * P], y[:, (q + 4) * P:(q + 5) * P], ident[:])
                        mm.then_inc(t_c.sem, 1)
                    if b:
                        wait(pe, v_b, j, "ln_b")
                        wait(pe, v_b, j - 1, "um")
                        wait(pe, v_b, j - 1, "o1")
                        pe.wait_ge(gmw_ready, layer + 1)
                        for h in range(GH):
                            mm = pe.matmul(MX[:, h * HEAD:(h + 1) * HEAD], gm_wT[:, h, :],
                                           pj[:, C_V + h * HEAD:C_V + (h + 1) * HEAD], start=True, stop=True)
                        mm.then_inc(t_b.sem, 1)
                        wait(pe, a_b, j, "low")
                        wait(pe, v_b, j - 1, "att")
                        pe.matmul(GL[:, 0:P], wg2[:, :], g_low[:, :], start=True, stop=True).then_inc(t_b.sem, 1)
                    if a:
                        wait(pe, a_a, n - 1, "c5")
                        wait_block(2)
                        wait_block(3)
                        chunk(n, 1)
                    if b:
                        wait(pe, v_b, j, "rk2")
                        if c:
                            wait(pe, a_c, k, "hi0")
                            wait(pe, v_c, k, "lo0")
                        for r in range(4):
                            mm = pe.transpose(TR[1][:, r * P:(r + 1) * P], roped[:, r * P:(r + 1) * P], ident[:])
                        mm.then_inc(t_b.sem, 1)
                        if c:
                            wait(pe, a_c, k, "hi1")
                            wait(pe, v_c, k, "lo1")
                        pe.transpose(TR[0][:, 0:P], roped[:, 512:640], ident[:]).then_inc(t_b.sem, 1)
                    if c:
                        wait(pe, a_c, k, "hi1")
                        wait(pe, v_c, k, "lo1")
                        wait(pe, a_c, k - 1, "ev0")
                        if a:
                            wait(pe, a_a, n, "c0")
                        if isinstance(k, int) and k == base:
                            wait(pe, a_w, layer * NB + NB - 1, "hi")
                            wait(pe, v_w, layer * NB + NB - 1, "lo")
                        out_half(k, 0)
                    if b:
                        wait(pe, a_b, j, "kT")
                        wait(pe, v_b, j - 1, "mask1")
                        pe.wait_ge(layer_state, layer + 1)
                        wait(pe, p_b, j - 1, "kcopy")
                        scores(0)
                    if c:
                        wait(pe, a_c, k - 1, "ev1")
                        if a:
                            wait(pe, a_a, n, "c1")
                        out_half(k, 1)
                    if b:
                        wait(pe, v_b, j, "kdec")
                        for i in range(NSUB):
                            mm = pe.matmul(GL[:, i * P:(i + 1) * P], k_ref[:, i, :], q_bd[:, i * P:(i + 1) * P],
                                           start=True, stop=True)
                        mm.then_inc(t_b.sem, 1)
                        wait(pe, a_b, j, "kT")
                        pe.transpose(TR[0][:, 0:P], k_dec[:], ident[:]).then_inc(t_b.sem, 1)
                    if a:
                        wait(pe, a_a, n, "c0")
                        if c:
                            wait(pe, a_c, k, "ev0")
                        wait_block(4)
                        wait_block(5)
                        chunk(n, 2)
                    if b:
                        wait(pe, v_b, j, "mask0")
                        scores(1)
                        wait(pe, v_b, j, "am")
                        wait(pe, v_b, j, "sv")
                        wait(pe, v_b, j - 1, "state")
                        wait(pe, a_b, j, "gv")
                        pe.matmul(MX[:, 0:GLA], q_dec[:], state[:], start=True, stop=False, skip_group_check=True)
                        for h in range(GH):
                            mm = pe.matmul(MX[:, h * HEAD:(h + 1) * HEAD], a_mask[:, h, :],
                                           g_v[:, h * HEAD:(h + 1) * HEAD], start=False, stop=(h == GH - 1),
                                           skip_group_check=True)
                        mm.then_inc(t_b.sem, 1)
                        wait(pe, a_b, j, "kdn")
                        pe.matmul(MX[:, GLA:2 * GLA], k_decN[:], g_v[:], start=True, stop=True,
                                  skip_group_check=True).then_inc(t_b.sem, 1)
                    if a:
                        wait(pe, a_a, n, "c1")
                        if c:
                            wait(pe, a_c, k, "ev1")
                        wait_block(6)
                        wait_block(7)
                        chunk(n, 3)
                    if b:
                        wait(pe, a_b, j, "exp0")
                        wait(pe, a_b, j, "kdn")
                        wait(pe, a_b, j, "qT")
                        prob_transposes(0)
                    if a:
                        wait(pe, a_a, n, "c2")
                        wait_block(8)
                        wait_block(9)
                        chunk(n, 4)
                    if b:
                        wait(pe, a_b, j, "pt0")
                        wait(pe, v_b, j, "pt0")
                        wait(pe, a_b, j, "vv")
                        wait(pe, v_b, j, "am")
                        wait(pe, p_b, j - 1, "vcopy")
                        attend(0)
                        wait(pe, a_b, j, "exp1")
                        prob_transposes(1)
                    if a:
                        wait(pe, a_a, n, "c3")
                        wait_block(10)
                        wait_block(11)
                        chunk(n, 5)
                    if x:
                        if b:
                            wait(pe, a_b, j, "pt1")
                            wait(pe, v_b, j, "pt1")
                        transpose_x(n + 1)
                    if b:
                        wait(pe, a_b, j, "pt1")
                        wait(pe, v_b, j, "pt1")
                        attend(1)

                for _ in run_layer(pe, layer, iteration):
                    pass

        @block.scalar
        def _(act):
            copy = ACT.Copy
            for half in range(2):
                act.wait_ge(table_v, 15)
                act.activation(pt[:].rearrange("p (t e d) -> p t e d", t=NT, e=2)[:, :, half, :],
                               s_buf[:, 1024 + 512 * half:1536 + 512 * half].rearrange("p (t d) -> p t d", t=NT),
                               ACT.Sin).then_inc(table_a, 1)

            def x_scale(n):
                wait(act, p_x, n, "pow")
                act.activation(xt[:], xt[:], copy, scale=x_r[:, 0:1]).then_inc(a_x.sem, 1)

            def x_hi(n):
                wait(act, t_a, n - 1, "c5")
                for half in range(2):
                    wait(act, t_x, n, f"x{half}")
                    act.activation(h_hi[:, 4 * half:4 * half + 4, :], TR[half][:].rearrange("p (k t) -> p k t", k=4),
                                   copy).then_inc(a_x.sem, 1)

            def split_hi(layer, b):
                n = layer * NB + b
                wait(act, v_w, n, "mult")
                if b == 0:
                    wait(act, t_a, layer * NT - 1, "c5")
                if b == N_WIN:
                    wait(act, t_c, layer * NT - 1, "out1")
                w, dst = (WG, w_hi[:, :, b * WG:(b + 1) * WG]) if b < N_WIN else \
                         (OG, wo_hi[:, :, (b - N_WIN) * OG:(b - N_WIN + 1) * OG])
                for k in range(KC):
                    mm = act.activation(dst[:, k, :], raw[:, n % 2, k, 0:w], copy, scale=wscale[:, n % 2, k:k + 1])
                mm.then_inc(a_w.sem, 1)

            for layer in range(DEPTH):
                base = layer * NT
                x_scale(base)
                x_hi(base)
                for b in range(N_WIN):
                    split_hi(layer, b)
                act.wait_ge(params, 16 * N_PARAMS * (layer + 1))

                def iteration(n, a, b, c, x):
                    j, k = n - 1, n - 2

                    def evac(chunk):
                        wait(act, t_a, n, f"c{chunk}")
                        for g in range(2 * chunk, 2 * chunk + 2):
                            mm = act.activation(pj[:, g * WG:(g + 1) * WG], PJ[chunk % 2][:, (g % 2) * WG:(g % 2 + 1) * WG],
                                                copy, scale=unscale_in[:, g:g + 1])
                        mm.then_inc(a_a.sem, 1)

                    def probs(half):
                        wait(act, v_b, j, f"negm{half}")
                        for g in range(2):
                            for r in range(2 * half, 2 * half + 2):
                                head = 4 * g + r
                                mm = act.activation(s4[:, g, r, :], s4[:, g, r, :], ACT.Exp,
                                                    bias=neg_max[:, head:head + 1],
                                                    accum_out=row_sum[:, head:head + 1])
                        mm.then_inc(a_b.sem, 1)

                    if b:
                        wait(act, t_b, j, "gla")
                        wait(act, v_b, j - 1, "kdec")
                        act.activation(g_qk[:], TR[0][:, 0:2 * P].rearrange("p (e t) -> p e t", e=2), copy).then_inc(a_b.sem, 1)
                        wait(act, t_b, j - 1, "logit")
                        act.activation(g_low[:], TR[0][0:RANK, 2 * P:3 * P], copy).then_inc(a_b.sem, 1)
                        wait(act, t_b, j - 1, "u")
                        act.activation(g_v[:], pj[:, C_GV:C_GV + GLA], copy).then_inc(a_b.sem, 1)
                        wait(act, t_b, j - 1, "pv1")
                        wait(act, p_b, j - 1, "vcopy")
                        act.activation(vv[:, 1, :], pj[:, C_SV:C_SV + P], copy).then_inc(a_b.sem, 1)
                    if c:
                        wait(act, t_b, k, "pv1")
                        for half in range(2):
                            wait(act, t_c, k, f"y{half}")
                            act.activation(y_hi[:, 4 * half:4 * half + 4, :],
                                           TR[1 - half][:].rearrange("p (k t) -> p k t", k=4), copy).then_inc(a_c.sem, 1)
                    if b:
                        wait(act, t_c, j - 1, "y1")
                        if not c:
                            wait(act, a_b, j - 1, "yscale")
                        act.activation(y[:, 0:GM], pj[:, C_Z:C_Z + GM], ACT.Silu).then_inc(a_b.sem, 1)
                        act.activation(y[:, GM:GM + GLA], pj[:, C_GZ:C_GZ + GLA], ACT.Silu).then_inc(a_b.sem, 1)
                        act.activation(y[:, GM + GLA:], pj[:, C_SZ:C_SZ + SWA], ACT.Silu).then_inc(a_b.sem, 1)
                    if a:
                        if b:
                            wait(act, v_b, j, "gate_u")
                            wait(act, t_b, j, "gm")
                        evac(0)
                    if b:
                        wait(act, t_b, j, "logit")
                        wait(act, v_b, j - 1, "la")
                        act.activation(gate_a[:], GL[:, 0:P], ACT.Abs, bias=gate_b[:, 0:1]).then_inc(a_b.sem, 1)
                        wait(act, a_b, j, "abs")
                        act.activation(gate_a[:], gate_a[:], ACT.Exp, scale=-1.0).then_inc(a_b.sem, 1)
                        wait(act, a_b, j, "exp")
                        act.activation(gate_a[:], gate_a[:], ACT.Ln, bias=one[:, 0:1]).then_inc(a_b.sem, 1)
                    if a:
                        evac(1)
                    if b:
                        wait(act, t_b, j, "ropeq")
                        wait(act, t_b, j - 1, "sc1")
                        act.activation(qT[:], TR[1][:].rearrange("p (r t) -> p r t", r=4), copy,
                                       scale=float(HEAD) ** -0.5).then_inc(a_b.sem, 1)
                        wait(act, t_b, j, "ropek")
                        wait(act, p_b, j - 1, "kcopy")
                        act.activation(kT[:, 1, :], TR[0][:, 0:P], copy).then_inc(a_b.sem, 1)
                        wait(act, v_b, j, "refn")
                        wait(act, t_b, j - 1, "at")
                        for i in range(NSUB):
                            m = (i + 1) * SUB
                            mm = act.activation(k_ref[:, i, 0:m], cum[:, 0:m], ACT.Exp, scale=-1.0 / GATE_TAU,
                                                bias=ref_p[:, i:i + 1])
                        mm.then_inc(a_b.sem, 1)
                        wait(act, v_b, j - 1, "qbd")
                        for i in range(NSUB):
                            cols = slice(i * SUB, (i + 1) * SUB)
                            mm = act.activation(q_ref[:, cols], cum[:, cols], ACT.Exp, scale=1.0 / GATE_TAU,
                                                bias=ref_n[:, i:i + 1])
                        mm.then_inc(a_b.sem, 1)
                        wait(act, v_b, j - 1, "state")
                        act.activation(decay[:], cum[:], ACT.Exp, scale=1.0 / GATE_TAU).then_inc(a_b.sem, 1)
                        wait(act, t_b, j - 1, "kd")
                        act.activation(k_dec[:], cum[:], ACT.Exp, scale=-1.0 / GATE_TAU,
                                       bias=ref_p[:, NSUB:NSUB + 1]).then_inc(a_b.sem, 1)
                    if c:
                        wait(act, v_c, k, "fac")
                        wait(act, v_c, k - 1, "add")
                        if not (isinstance(k, int) and k == 0):
                            act.wait_ge(out_stored, k * 16)
                        for half in range(2):
                            wait(act, t_c, k, f"out{half}")
                            for g in range(2 * half, 2 * half + 2):
                                mm = act.activation(ot[:, g * OG:(g + 1) * OG], PJ[half][:, (g % 2) * OG:(g % 2 + 1) * OG],
                                                    copy, scale=fac[:, g:g + 1])
                            mm.then_inc(a_c.sem, 1)
                    if b:
                        wait(act, t_b, j, "kd")
                        wait(act, t_b, j - 1, "u")
                        act.activation(k_decN[:], TR[0][:, 0:P], copy).then_inc(a_b.sem, 1)
                        probs(0)
                    if a:
                        evac(2)
                    if b:
                        wait(act, t_b, j, "u")
                        wait(act, v_b, j, "ya")
                        act.activation(mix[:], MX[:, 0:GLA], ACT.Square).then_inc(a_b.sem, 1)
                        probs(1)
                        wait(act, v_b, j, "sinkd")
                        act.activation(sink_e[:], sink_e[:], ACT.Exp).then_inc(a_b.sem, 1)
                    if a:
                        if b:
                            wait(act, v_b, j, "xs")
                        evac(3)
                    if b:
                        wait(act, t_b, j, "pt0a")
                        wait(act, t_b, j - 1, "pv1")
                        wait(act, t_c, k, "out1")
                        act.activation(pt4[:, 0, :, :], TR[0][:].rearrange("p (c q) -> p c q", c=4), copy).then_inc(a_b.sem, 1)
                    if a:
                        evac(4)
                    if b:
                        wait(act, t_b, j, "pt1a")
                        act.activation(pt4[:, 0, :, :], TR[0][:].rearrange("p (c q) -> p c q", c=4), copy).then_inc(a_b.sem, 1)
                    if x:
                        x_scale(n + 1)
                    if a:
                        evac(5)
                    if x:
                        x_hi(n + 1)
                    if b:
                        wait(act, v_b, j, "yscale")
                        act.activation(y[:], y[:], copy, scale=y_scale[:, 0:1]).then_inc(a_b.sem, 1)

                steps = run_layer(act, layer, iteration)
                next(steps)
                for b in range(N_WIN, NB):
                    split_hi(layer, b)
                for _ in steps:
                    pass

        @block.vector
        def _(dve):
            tsteps = [0]

            def table(ins):
                tsteps[0] += 1
                ins.then_inc(table_v, 1)
                dve.wait_ge(table_v, tsteps[0])

            dve.wait_ge(pos_loaded, 32)
            ang, tmp = s_buf[:, 0:512], s_buf[:, 1024:1536]
            ang3 = ang.rearrange("p (t d) -> p t d", t=NT)
            table(dve.tensor_copy(s_buf[:, 560:576], s_buf[:, 512:528].bitcast(I32)))
            table(dve.tensor_tensor(ang3, s_buf[:, 560:576].unsqueeze(2).broadcast_to([P, NT, HEAD // 2]),
                                    s_buf[:, 528:560].unsqueeze(1).broadcast_to([P, NT, HEAD // 2]), ALU.mult))
            for half in range(2):
                arg = s_buf[:, 1024 + 512 * half:1536 + 512 * half]
                turns = s_buf[:, 512:1024] if half == 0 else s_buf[:, 512:1024]
                quarter = 0.25 if half == 0 else 0.0
                table(dve.tensor_scalar(turns, ang, 1.0 / (2.0 * np.pi), quarter, ALU.mult, ALU.add))
                table(dve.tensor_scalar(turns, turns, ROUND, ROUND, ALU.add, ALU.subtract))
                table(dve.scalar_tensor_tensor(arg, turns, -TWO_PI_HI, ang, ALU.mult, ALU.add))
                table(dve.scalar_tensor_tensor(arg, turns, -TWO_PI_LO, arg, ALU.mult, ALU.add))
                table(dve.tensor_scalar(arg, arg, quarter * 2.0 * np.pi, PI_SAFE, ALU.add, ALU.min))
                table(dve.tensor_scalar(arg, arg, -PI_SAFE, None, ALU.max))
            table(dve.memset(one[:], 1.0))
            dve.wait_ge(const_ready, 1)

            def x_stats_of(n, t):
                dve.wait_ge(x_loaded, 16 * (n + 1))
                for h in range(2):
                    ins = dve.bn_stats(x_stats[:, h, :], xt[:, h * 512:(h + 1) * 512])
                ins.then_inc(v_x.sem, 1)
                wait(dve, v_x, n, "stats")
                before_aggregate(dve)
                dve.bn_aggr(x_mv[:], x_stats[:]).then_inc(v_x.sem, 1)
                wait(dve, v_x, n, "aggr")
                dve.scalar_tensor_tensor(x_mv[:, 1:2], x_mv[:, 0:1], x_mv[:, 0:1], x_mv[:, 1:2],
                                         ALU.mult, ALU.add).then_inc(v_x.sem, 1)
                wait(dve, v_x, n, "msq")
                wait(dve, a_x, n - 1, "scale")
                dve.tensor_scalar(x_mv[:, 0:1], x_mv[:, 1:2], EPS, H_SCALE ** -2, ALU.add, ALU.mult).then_inc(v_x.sem, 1)

            def x_lo(n):
                wait(dve, t_a, n - 1, "c5")
                for half in range(2):
                    wait(dve, a_x, n, f"hi{half}")
                    dve.tensor_tensor(h_lo[:, 4 * half:4 * half + 4, :], TR[half][:].rearrange("p (k t) -> p k t", k=4),
                                      h_hi[:, 4 * half:4 * half + 4, :], ALU.subtract).then_inc(v_x.sem, 1)

            def split_max(layer, b):
                n = layer * NB + b
                w = WG if b < N_WIN else OG
                dve.wait_ge(raw_loaded[n % 2], 16 * (n // 2 + 1))
                wait(dve, v_w, n - 1, "bmax") if b else None
                dve.tensor_reduce(kmax[:], raw[:, n % 2, :, 0:w], AX.X, ALU.max,
                                  apply_absolute_value=True).then_inc(v_w.sem, 1)
                wait(dve, v_w, n, "kmax")
                src = preg_abs if b < N_WIN else None
                if src is not None:
                    dve.tensor_tensor(kmax[:], kmax[:], src[:], ALU.mult).then_inc(v_w.sem, 1)
                else:
                    dve.tensor_copy(kmax[:, 0:1], kmax[:, 0:1]).then_inc(v_w.sem, 1)
                wait(dve, v_w, n, "gmul")
                dve.tensor_reduce(bmax[:], kmax[:], AX.X, ALU.max).then_inc(v_w.sem, 1)

            def split_lo(layer, b):
                n = layer * NB + b
                half = wpow[:, 0:1]
                wait(dve, p_w, n, "all")
                dve.tensor_scalar(wpow[:, 0:1], gmax[:], TINY, None, ALU.max).then_inc(v_w.sem, 1)
                wait(dve, v_w, n, "guard")
                dve.tensor_scalar(half.bitcast(U32), half.bitcast(U32), EXP_BITS, None, ALU.bitwise_and).then_inc(v_w.sem, 1)
                wait(dve, v_w, n, "bits")
                dve.reciprocal(wpow[:, 1:2], wpow[:, 0:1]).then_inc(v_w.sem, 1)
                wait(dve, v_w, n, "recip")
                dve.tensor_scalar(wpow[:, 1:2], wpow[:, 1:2], TOP, None, ALU.mult).then_inc(v_w.sem, 1)
                if b < N_WIN:
                    if b == 0:
                        wait(dve, a_a, layer * NT - 1, "c5")
                    dve.tensor_scalar(unscale_in[:, b:b + 1], wpow[:, 0:1], 1.0 / (TOP * H_SCALE), None,
                                      ALU.mult).then_inc(v_w.sem, 1)
                else:
                    dve.tensor_scalar(unscale_out[:, b - N_WIN:b - N_WIN + 1], wpow[:, 0:1], 1.0 / TOP, None,
                                      ALU.mult).then_inc(v_w.sem, 1)
                wait(dve, v_w, n, "scale")
                if b < N_WIN:
                    dve.tensor_scalar(wscale[:, n % 2, :], preg[:], wpow[:, 1:2], None, ALU.mult).then_inc(v_w.sem, 1)
                else:
                    dve.tensor_copy(wscale[:, n % 2, :], wpow[:, 1:2].broadcast_to([P, KC])).then_inc(v_w.sem, 1)
                w, hi, lo, at = (WG, w_hi, w_lo, b * WG) if b < N_WIN else (OG, wo_hi, wo_lo, (b - N_WIN) * OG)
                wait(dve, a_w, n, "hi")
                wait(dve, v_w, n, "mult")
                for k in range(KC):
                    ins = dve.scalar_tensor_tensor(lo[:, k, at:at + w], raw[:, n % 2, k, 0:w], wscale[:, n % 2, k:k + 1],
                                                   hi[:, k, at:at + w], ALU.mult, ALU.subtract)
                ins.then_inc(v_w.sem, 1)

            for layer in range(DEPTH):
                base = layer * NT
                dve.wait_ge(params, 16 * (N_PARAMS * layer + N_PARAMS - 1))
                dve.tensor_scalar(preg_abs[:], preg[:], -1.0, None, ALU.mult).then_inc(preg_ready, 1)
                dve.wait_ge(preg_ready, 2 * layer + 1)
                dve.tensor_tensor(preg_abs[:], preg_abs[:], preg[:], ALU.max).then_inc(preg_ready, 1)
                dve.wait_ge(preg_ready, 2 * layer + 2)
                dve.wait_ge(gmw_t, layer + 1)
                wait(dve, t_b, base - 1, "gm")
                dve.tensor_tensor(gm_wT[:], TR[0][:].rearrange("p (h t) -> p h t", h=GH),
                                  causal[:].unsqueeze(1).broadcast_to([P, GH, P]), ALU.mult).then_inc(gmw_ready, 1)
                x_stats_of(base, 0)
                x_lo(base)
                for b in range(N_WIN):
                    split_max(layer, b)
                    split_lo(layer, b)
                dve.wait_ge(params, 16 * N_PARAMS * (layer + 1))

                def iteration(n, a, b, c, x):
                    j, k = n - 1, n - 2

                    def b_wait(step):
                        wait(dve, v_b, j, step)

                    def b_done(ins):
                        ins.then_inc(v_b.sem, 1)

                    def mask_max(half):
                        wait(dve, t_b, j, f"sc{half}")
                        first = isinstance(j, int) and j == base
                        r2 = slice(2 * half, 2 * half + 2)
                        for g in range(2):
                            ins = dve.tensor_tensor(s4[:, g, r2, :], SC[g][:].rearrange("p (r k) -> p r k", r=2),
                                                    band[:, 0 if first else 1, :].unsqueeze(1).broadcast_to([P, 2, 2 * P]),
                                                    ALU.add)
                        b_done(ins)
                        b_wait(f"mask{half}")
                        heads = [t[:].rearrange("p (g r) -> p g r", g=2)[:, :, r2] for t in (row_max, neg_max, sinks)]
                        wait(dve, v_b, j - 1, "sinkd")
                        b_done(dve.tensor_reduce(heads[0], s4[:, :, r2, :], AX.X, ALU.max))
                        b_wait(f"max{half}")
                        b_done(dve.tensor_tensor(heads[0], heads[0], heads[2], ALU.max))
                        b_wait(f"neg{half}")
                        b_done(dve.tensor_scalar(heads[1], heads[0], -1.0, None, ALU.mult))

                    if b:
                        wait(dve, a_a, j, "c5")
                        wait(dve, v_b, j - 1, "ln_norm")
                        b_done(dve.bn_stats(v_stats[:], pj[:, C_V:C_V + GM]))
                        b_wait("ln_stats")
                        before_aggregate(dve)
                        b_done(dve.bn_aggr(v_mv[:], v_stats[:]))
                        b_wait("ln_aggr")
                        wait(dve, p_b, j - 1, "ln_pow")
                        b_done(dve.tensor_scalar(v_mv[:, 1:2], v_mv[:, 1:2], EPS, None, ALU.add))
                        wait(dve, p_b, j, "ln_pow")
                        b_done(dve.tensor_scalar(pj[:, C_V:C_V + GM], pj[:, C_V:C_V + GM], v_mv[:, 0:1], v_r[:, 0:1],
                                                 ALU.subtract, ALU.mult))
                        b_wait("ln_norm")
                        b_done(dve.tensor_tensor(pj[:, C_V:C_V + GM], pj[:, C_V:C_V + GM], ln_g[:], ALU.mult))
                        b_wait("ln_g")
                        b_done(dve.tensor_tensor(pj[:, C_V:C_V + GM], pj[:, C_V:C_V + GM], ln_b[:], ALU.add))
                        dve.wait_ge(rope_loaded, 16 * (j + 1))
                        wait(dve, t_b, j - 1, "pt1b")
                        wait(dve, v_b, j - 1, "yc")
                        qk = pj[:, C_SQ:C_SQ + 640].rearrange("p (m d) -> p m d", d=HEAD // 2)
                        for half, dst in ((0, xc), (1, xs)):
                            b_done(dve.tensor_tensor(dst.rearrange("p (m d) -> p m d", d=HEAD // 2), qk,
                                                     rope[:, 32 * half:32 * half + 32].unsqueeze(1).broadcast_to([P, 20, 32]),
                                                     ALU.mult))
                        b_wait("xs")
                        qc = xc[:, 0:512].rearrange("p (g r e d) -> p g r e d", g=2, r=4, e=2)
                        qs = xs[:, 0:512].rearrange("p (g r e d) -> p g r e d", g=2, r=4, e=2)
                        qo = roped[:, 0:512].rearrange("p (r g e d) -> p g r e d", r=4, g=2, e=2)
                        kc, ks, ko = (halves(t[:, 512:640], 2) for t in (xc, xs, roped))
                        b_done(dve.tensor_tensor(qo[:, :, :, 0, :], qc[:, :, :, 0, :], qs[:, :, :, 1, :], ALU.subtract))
                        b_done(dve.tensor_tensor(qo[:, :, :, 1, :], qc[:, :, :, 1, :], qs[:, :, :, 0, :], ALU.add))
                        b_done(dve.tensor_tensor(ko[:, :, 0, :], kc[:, :, 0, :], ks[:, :, 1, :], ALU.subtract))
                        b_done(dve.tensor_tensor(ko[:, :, 1, :], kc[:, :, 1, :], ks[:, :, 0, :], ALU.add))
                    if c:
                        for half in range(2):
                            wait(dve, t_b, k, "pv1")
                            wait(dve, a_c, k, f"hi{half}")
                            dve.tensor_tensor(y_lo[:, 4 * half:4 * half + 4, :], TR[1 - half][:].rearrange("p (k t) -> p k t", k=4),
                                              y_hi[:, 4 * half:4 * half + 4, :], ALU.subtract).then_inc(v_c.sem, 1)
                        wait(dve, v_b, k, "yun")
                        wait(dve, a_c, k - 1, "ev1")
                        if isinstance(k, int) and k == base:
                            wait(dve, v_w, layer * NB + NB - 1, "lo")
                        dve.tensor_scalar(fac[:], unscale_out[:], y_unscale[:, 0:1], None, ALU.mult).then_inc(v_c.sem, 1)
                    if b:
                        wait(dve, a_b, j, "silu_a")
                        b_done(dve.tensor_tensor(y[:, 0:GM], y[:, 0:GM], pj[:, C_U:C_U + GM], ALU.mult))
                        wait(dve, a_b, j, "silu_b")
                        y_gla = y[:, GM:GM + GLA].rearrange("p (h d) -> p h d", h=GH)
                        b_done(dve.tensor_tensor(y_gla, y_gla, norm_g[:].unsqueeze(1).broadcast_to([P, GH, HEAD]), ALU.mult))
                        wait(dve, a_b, j, "abs")
                        wait(dve, v_b, j - 1, "cum")
                        b_done(dve.tensor_scalar(gate_m[:], GL[:, 0:P], gate_b[:, 0:1], 0.0, ALU.add, ALU.min))
                        b_wait("min")
                        wait(dve, a_b, j, "ln")
                        b_done(dve.tensor_tensor(gate_m[:], gate_m[:], gate_a[:], ALU.subtract))
                        b_wait("la")
                        wait(dve, a_b, j - 1, "kdec")
                        b_done(dve.tensor_tensor_scan(cum[:], one[:, 0:1].broadcast_to([P, P]), gate_m[:], 0.0,
                                                      ALU.mult, ALU.add))
                        b_wait("cum")
                        dve.tensor_scalar(ref_p[:, 0:NSUB], cum[:, SUB // 2 - 1::SUB], 1.0 / GATE_TAU, None, ALU.mult)
                        b_done(dve.tensor_scalar(ref_p[:, NSUB:NSUB + 1], cum[:, P - 1:P], 1.0 / GATE_TAU, None, ALU.mult))
                        b_wait("refs")
                        b_done(dve.tensor_scalar(ref_n[:], ref_p[:, 0:NSUB], -1.0, None, ALU.mult))
                        wait(dve, t_b, j, "gm")
                        wait(dve, v_b, j - 1, "yb")
                        mix4 = mix[:].rearrange("p (h d) -> p h d", h=GH)
                        mx4 = MX[:, 0:GM].rearrange("p (h d) -> p h d", h=GH)
                        b_done(dve.tensor_tensor(mix4, mx4, gm_bias[:].unsqueeze(2).broadcast_to([P, GH, HEAD]), ALU.add))
                        b_wait("sv")
                        b_done(dve.tensor_tensor(y[:, 0:GM], y[:, 0:GM], mix[:], ALU.mult))
                        wait(dve, a_b, j, "kref")
                        b_done(dve.tensor_tensor(k_ref[:], k_ref[:], g_qk[:, 1, :].unsqueeze(1).broadcast_to([P, NSUB, P]),
                                                 ALU.mult))
                        wait(dve, a_b, j, "qref")
                        b_done(dve.scalar_tensor_tensor(q_ref[:], g_qk[:, 0, :], float(GK) ** -0.5, q_ref[:],
                                                        ALU.mult, ALU.mult))
                        b_wait("qref")
                        wait(dve, t_b, j - 1, "o")
                        b_done(dve.tensor_tensor(
                            q_bd[:].rearrange("p (i h t) -> p i h t", i=NSUB, h=GH),
                            q_ref[:].rearrange("p (i t) -> p i t", i=NSUB).unsqueeze(2).broadcast_to([P, NSUB, GH, SUB]),
                            head_mask[:].unsqueeze(1).unsqueeze(3).broadcast_to([P, NSUB, GH, SUB]), ALU.mult))
                        wait(dve, a_b, j, "decay")
                        wait(dve, v_b, j - 1, "state")
                        b_done(dve.tensor_copy(tile_decay[:], decay[:, P - 1:P]))
                        b_wait("dlast")
                        b_done(dve.scalar_tensor_tensor(q_dec[:], g_qk[:, 0, :], float(GK) ** -0.5, decay[:],
                                                        ALU.mult, ALU.mult))
                        wait(dve, a_b, j, "kdec")
                        b_done(dve.tensor_tensor(k_dec[:], k_dec[:], g_qk[:, 1, :], ALU.mult))
                        wait(dve, t_b, j, "at")
                        b_done(dve.tensor_tensor(
                            a_mask.rearrange("p h (i t) -> p i h t", i=NSUB),
                            GL[:].rearrange("p (i h t) -> p i h t", i=NSUB, h=GH),
                            causal[:].rearrange("p (i t) -> p i t", i=NSUB).unsqueeze(2).broadcast_to([P, NSUB, GH, SUB]),
                            ALU.mult))
                        mask_max(0)
                    if c:
                        wait(dve, a_c, k, "ev1")
                        for h in range(2):
                            ins = dve.bn_stats(o_stats[:, h, :], ot[:, h * 512:(h + 1) * 512])
                        ins.then_inc(v_c.sem, 1)
                        wait(dve, v_c, k, "stats")
                        before_aggregate(dve)
                        dve.bn_aggr(o_mv[:], o_stats[:]).then_inc(v_c.sem, 1)
                        wait(dve, v_c, k, "aggr")
                        dve.scalar_tensor_tensor(o_mv[:, 1:2], o_mv[:, 0:1], o_mv[:, 0:1], o_mv[:, 1:2],
                                                 ALU.mult, ALU.add).then_inc(v_c.sem, 1)
                        wait(dve, v_c, k, "msq")
                        dve.tensor_scalar(o_mv[:, 0:1], o_mv[:, 1:2], EPS, None, ALU.add).then_inc(v_c.sem, 1)
                    if b:
                        mask_max(1)
                        b_wait("negm1")
                        wait(dve, v_b, j - 1, "den")
                        b_done(dve.tensor_tensor(sink_e[:], sinks[:], neg_max[:], ALU.add))
                    if c:
                        wait(dve, p_c, k, "pow")
                        dve.scalar_tensor_tensor(ot[:], ot[:], out_r[:, 0:1], postg[:], ALU.mult, ALU.mult).then_inc(v_c.sem, 1)
                        wait(dve, v_c, k, "post")
                        dve.wait_ge(res_loaded, 16 * (k + 1))
                        dve.tensor_tensor(ot[:], ot[:], res[:], ALU.add).then_inc(v_c.sem, 1)
                    if b:
                        wait(dve, a_b, j, "sq")
                        b_done(dve.tensor_tensor(update.rearrange("p (h d) -> p h d", h=GH),
                                                 MX[:, GLA:2 * GLA].rearrange("p (h d) -> p h d", h=GH),
                                                 head_mask[:].unsqueeze(2).broadcast_to([P, GH, HEAD]), ALU.mult))
                        b_wait("um")
                        b_done(dve.scalar_tensor_tensor(state[:], state[:], tile_decay[:, 0:1], update, ALU.mult, ALU.add))
                        wait(dve, a_b, j, "sq")
                        b_done(dve.tensor_reduce(o_sum[:], mix4, AX.X, ALU.add))
                        b_wait("ored")
                        b_done(dve.tensor_scalar(o_sum[:], o_sum[:], 1.0 / HEAD, EPS, ALU.mult, ALU.add))
                        wait(dve, p_b, j, "o_pow")
                        b_done(dve.tensor_tensor(mix4, mx4, o_r[:].unsqueeze(2).broadcast_to([P, GH, HEAD]), ALU.mult))
                        b_wait("o1")
                        b_done(dve.tensor_tensor(y[:, GM:GM + GLA], y[:, GM:GM + GLA], mix[:], ALU.mult))
                        wait(dve, t_b, j, "pt0b")
                        wait(dve, t_c, k, "out1")
                        b_done(dve.tensor_copy(pt4[:, 1, :, :], TR[1][:].rearrange("p (c q) -> p c q", c=4)))
                    if x:
                        x_stats_of(n + 1, None)
                    if b:
                        wait(dve, t_b, j, "pt1b")
                        b_done(dve.tensor_copy(pt4[:, 1, :, :], TR[1][:].rearrange("p (c q) -> p c q", c=4)))
                        wait(dve, a_b, j, "sink")
                        b_done(dve.tensor_tensor(denom[:], row_sum[:], sink_e[:], ALU.add))
                        b_wait("den")
                        b_done(dve.reciprocal(denom[:], denom[:]))
                    if x:
                        x_lo(n + 1)
                    if b:
                        wait(dve, t_b, j, "pv1")
                        b_wait("recip")
                        b_done(dve.tensor_tensor(att.rearrange("p (h d) -> p h d", h=8), GL[:].rearrange("p (h d) -> p h d", h=8),
                                                 denom[:].unsqueeze(2).broadcast_to([P, 8, HEAD]), ALU.mult))
                        b_wait("att")
                        wait(dve, a_b, j, "silu_c")
                        b_done(dve.tensor_tensor(y[:, GM + GLA:], y[:, GM + GLA:], att, ALU.mult))
                        b_wait("yc")
                        b_done(dve.tensor_reduce(y_max[:], y[:], AX.X, ALU.max, apply_absolute_value=True))
                        b_wait("ymax")
                        b_done(dve.tensor_scalar(y_max[:], y_max[:], TINY, None, ALU.max))
                        b_wait("yguard")
                        bits = y_max[:].bitcast(U32)
                        b_done(dve.tensor_scalar(bits, bits, EXP_BITS, None, ALU.bitwise_and))
                        b_wait("ybits")
                        wait(dve, a_b, j - 1, "yscale")
                        b_done(dve.reciprocal(y_scale[:], y_max[:]))
                        b_wait("yrecip")
                        b_done(dve.tensor_scalar(y_scale[:], y_scale[:], TOP, None, ALU.mult))
                        wait(dve, v_c, j - 1, "fac")
                        b_done(dve.tensor_scalar(y_unscale[:], y_max[:], 1.0 / TOP, None, ALU.mult))

                steps = run_layer(dve, layer, iteration)
                next(steps)
                for b in range(N_WIN, NB):
                    split_max(layer, b)
                    if b == N_WIN:
                        wait(dve, a_c, base - 1, "ev1")
                    split_lo(layer, b)
                for _ in steps:
                    pass

        @block.gpsimd
        def _(pool):
            own = sem("pool_constants")
            pool.memset(ident[:], 0.0)
            pool.memset(causal[:], 1.0)
            pool.memset(pool_one[:], 1.0)
            pool.memset(band[:], 0.0)
            pool.memset(head_mask[:], 1.0)
            pool.memset(k_ref[:], 0.0)
            pool.memset(neg_half[:], -0.5).then_inc(own, 1)
            pool.wait_ge(own, 1)
            pool.affine_select(out=ident[:], in_=ident[:], compare_op=ALU.not_equal, fill=1.0, base=0,
                               pattern=[[-1, P]], channel_multiplier=1)
            pool.affine_select(out=causal[:], in_=causal[:], compare_op=ALU.is_ge, fill=0.0, base=0,
                               pattern=[[1, P]], channel_multiplier=-1)
            for v in range(2):
                pool.affine_select(out=band[:, v, P:], in_=band[:, v, P:], compare_op=ALU.is_ge, fill=NEG, base=0,
                                   pattern=[[-1, P]], channel_multiplier=1)
            pool.affine_select(out=band[:, 1, 0:P], in_=band[:, 1, 0:P], compare_op=ALU.is_gt, fill=NEG, base=0,
                               pattern=[[1, P]], channel_multiplier=-1)
            pool.memset(band[:, 0, 0:P], NEG)
            pool.affine_select(out=head_mask[:], in_=head_mask[:], compare_op=ALU.is_ge, fill=0.0, base=0,
                               pattern=[[-GK, GH]], channel_multiplier=1).then_inc(own, 1)
            pool.wait_ge(own, 2)
            pool.affine_select(out=head_mask[:], in_=head_mask[:], compare_op=ALU.is_ge, fill=0.0, base=GK - 1,
                               pattern=[[GK, GH]], channel_multiplier=-1).then_inc(const_ready, 1)
            pool.wait_ge(const_ready, 1)

            def x_pow(n):
                wait(pool, v_x, n, "eps")
                wait(pool, a_x, n - 1, "scale")
                pool.tensor_tensor(x_r[:], x_mv[:, 0:1], neg_half[:, 0:1], ALU.pow).then_inc(p_x.sem, 1)

            def block_max(layer, b):
                n = layer * NB + b
                wait(pool, v_w, n, "bmax")
                pool.partition_all_reduce(gmax[:], bmax[:], P, ABSMAX).then_inc(p_w.sem, 1)

            for layer in range(DEPTH):
                base = layer * NT
                wait(pool, t_b, base - 1, "pv1")
                wait(pool, p_b, base - 1, "vcopy")
                wait(pool, v_b, base - 1, "state")
                pool.memset(kT[:, 0, :], 0.0)
                pool.memset(vv[:, 0, :], 0.0)
                pool.memset(state[:], 0.0).then_inc(layer_state, 1)
                x_pow(base)
                for b in range(N_WIN):
                    block_max(layer, b)

                def iteration(n, a, b, c, x):
                    j, k = n - 1, n - 2
                    if b:
                        wait(pool, v_b, j, "ln_eps")
                        wait(pool, v_b, j - 1, "ln_norm")
                        pool.tensor_tensor(v_r[:], v_mv[:, 1:2], neg_half[:, 0:1], ALU.pow).then_inc(p_b.sem, 1)
                    if c:
                        wait(pool, v_c, k, "eps")
                        wait(pool, v_c, k - 1, "post")
                        pool.tensor_tensor(out_r[:], o_mv[:, 0:1], neg_half[:, 0:1], ALU.pow).then_inc(p_c.sem, 1)
                    if b:
                        wait(pool, v_b, j, "oeps")
                        pool.tensor_tensor(o_r[:], o_sum[:], neg_half[:], ALU.pow).then_inc(p_b.sem, 1)
                        wait(pool, t_b, j, "sc1")
                        pool.tensor_tensor(kT[:, 0, :], kT[:, 1, :], pool_one[:, 0:1].broadcast_to([P, P]), ALU.mult).then_inc(p_b.sem, 1)
                    if x:
                        x_pow(n + 1)
                    if b:
                        wait(pool, t_b, j, "pv1")
                        pool.tensor_tensor(vv[:, 0, :], vv[:, 1, :], pool_one[:, 0:1].broadcast_to([P, P]), ALU.mult).then_inc(p_b.sem, 1)

                steps = run_layer(pool, layer, iteration)
                next(steps)
                for b in range(N_WIN, NB):
                    block_max(layer, b)
                for _ in steps:
                    pass


_INS = ["x", "positions", "pre_g", "w_in", "gm_ln_g", "gm_ln_b", "gm_ws", "gm_bs", "gla_wg2", "gla_bg",
        "gla_norm_g", "swa_sinks", "w_out", "post_g"]


def kernel(**inputs):
    import concourse.bacc as _bacc
    from concourse.bass_utils import run_bass_kernel_spmd as _run

    nc = _bacc.Bacc("TRN2", target_bir_lowering=False, num_devices=1)
    arrays = {n: np.ascontiguousarray(inputs[n]) for n in _INS}
    arrays["x"] = arrays["x"].reshape(SEQ, D_MODEL)
    arrays["inv_freq"] = (ROPE_THETA ** (-np.arange(HEAD // 2) * 2.0 / HEAD)).astype(np.float32).reshape(1, -1)
    aps = [nc.dram_tensor("in_" + n, a.shape, mybir.dt.from_np(a.dtype), kind="ExternalInput").ap()
           for n, a in arrays.items()]
    out = nc.dram_tensor("out_y", (SEQ, D_MODEL), F32, kind="ExternalOutput").ap()
    hybrid_trunk(nc, *aps, out)
    r = _run(nc, [{"in_" + n: a for n, a in arrays.items()}], core_ids=[0])
    return r.results[0]["out_y"].reshape(1, SEQ, D_MODEL)
```

```python
from contextlib import ExitStack

import numpy as np

import concourse.bass as bass
from concourse import mybir

F32 = mybir.dt.float32
F16 = mybir.dt.float16
BF16 = mybir.dt.bfloat16
I32 = mybir.dt.int32
U32 = mybir.dt.uint32
ALU = mybir.AluOpType
ACT = mybir.ActivationFunctionType
AX = mybir.AxisListType
ABSMAX = bass.bass_isa.ReduceOp.max

P = 128
D_MODEL, SEQ, DEPTH = 1024, 2048, 2
NT = SEQ // P
KC = D_MODEL // P
HEAD = 64
EPS = 1e-6
GM, GLA, SWA = 256, 256, 512
GH, GK = 4, 32
GATE_TAU = 16.0
NSUB, SUB = 4, 32
ROPE_THETA = 10000.0

C_U, C_V, C_Z = 0, 256, 512
C_GQ, C_GK, C_GV, C_GL, C_GZ = 768, 896, 1024, 1280, 1296
C_SQ, C_SK, C_SV, C_SZ = 1552, 2064, 2192, 2320
D_IN = 2832
RANK = C_GZ - C_GL
N_CHUNK = 6
CH = D_IN // N_CHUNK
WG = CH // 2
N_WIN = D_IN // WG
OG = 256
N_WOUT = D_MODEL // OG
RAW_W = max(WG, OG)

H_SCALE = 2.0 ** 10
TOP = 2.0 ** 14
NEG = -1.0e30
TINY = 1.0e-30
EXP_BITS = 0x7F800000
ROUND = 12582912.0
TWO_PI_HI, TWO_PI_LO = 6.28125, 0.0019353071795864769
PI_SAFE = 3.1415925


class Stage:

    def __init__(self, sem, steps):
        self.sem = sem
        self.steps = steps.split()
        assert len(set(self.steps)) == len(self.steps)

    def count(self, n, step):
        return n * len(self.steps) + (self.steps.index(step) + 1)


def wait(engine, stage, n, step):
    if isinstance(n, int) and n < 0:
        return
    engine.wait_ge(stage.sem, stage.count(n, step))


def hybrid_trunk(nc, x, positions, pre_g, w_in, gm_ln_g, gm_ln_b, gm_ws, gm_bs, gla_wg2, gla_bg,
                 gla_norm_g, swa_sinks, w_out, post_g, inv_freq, out):
    with ExitStack() as ctx:
        def sb(name, shape, dt=F32):
            return ctx.enter_context(nc.sbuf_tensor(name, shape, dt))

        def bank(name):
            return ctx.enter_context(nc.psum_tensor(name, [P, 512], F32))

        def sem(name):
            return ctx.enter_context(nc.semaphore(name))

        rope_dram = nc.dram_tensor("rope_tables", (NT, P, HEAD), F32, kind="Internal").ap()

        columns = sb("columns", [P, 200])
        used = [0]

        def col(n, *shape):
            at = used[0]
            used[0] += n
            ap = columns[:, at:at + n]
            return ap if not shape else ap.rearrange("p (a b) -> p a b", a=shape[0])

        w_hi = sb("w_hi", [P, KC, D_IN], F16)
        w_lo = sb("w_lo", [P, KC, D_IN], F16)
        wo_hi = sb("wo_hi", [P, KC, D_MODEL], F16)
        wo_lo = sb("wo_lo", [P, KC, D_MODEL], F16)
        raw = sb("raw", [P, 2, KC, RAW_W])
        part_sum = col(2)
        part_bound = col(2)
        bound = col(2)
        wpow = col(2)
        wscale = col(2 * KC, 2)
        unscale_in = col(N_WIN)
        unscale_out = col(N_WOUT)
        preg = col(KC)
        preg_top = col(1)
        postg = sb("postg", [P, D_MODEL])
        ln_g = sb("ln_g", [P, GM])
        ln_b = sb("ln_b", [P, GM])
        gm_wT = sb("gm_wT", [P, GH, P])
        gm_bias = col(GH)
        wg2 = sb("wg2", [RANK, P])
        gate_b = col(1)
        norm_g = sb("norm_g", [P, HEAD])
        sinks = col(8)
        ident = sb("ident", [P, P])
        causal = sb("causal", [P, P])
        band = sb("band", [P, 2, 2 * P])
        head_mask = col(GH)
        one = col(1)
        unused = col(1)
        pool_one = col(1)
        neg_half = col(GH)
        xt = sb("xt", [P, D_MODEL])
        h_hi = sb("h_hi", [P, KC, P], F16)
        h_lo = sb("h_lo", [P, KC, P], F16)
        x_stats = col(2 * 6, 2)
        x_mv = col(2)
        x_r = col(1)
        pj = sb("pj", [P, D_IN])
        y = sb("y", [P, D_MODEL])
        s_buf = sb("s_buf", [P, 8 * 2 * P])
        pt = sb("pt", [P, 2 * 4 * P])
        qT = sb("qT", [P, 4, P])
        kT = sb("kT", [P, 2, P])
        vv = sb("vv", [P, 2, P])
        rope = sb("rope", [P, HEAD])
        row_max = col(8)
        neg_max = col(8)
        row_sum = col(8)
        sink_e = col(8)
        denom = col(8)
        g_v = sb("g_v", [P, GLA])
        g_qk = sb("g_qk", [P, 2, P])
        g_low = sb("g_low", [RANK, P])
        gate_a = sb("gate_a", [P, P])
        gate_m = sb("gate_m", [P, P])
        cum = sb("cum", [P, P])
        ref_p = col(NSUB + 1)
        ref_n = col(NSUB)
        k_ref = sb("k_ref", [P, NSUB, P])
        q_ref = gate_m
        q_bd = sb("q_bd", [P, NSUB * GH * SUB])
        decay = sb("decay", [P, P])
        q_dec = decay
        tile_decay = col(1)
        k_dec = sb("k_dec", [P, P])
        k_decN = gate_a
        state = sb("state", [P, GLA])
        update = q_bd[:, 0:GLA]
        mix = sb("mix", [P, GLA])
        o_sum = col(GH)
        o_r = col(GH)
        v_stats = col(6)
        v_mv = col(2)
        v_r = col(1)
        y_max = col(1)
        y_scale = col(1)
        y_unscale = col(1)
        y_parts = pt[:].bitcast(F16).rearrange("p (s k t) -> p s k t", s=2, k=KC)
        y_hi, y_lo = y_parts[:, 0], y_parts[:, 1]
        fac = col(N_WOUT)
        ot = sb("ot", [P, D_MODEL])
        res = sb("res", [P, D_MODEL])
        o_stats = col(2 * 6, 2)
        o_mv = col(2)
        out_r = col(1)

        PJ = [bank("PJ0"), bank("PJ1")]
        TR = [bank("TR0"), bank("TR1")]
        SC = [bank("SC0"), bank("SC1")]
        MX = bank("MX")
        GL = bank("GL")

        s4 = s_buf[:].rearrange("p (g r k) -> p g r k", g=2, r=4)
        xc, xs = s_buf[:, 0:640], s_buf[:, 640:1280]
        roped = s_buf[:, 1280:1920]
        att = s_buf[:, 0:512]
        pt4 = pt[:].rearrange("p (g c q) -> p g c q", g=2, c=4)
        a_mask = q_bd[:].rearrange("p (h t) -> p h t", h=GH)

        def halves(ap, n):
            return ap.rearrange("p (n e d) -> p n e d", n=n, e=2)

        params = sem("params_loaded")
        preg_loaded = sem("preg_loaded")
        postg_loaded = sem("postg_loaded")
        gmw_loaded = sem("gm_weights_loaded")
        raw_loaded = [sem("raw_even_loaded"), sem("raw_odd_loaded")]
        x_loaded = sem("x_loaded")
        rope_loaded = sem("rope_loaded")
        rope_stored = sem("rope_stored")
        res_loaded = sem("res_loaded")
        out_stored = sem("out_stored")
        const_ready = sem("const_ready")
        pos_loaded = sem("pos_loaded")
        table_v = sem("rope_table_vector_steps")
        table_a = sem("rope_table_sines")
        layer_state = sem("layer_state_cleared")
        gmw_t = sem("gm_weights_transposed")
        gmw_ready = sem("gm_weights_ready")
        preg_ready = sem("preg_ready")

        NB = N_WIN + N_WOUT
        a_m = Stage(sem("a_m"), "sum")
        v_w = Stage(sem("v_w"), "guard bits recip unscale mult lo0 lo1 lo2 lo3")
        a_w = Stage(sem("a_w"), "hi0 hi1 hi2 hi3")
        p_w = Stage(sem("p_w"), "gain all")

        t_x = Stage(sem("t_x"), "x0 x1")
        a_x = Stage(sem("a_x"), "scale hi0 hi1")
        v_x = Stage(sem("v_x"), "stats aggr msq eps lo0 lo1")
        p_x = Stage(sem("p_x"), "pow")

        t_a = Stage(sem("t_a"), "c0 c1 c2 c3 c4 c5")
        a_a = Stage(sem("a_a"), "c0 c1 c2 c3 c4 c5")

        t_b = Stage(sem("t_b"), "gla gm logit ropeq ropek sc0 at kd sc1 o u pt0a pt0b pv0 pt1a pt1b pv1")
        a_b = Stage(sem("a_b"), "qk low gv vv silu_a silu_b silu_c abs exp ln qT kT kref qref decay kdec kdn"
                                " exp0 sq exp1 sink pt0 pt1 yscale")
        v_l = Stage(sem("v_l"), "stats aggr eps norm gain bias")
        p_l = Stage(sem("p_l"), "pow")
        v_b = Stage(sem("v_b"), "xc xs rq1 rq2 rk1 rk2 gate_u gate_g"
                                " min la cum refs refn sv ya kref qref qbd dlast qdec kdec am"
                                " mask0 max0 neg0 negm0 mask1 max1 neg1 negm1 sinkd um state ored oeps o1 yb"
                                " pt0 pt1 den recip att yc ymax yguard ybits yrecip yscale yun")
        p_b = Stage(sem("p_b"), "o_pow kcopy vcopy")

        t_c = Stage(sem("t_c"), "y0 y1 out0 out1")
        a_c = Stage(sem("a_c"), "hi0 hi1 ev0 ev1")
        v_c = Stage(sem("v_c"), "lo0 lo1 fac stats aggr msq eps post add")
        p_c = Stage(sem("p_c"), "pow")

        N_PARAMS = 7

        def layer_of(n, layer):
            return n // NT if isinstance(n, int) else layer

        def run_pipeline(engine, iteration):
            for layer in range(DEPTH):
                base, last = layer * NT, layer == DEPTH - 1
                first = 3 if layer == 0 else 2
                for i in range(first):
                    n = base + i
                    iteration(n, layer, a=True, b=n >= 1, c=n >= 2, x=True)
                with engine.Fori(first, NT - 1) as i:
                    iteration(i + base, layer, a=True, b=True, c=True, x=True)
                iteration(base + NT - 1, layer, a=True, b=True, c=True, x=not last)
            end = DEPTH * NT
            iteration(end, DEPTH - 1, a=False, b=True, c=True, x=False)
            iteration(end + 1, DEPTH - 1, a=False, b=False, c=True, x=False)

        N_FIRST = 6
        SPLITS = {(0, 0): {1: [6], 2: [7], 3: [8, 9], 4: [10, 11], 5: [12], 6: [13]},
                  (0, 1): {3: [14], 6: [15]}}
        for l in range(1, DEPTH):
            SPLITS.update({(l - 1, NT - 1): {1: [0], 2: [1], 3: [2, 3], 4: [4], 5: [5]},
                           (l, 0): {1: [6], 2: [7], 3: [8, 9], 4: [10], 5: [11]},
                           (l, 1): {3: [12], 4: [13], 5: [14], 6: [15]}})

        def blocks_at(n, hook):
            if not isinstance(n, int):
                return []
            layer, i = divmod(n, NT)
            return [(layer + (i == NT - 1), b) for b in SPLITS.get((layer, i), {}).get(hook, [])]

        def starts_run(layer, b):
            return b == 0 or (b == N_WIN and layer > 0)

        def before_aggregate(dve):
            dve.memset(unused[:], 0.0)

        block = ctx.enter_context(nc.Block())

        @block.sync
        def _(sp):
            def rows(t):
                return bass.ts(t, P)

            x_rows = x

            sp.dma_start(s_buf[:, 512:528].bitcast(I32), positions.rearrange("b (t p) -> p (b t)", p=P),
                         allow_slow_non_contiguous=True).then_inc(pos_loaded, 16)
            sp.dma_start(s_buf[:, 528:560], inv_freq.broadcast_to([P, HEAD // 2])).then_inc(pos_loaded, 16)
            sp.wait_ge(table_a, 2)
            sp.dma_start(rope_dram.rearrange("t p c -> p t c"),
                         pt[:].rearrange("p (t c) -> p t c", t=NT)).then_inc(rope_stored, 16)
            sp.wait_ge(rope_stored, 16)

            def load_block(layer, b):
                n = layer * NB + b
                wait(sp, v_w, n - 2, "lo3")
                wait(sp, a_w, n - 2, "hi3")
                w, src = ((WG, w_in[layer][:, b * WG:(b + 1) * WG]) if b < N_WIN else
                          (OG, w_out[layer][:, (b - N_WIN) * OG:(b - N_WIN + 1) * OG]))
                sp.dma_start(raw[:, n % 2, :, 0:w],
                             src.rearrange("(k p) c -> p k c", p=P)).then_inc(raw_loaded[n % 2], 16)

            def load_x(n, layer):
                wait(sp, t_x, n - 1, "x1")
                layer = layer_of(n, layer)
                t = n - layer * NT
                if layer:
                    sp.wait_ge(out_stored, 16 * (t + 1))
                sp.dma_start(xt[:], (out if layer else x_rows)[rows(t), :]).then_inc(x_loaded, 16)

            def load_preg(layer):
                wait(sp, v_w, layer * NB - 1, "mult")
                wait(sp, p_w, layer * NB - 1, "gain")
                sp.dma_start(preg[:], pre_g[layer].rearrange("(k p) -> p k", p=P),
                             allow_slow_non_contiguous=True).then_inc(preg_loaded, 16)

            def load_params(layer):
                n = layer * NT - 1
                wait(sp, v_b, n, "sinkd")
                wait(sp, a_b, n, "abs")
                wait(sp, t_b, n, "logit")
                sp.dma_start(ln_g[:], gm_ln_g[layer:layer + 1].broadcast_to([P, GM])).then_inc(params, 16)
                sp.dma_start(ln_b[:], gm_ln_b[layer:layer + 1].broadcast_to([P, GM])).then_inc(params, 16)
                sp.dma_start(gm_bias[:], gm_bs[layer].rearrange("h t -> t h"),
                             allow_slow_non_contiguous=True).then_inc(params, 16)
                sp.dma_start(wg2[:], gla_wg2[layer]).then_inc(params, 16)
                sp.dma_start(gate_b[:], gla_bg[layer].rearrange("(c o) -> c o", o=1),
                             allow_slow_non_contiguous=True).then_inc(params, 16)
                sp.dma_start(norm_g[:], gla_norm_g[layer:layer + 1].broadcast_to([P, HEAD])).then_inc(params, 16)
                sp.dma_start(sinks[:], swa_sinks[layer:layer + 1].broadcast_to([P, 8])).then_inc(params, 16)

            def load_gm_weights(layer):
                wait(sp, v_b, layer * NT - 1, "state")
                sp.dma_start(q_bd[:].rearrange("p (h c) -> p h c", h=GH),
                             gm_ws[layer].rearrange("h t c -> t h c")).then_inc(gmw_loaded, 16)

            def load_postg(layer):
                wait(sp, v_c, layer * NT - 1, "post")
                sp.dma_start(postg[:], post_g[layer:layer + 1].broadcast_to([P, D_MODEL])).then_inc(postg_loaded, 16)

            def iteration(n, layer, a, b, c, x):
                i = n % NT if isinstance(n, int) else None
                if x:
                    load_x(n + 1, layer)
                if b:
                    j = n - 1
                    t = j - layer_of(j, layer) * NT
                    wait(sp, v_b, j - 1, "xs")
                    sp.dma_start(rope[:], rope_dram[t] if isinstance(t, int) else
                                 rope_dram[bass.ds(t, 1)].rearrange("o p c -> (o p) c")).then_inc(rope_loaded, 16)
                if c:
                    k = n - 2
                    lk = layer_of(k, layer)
                    k_rows = rows(k - lk * NT)
                    wait(sp, v_c, k - 1, "add")
                    sp.dma_start(res[:], (out if lk else x_rows)[k_rows, :]).then_inc(res_loaded, 16)
                new_layer = i == NT - 1 and layer + 1 < DEPTH
                if new_layer:
                    load_preg(layer + 1)
                    load_block(layer + 1, 0)
                    load_block(layer + 1, 1)

                def blocks(*hooks):
                    for hook in hooks:
                        for l, blk in blocks_at(n, hook):
                            if blk + 2 < NB:
                                load_block(l, blk + 2)

                blocks(1, 2)
                if c:
                    wait(sp, v_c, k, "add")
                    sp.dma_start(out[k_rows, :], ot[:]).then_inc(out_stored, 16)
                if i == 0 and layer and n < NT * DEPTH:
                    load_params(layer)
                if i == 1 and layer and n < NT * DEPTH:
                    load_postg(layer)
                blocks(3)
                if i == 0 and layer and n < NT * DEPTH:
                    load_gm_weights(layer)
                blocks(4, 5, 6)

            load_preg(0)
            load_x(0, 0)
            load_block(0, 0)
            load_block(0, 1)
            load_params(0)
            load_gm_weights(0)
            load_postg(0)
            for b in range(2, N_FIRST + 2):
                load_block(0, b)
            run_pipeline(sp, iteration)
            sp.wait_ge(out_stored, 16 * NT * DEPTH)

        @block.tensor
        def _(pe):
            pe.wait_ge(const_ready, 1)

            def transpose_x(n):
                wait(pe, a_x, n, "scale")
                for half in range(2):
                    for q in range(4):
                        k = 4 * half + q
                        mm = pe.transpose(TR[half][:, q * P:(q + 1) * P], xt[:, k * P:(k + 1) * P], ident[:])
                    mm.then_inc(t_x.sem, 1)

            def chunk(n, c):
                if c == 0:
                    wait(pe, a_x, n, "hi1")
                    wait(pe, v_x, n, "lo1")
                for k in range(KC):
                    for part, (h, w) in enumerate(((h_hi, w_hi), (h_hi, w_lo), (h_lo, w_hi))):
                        mm = pe.matmul(PJ[c % 2][:, 0:CH], h[:, k, :], w[:, k, c * CH:(c + 1) * CH],
                                       start=(k == 0 and part == 0), stop=(k == KC - 1 and part == 2))
                mm.then_inc(t_a.sem, 1)

            def out_half(n, half):
                for k in range(KC):
                    for part, (h, w) in enumerate(((y_hi, wo_hi), (y_hi, wo_lo), (y_lo, wo_hi))):
                        mm = pe.matmul(PJ[half][:, :], h[:, k, :], w[:, k, half * 512:(half + 1) * 512],
                                       start=(k == 0 and part == 0), stop=(k == KC - 1 and part == 2))
                mm.then_inc(t_c.sem, 1)

            def scores(half):
                for r in range(2 * half, 2 * half + 2):
                    for g in range(2):
                        rows = slice(g * HEAD, (g + 1) * HEAD)
                        mm = pe.matmul(SC[g][:, (r % 2) * 2 * P:(r % 2 + 1) * 2 * P], qT[rows, r, :], kT[rows, :, :],
                                       start=True, stop=True)
                mm.then_inc(t_b.sem, 1)

            def prob_transposes(half):
                for g in range(2):
                    for c in range(4):
                        r, blk = 2 * half + c // 2, c % 2
                        mm = pe.transpose(TR[g][:, c * P:(c + 1) * P], s4[:, g, r, blk * P:(blk + 1) * P], ident[:])
                    mm.then_inc(t_b.sem, 1)

            def attend(half):
                for g in range(2):
                    for r2 in range(2):
                        head = 4 * g + 2 * half + r2
                        for blk in range(2):
                            mm = pe.matmul(GL[:, head * HEAD:(head + 1) * HEAD], pt4[:, g, 2 * r2 + blk, :],
                                           vv[:, blk, g * HEAD:(g + 1) * HEAD], start=(blk == 0), stop=(blk == 1))
                mm.then_inc(t_b.sem, 1)

            transpose_x(0)

            def iteration(n, layer, a, b, c, x):
                    j, k = n - 1, n - 2
                    i = n % NT if isinstance(n, int) else None

                    def wait_block(blk):
                        if i == 0:
                            wait(pe, a_w, layer * NB + blk, "hi3")
                            wait(pe, v_w, layer * NB + blk, "lo3")

                    def wait_out_block(blk):
                        if isinstance(k, int) and k % NT == 0:
                            wait(pe, a_w, k // NT * NB + blk, "hi3")
                            wait(pe, v_w, k // NT * NB + blk, "lo3")

                    if i == 1 and a:
                        pe.wait_ge(gmw_loaded, 16 * (layer + 1))
                        wait(pe, v_x, n, "lo1")
                        wait(pe, a_x, n, "hi1")
                        for h in range(GH):
                            mm = pe.transpose(TR[0][:, h * P:(h + 1) * P], q_bd[:, h * P:(h + 1) * P], ident[:])
                        mm.then_inc(gmw_t, 1)
                        pe.wait_ge(gmw_ready, layer + 1)
                    if b:
                        wait(pe, a_a, j, "c5")
                        wait(pe, v_x, j + 1 if a else j, "lo0")
                        wait(pe, a_x, j + 1 if a else j, "hi0")
                        pe.transpose(TR[0][:, 0:P], pj[:, C_GQ:C_GQ + P], ident[:])
                        pe.transpose(TR[0][:, P:2 * P], pj[:, C_GK:C_GK + P], ident[:])
                        pe.transpose(TR[0][0:RANK, 2 * P:3 * P], pj[:, C_GL:C_GL + RANK], ident[:]).then_inc(t_b.sem, 1)
                    if a:
                        wait(pe, a_a, n - 1, "c4")
                        wait_block(0)
                        wait_block(1)
                        chunk(n, 0)
                    if c:
                        wait(pe, a_b, k, "yscale")
                        if a:
                            wait(pe, v_x, n, "lo1")
                            wait(pe, a_x, n, "hi1")
                        if not b:
                            wait(pe, v_b, k, "pt1")
                            wait(pe, a_b, k, "pt1")
                        wait(pe, v_b, k, "pt1")
                        for q in range(4):
                            mm = pe.transpose(TR[1][:, q * P:(q + 1) * P], y[:, q * P:(q + 1) * P], ident[:])
                        mm.then_inc(t_c.sem, 1)
                        if b:
                            wait(pe, a_b, j, "low")
                        for q in range(4):
                            mm = pe.transpose(TR[0][:, q * P:(q + 1) * P], y[:, (q + 4) * P:(q + 5) * P], ident[:])
                        mm.then_inc(t_c.sem, 1)
                    if b:
                        wait(pe, v_l, j, "bias")
                        wait(pe, v_b, j - 1, "um")
                        wait(pe, v_b, j - 1, "o1")
                        pe.wait_ge(gmw_ready, layer_of(j, layer) + 1)
                        pe.wait_ge(params, 16 * N_PARAMS * (layer_of(j, layer) + 1))
                        for h in range(GH):
                            mm = pe.matmul(MX[:, h * HEAD:(h + 1) * HEAD], gm_wT[:, h, :],
                                           pj[:, C_V + h * HEAD:C_V + (h + 1) * HEAD], start=True, stop=True)
                        mm.then_inc(t_b.sem, 1)
                        wait(pe, a_b, j, "low")
                        wait(pe, v_b, j - 1, "att")
                        pe.matmul(GL[:, 0:P], wg2[:, :], g_low[:, :], start=True, stop=True).then_inc(t_b.sem, 1)
                    if a:
                        wait(pe, a_a, n - 1, "c5")
                        wait_block(2)
                        wait_block(3)
                        chunk(n, 1)
                    if b:
                        wait(pe, v_b, j, "rk2")
                        if c:
                            wait(pe, a_c, k, "hi0")
                            wait(pe, v_c, k, "lo0")
                        for r in range(4):
                            mm = pe.transpose(TR[1][:, r * P:(r + 1) * P], roped[:, r * P:(r + 1) * P], ident[:])
                        mm.then_inc(t_b.sem, 1)
                        if c:
                            wait(pe, a_c, k, "hi1")
                            wait(pe, v_c, k, "lo1")
                        pe.transpose(TR[0][:, 0:P], roped[:, 512:640], ident[:]).then_inc(t_b.sem, 1)
                    if c:
                        wait(pe, a_c, k, "hi1")
                        wait(pe, v_c, k, "lo1")
                        wait(pe, a_c, k - 1, "ev0")
                        if a:
                            wait(pe, a_a, n, "c0")
                        wait_out_block(N_WIN + 1)
                        out_half(k, 0)
                    if b:
                        wait(pe, a_b, j, "kT")
                        wait(pe, v_b, j - 1, "mask1")
                        pe.wait_ge(layer_state, layer_of(j, layer) + 1)
                        wait(pe, p_b, j - 1, "kcopy")
                        scores(0)
                    if c:
                        wait(pe, a_c, k - 1, "ev1")
                        if a:
                            wait(pe, a_a, n, "c1")
                        wait_out_block(N_WIN + 3)
                        out_half(k, 1)
                    if b:
                        wait(pe, v_b, j, "kdec")
                        for sub in range(NSUB):
                            cols = slice(sub * P, (sub + 1) * P)
                            mm = pe.matmul(GL[:, cols], k_ref[:, sub, :], q_bd[:, cols],
                                           start=True, stop=True)
                        mm.then_inc(t_b.sem, 1)
                        wait(pe, a_b, j, "kT")
                        pe.transpose(TR[0][:, 0:P], k_dec[:], ident[:]).then_inc(t_b.sem, 1)
                    if a:
                        wait(pe, a_a, n, "c0")
                        if c:
                            wait(pe, a_c, k, "ev0")
                        wait_block(4)
                        wait_block(5)
                        chunk(n, 2)
                    if b:
                        wait(pe, v_b, j, "mask0")
                        scores(1)
                        wait(pe, v_b, j, "am")
                        wait(pe, v_b, j, "sv")
                        wait(pe, v_b, j - 1, "state")
                        wait(pe, a_b, j, "gv")
                        pe.matmul(MX[:, 0:GLA], q_dec[:], state[:], start=True, stop=False, skip_group_check=True)
                        for h in range(GH):
                            mm = pe.matmul(MX[:, h * HEAD:(h + 1) * HEAD], a_mask[:, h, :],
                                           g_v[:, h * HEAD:(h + 1) * HEAD], start=False, stop=(h == GH - 1),
                                           skip_group_check=True)
                        mm.then_inc(t_b.sem, 1)
                        wait(pe, a_b, j, "kdn")
                        pe.matmul(MX[:, GLA:2 * GLA], k_decN[:], g_v[:], start=True, stop=True,
                                  skip_group_check=True).then_inc(t_b.sem, 1)
                    if a:
                        wait(pe, a_a, n, "c1")
                        if c:
                            wait(pe, a_c, k, "ev1")
                        wait_block(6)
                        wait_block(7)
                        chunk(n, 3)
                    if b:
                        wait(pe, a_b, j, "exp0")
                        wait(pe, a_b, j, "kdn")
                        wait(pe, a_b, j, "qT")
                        prob_transposes(0)
                    if a:
                        wait(pe, a_a, n, "c2")
                        wait_block(8)
                        wait_block(9)
                        chunk(n, 4)
                    if b:
                        wait(pe, a_b, j, "pt0")
                        wait(pe, v_b, j, "pt0")
                        wait(pe, a_b, j, "vv")
                        wait(pe, v_b, j, "am")
                        wait(pe, p_b, j - 1, "vcopy")
                        attend(0)
                        wait(pe, a_b, j, "exp1")
                        prob_transposes(1)
                    if a:
                        wait(pe, a_a, n, "c3")
                        wait_block(10)
                        wait_block(11)
                        chunk(n, 5)
                    if x:
                        if b:
                            wait(pe, a_b, j, "pt1")
                            wait(pe, v_b, j, "pt1")
                        transpose_x(n + 1)
                    if b:
                        wait(pe, a_b, j, "pt1")
                        wait(pe, v_b, j, "pt1")
                        attend(1)

            run_pipeline(pe, iteration)

        @block.scalar
        def _(act):
            copy = ACT.Copy
            for half in range(2):
                act.wait_ge(table_v, 15)
                act.activation(pt[:].rearrange("p (t e d) -> p t e d", t=NT, e=2)[:, :, half, :],
                               s_buf[:, 1024 + 512 * half:1536 + 512 * half].rearrange("p (t d) -> p t d", t=NT),
                               ACT.Sin).then_inc(table_a, 1)

            def x_scale(n):
                wait(act, p_x, n, "pow")
                act.activation(xt[:], xt[:], copy, scale=x_r[:, 0:1]).then_inc(a_x.sem, 1)

            def x_hi(n):
                wait(act, t_a, n - 1, "c5")
                for half in range(2):
                    wait(act, t_x, n, f"x{half}")
                    act.activation(h_hi[:, 4 * half:4 * half + 4, :], TR[half][:].rearrange("p (k t) -> p k t", k=4),
                                   copy).then_inc(a_x.sem, 1)

            def block_sum(layer, b):
                n = layer * NB + b
                act.wait_ge(raw_loaded[n % 2], 16 * (n // 2 + 1))
                wait(act, p_w, n - 2, "all")
                if b < N_WIN:
                    wait(act, t_a, layer * NT - 1, f"c{b // 2}")
                    w, room = WG, w_lo[:, :, b * WG:(b + 1) * WG]
                else:
                    wait(act, t_c, layer * NT - 1, "out1")
                    w, room = OG, wo_lo[:, :, (b - N_WIN) * OG:(b - N_WIN + 1) * OG]
                act.activation(room.bitcast(BF16), raw[:, n % 2, :, 0:w], ACT.Abs,
                               accum_out=part_sum[:, n % 2:n % 2 + 1]).then_inc(a_m.sem, 1)

            def split_hi(layer, b):
                n = layer * NB + b
                wait(act, v_w, n, "mult")
                if b < N_WIN:
                    wait(act, t_a, layer * NT - 1, f"c{b // 2}")
                else:
                    wait(act, t_c, layer * NT - 1, "out1")
                w, dst = (WG, w_hi[:, :, b * WG:(b + 1) * WG]) if b < N_WIN else \
                         (OG, wo_hi[:, :, (b - N_WIN) * OG:(b - N_WIN + 1) * OG])
                for k in range(KC):
                    mm = act.activation(dst[:, k, :], raw[:, n % 2, k, 0:w], copy, scale=wscale[:, n % 2, k:k + 1])
                    if k % 2:
                        mm.then_inc(a_w.sem, 1)

            x_scale(0)
            x_hi(0)
            block_sum(0, 0)
            for blk in range(N_FIRST):
                split_hi(0, blk)
                block_sum(0, blk + 1)

            def iteration(n, layer, a, b, c, x):
                    j, k = n - 1, n - 2

                    def splits(hook):
                        for l, blk in blocks_at(n, hook):
                            if starts_run(l, blk):
                                block_sum(l, blk)
                            split_hi(l, blk)
                            if blk + 1 < NB and not starts_run(l, blk + 1):
                                block_sum(l, blk + 1)

                    def evac(chunk):
                        wait(act, t_a, n, f"c{chunk}")
                        for g in range(2 * chunk, 2 * chunk + 2):
                            mm = act.activation(pj[:, g * WG:(g + 1) * WG], PJ[chunk % 2][:, (g % 2) * WG:(g % 2 + 1) * WG],
                                                copy, scale=unscale_in[:, g:g + 1])
                        mm.then_inc(a_a.sem, 1)

                    def probs(half):
                        wait(act, v_b, j, f"negm{half}")
                        for g in range(2):
                            for r in range(2 * half, 2 * half + 2):
                                head = 4 * g + r
                                mm = act.activation(s4[:, g, r, :], s4[:, g, r, :], ACT.Exp,
                                                    bias=neg_max[:, head:head + 1],
                                                    accum_out=row_sum[:, head:head + 1])
                        mm.then_inc(a_b.sem, 1)

                    if b:
                        wait(act, t_b, j, "gla")
                        wait(act, v_b, j - 1, "kdec")
                        act.activation(g_qk[:], TR[0][:, 0:2 * P].rearrange("p (e t) -> p e t", e=2), copy).then_inc(a_b.sem, 1)
                        wait(act, t_b, j - 1, "logit")
                        act.activation(g_low[:], TR[0][0:RANK, 2 * P:3 * P], copy).then_inc(a_b.sem, 1)
                        wait(act, t_b, j - 1, "u")
                        act.activation(g_v[:], pj[:, C_GV:C_GV + GLA], copy).then_inc(a_b.sem, 1)
                        wait(act, t_b, j - 1, "pv1")
                        wait(act, p_b, j - 1, "vcopy")
                        act.activation(vv[:, 1, :], pj[:, C_SV:C_SV + P], copy).then_inc(a_b.sem, 1)
                    if c:
                        wait(act, t_b, k, "pv1")
                        for half in range(2):
                            wait(act, t_c, k, f"y{half}")
                            act.activation(y_hi[:, 4 * half:4 * half + 4, :],
                                           TR[1 - half][:].rearrange("p (k t) -> p k t", k=4), copy).then_inc(a_c.sem, 1)
                    if b:
                        wait(act, t_c, j - 1, "y1")
                        if not c:
                            wait(act, a_b, j - 1, "yscale")
                        act.activation(y[:, 0:GM], pj[:, C_Z:C_Z + GM], ACT.Silu).then_inc(a_b.sem, 1)
                        act.activation(y[:, GM:GM + GLA], pj[:, C_GZ:C_GZ + GLA], ACT.Silu).then_inc(a_b.sem, 1)
                        act.activation(y[:, GM + GLA:], pj[:, C_SZ:C_SZ + SWA], ACT.Silu).then_inc(a_b.sem, 1)
                    if a:
                        if b:
                            wait(act, v_b, j, "gate_u")
                            wait(act, t_b, j, "gm")
                        evac(0)
                    if b:
                        wait(act, t_b, j, "logit")
                        wait(act, v_b, j - 1, "la")
                        act.wait_ge(params, 16 * N_PARAMS * (layer_of(j, layer) + 1))
                        act.activation(gate_a[:], GL[:, 0:P], ACT.Abs, bias=gate_b[:, 0:1]).then_inc(a_b.sem, 1)
                        wait(act, a_b, j, "abs")
                        act.activation(gate_a[:], gate_a[:], ACT.Exp, scale=-1.0).then_inc(a_b.sem, 1)
                        wait(act, a_b, j, "exp")
                        act.activation(gate_a[:], gate_a[:], ACT.Ln, bias=one[:, 0:1]).then_inc(a_b.sem, 1)
                    if a:
                        evac(1)
                    if b:
                        wait(act, t_b, j, "ropeq")
                        wait(act, t_b, j - 1, "sc1")
                        act.activation(qT[:], TR[1][:].rearrange("p (r t) -> p r t", r=4), copy,
                                       scale=float(HEAD) ** -0.5).then_inc(a_b.sem, 1)
                        wait(act, t_b, j, "ropek")
                        wait(act, p_b, j - 1, "kcopy")
                        act.activation(kT[:, 1, :], TR[0][:, 0:P], copy).then_inc(a_b.sem, 1)
                    splits(1)
                    if b:
                        wait(act, v_b, j, "refn")
                        wait(act, t_b, j - 1, "at")
                        for i in range(NSUB):
                            m = (i + 1) * SUB
                            mm = act.activation(k_ref[:, i, 0:m], cum[:, 0:m], ACT.Exp, scale=-1.0 / GATE_TAU,
                                                bias=ref_p[:, i:i + 1])
                        mm.then_inc(a_b.sem, 1)
                        wait(act, v_b, j - 1, "qbd")
                        for i in range(NSUB):
                            cols = slice(i * SUB, (i + 1) * SUB)
                            mm = act.activation(q_ref[:, cols], cum[:, cols], ACT.Exp, scale=1.0 / GATE_TAU,
                                                bias=ref_n[:, i:i + 1])
                        mm.then_inc(a_b.sem, 1)
                        wait(act, v_b, j - 1, "state")
                        act.activation(decay[:], cum[:], ACT.Exp, scale=1.0 / GATE_TAU).then_inc(a_b.sem, 1)
                        wait(act, t_b, j - 1, "kd")
                        act.activation(k_dec[:], cum[:], ACT.Exp, scale=-1.0 / GATE_TAU,
                                       bias=ref_p[:, NSUB:NSUB + 1]).then_inc(a_b.sem, 1)
                    if c:
                        wait(act, v_c, k, "fac")
                        wait(act, v_c, k - 1, "add")
                        if not (isinstance(k, int) and k == 0):
                            act.wait_ge(out_stored, k * 16)
                        for half in range(2):
                            wait(act, t_c, k, f"out{half}")
                            for g in range(2 * half, 2 * half + 2):
                                mm = act.activation(ot[:, g * OG:(g + 1) * OG], PJ[half][:, (g % 2) * OG:(g % 2 + 1) * OG],
                                                    copy, scale=fac[:, g:g + 1])
                            mm.then_inc(a_c.sem, 1)
                    if b:
                        wait(act, t_b, j, "kd")
                        wait(act, t_b, j - 1, "u")
                        act.activation(k_decN[:], TR[0][:, 0:P], copy).then_inc(a_b.sem, 1)
                    splits(2)
                    if b:
                        probs(0)
                    if a:
                        evac(2)
                    if b:
                        wait(act, t_b, j, "u")
                        wait(act, v_b, j, "ya")
                        act.activation(mix[:], MX[:, 0:GLA], ACT.Square).then_inc(a_b.sem, 1)
                        probs(1)
                        wait(act, v_b, j, "sinkd")
                        act.activation(sink_e[:], sink_e[:], ACT.Exp).then_inc(a_b.sem, 1)
                    splits(3)
                    if a:
                        if b:
                            wait(act, v_b, j, "xs")
                        evac(3)
                    if b:
                        wait(act, t_b, j, "pt0a")
                        wait(act, t_b, j - 1, "pv1")
                        wait(act, t_c, k, "out1")
                        act.activation(pt4[:, 0, :, :], TR[0][:].rearrange("p (c q) -> p c q", c=4), copy).then_inc(a_b.sem, 1)
                    splits(4)
                    if a:
                        evac(4)
                    if b:
                        wait(act, t_b, j, "pt1a")
                        act.activation(pt4[:, 0, :, :], TR[0][:].rearrange("p (c q) -> p c q", c=4), copy).then_inc(a_b.sem, 1)
                    splits(5)
                    if x:
                        x_scale(n + 1)
                    if a:
                        evac(5)
                    if x:
                        x_hi(n + 1)
                    if b:
                        wait(act, v_b, j, "yscale")
                        act.activation(y[:], y[:], copy, scale=y_scale[:, 0:1]).then_inc(a_b.sem, 1)
                    splits(6)

            run_pipeline(act, iteration)

        @block.vector
        def _(dve):
            tsteps = [0]

            def table(ins):
                tsteps[0] += 1
                ins.then_inc(table_v, 1)
                dve.wait_ge(table_v, tsteps[0])

            dve.wait_ge(pos_loaded, 32)
            ang, tmp = s_buf[:, 0:512], s_buf[:, 1024:1536]
            ang3 = ang.rearrange("p (t d) -> p t d", t=NT)
            table(dve.tensor_copy(s_buf[:, 560:576], s_buf[:, 512:528].bitcast(I32)))
            table(dve.tensor_tensor(ang3, s_buf[:, 560:576].unsqueeze(2).broadcast_to([P, NT, HEAD // 2]),
                                    s_buf[:, 528:560].unsqueeze(1).broadcast_to([P, NT, HEAD // 2]), ALU.mult))
            for half in range(2):
                arg = s_buf[:, 1024 + 512 * half:1536 + 512 * half]
                turns = s_buf[:, 512:1024] if half == 0 else s_buf[:, 512:1024]
                quarter = 0.25 if half == 0 else 0.0
                table(dve.tensor_scalar(turns, ang, 1.0 / (2.0 * np.pi), quarter, ALU.mult, ALU.add))
                table(dve.tensor_scalar(turns, turns, ROUND, ROUND, ALU.add, ALU.subtract))
                table(dve.scalar_tensor_tensor(arg, turns, -TWO_PI_HI, ang, ALU.mult, ALU.add))
                table(dve.scalar_tensor_tensor(arg, turns, -TWO_PI_LO, arg, ALU.mult, ALU.add))
                table(dve.tensor_scalar(arg, arg, quarter * 2.0 * np.pi, PI_SAFE, ALU.add, ALU.min))
                table(dve.tensor_scalar(arg, arg, -PI_SAFE, None, ALU.max))
            table(dve.memset(one[:], 1.0))
            dve.wait_ge(const_ready, 1)

            def x_stats_of(n):
                dve.wait_ge(x_loaded, 16 * (n + 1))
                for h in range(2):
                    ins = dve.bn_stats(x_stats[:, h, :], xt[:, h * 512:(h + 1) * 512])
                ins.then_inc(v_x.sem, 1)
                wait(dve, v_x, n, "stats")
                before_aggregate(dve)
                dve.bn_aggr(x_mv[:], x_stats[:]).then_inc(v_x.sem, 1)
                wait(dve, v_x, n, "aggr")
                dve.scalar_tensor_tensor(x_mv[:, 1:2], x_mv[:, 0:1], x_mv[:, 0:1], x_mv[:, 1:2],
                                         ALU.mult, ALU.add).then_inc(v_x.sem, 1)
                wait(dve, v_x, n, "msq")
                wait(dve, a_x, n - 1, "scale")
                dve.tensor_scalar(x_mv[:, 0:1], x_mv[:, 1:2], EPS, H_SCALE ** -2, ALU.add, ALU.mult).then_inc(v_x.sem, 1)

            def x_lo(n):
                wait(dve, t_a, n - 1, "c5")
                for half in range(2):
                    wait(dve, a_x, n, f"hi{half}")
                    dve.tensor_tensor(h_lo[:, 4 * half:4 * half + 4, :], TR[half][:].rearrange("p (k t) -> p k t", k=4),
                                      h_hi[:, 4 * half:4 * half + 4, :], ALU.subtract).then_inc(v_x.sem, 1)

            def split_scale(layer, b):
                n = layer * NB + b
                power, inverse = wpow[:, 0:1], wpow[:, 1:2]
                wait(dve, v_w, n - 1, "mult")
                wait(dve, p_w, n, "all")
                dve.tensor_scalar(power, bound[:, n % 2:n % 2 + 1], TINY, None, ALU.max).then_inc(v_w.sem, 1)
                wait(dve, v_w, n, "guard")
                dve.tensor_scalar(power.bitcast(U32), power.bitcast(U32), EXP_BITS, None, ALU.bitwise_and).then_inc(v_w.sem, 1)
                wait(dve, v_w, n, "bits")
                dve.reciprocal(inverse, power).then_inc(v_w.sem, 1)
                if b < N_WIN:
                    wait(dve, a_a, layer * NT - 1, f"c{b // 2}")
                    dve.tensor_scalar(unscale_in[:, b:b + 1], power, 1.0 / (TOP * H_SCALE), None,
                                      ALU.mult).then_inc(v_w.sem, 1)
                else:
                    wait(dve, v_c, layer * NT - 1, "fac")
                    dve.tensor_scalar(unscale_out[:, b - N_WIN:b - N_WIN + 1], power, 1.0 / TOP, None,
                                      ALU.mult).then_inc(v_w.sem, 1)
                wait(dve, v_w, n, "recip")
                wait(dve, v_w, n - 2, "lo3")
                wait(dve, a_w, n - 2, "hi3")
                gain = preg[:] if b < N_WIN else one[:, 0:1].broadcast_to([P, KC])
                dve.tensor_scalar(wscale[:, n % 2, :], gain, inverse, TOP, ALU.mult, ALU.mult).then_inc(v_w.sem, 1)

            def split_lo(layer, b):
                n = layer * NB + b
                w, hi, lo, at = (WG, w_hi, w_lo, b * WG) if b < N_WIN else (OG, wo_hi, wo_lo, (b - N_WIN) * OG)
                for k in range(KC):
                    if k % 2 == 0:
                        wait(dve, a_w, n, f"hi{k // 2}")
                    ins = dve.scalar_tensor_tensor(lo[:, k, at:at + w], raw[:, n % 2, k, 0:w], wscale[:, n % 2, k:k + 1],
                                                   hi[:, k, at:at + w], ALU.mult, ALU.subtract)
                    if k % 2:
                        ins.then_inc(v_w.sem, 1)

            def prepare_preg(layer):
                dve.wait_ge(preg_loaded, 16 * (layer + 1))
                wait(dve, p_w, layer * NB - 1, "gain")
                dve.tensor_reduce(preg_top[:], preg[:], AX.X, ALU.max, apply_absolute_value=True).then_inc(preg_ready, 1)

            prepare_preg(0)
            x_stats_of(0)
            x_lo(0)
            split_scale(0, 0)
            for blk in range(N_FIRST):
                split_lo(0, blk)
                split_scale(0, blk + 1)

            def iteration(n, layer, a, b, c, x):
                    j, k = n - 1, n - 2
                    i = n % NT if isinstance(n, int) else None

                    def splits(hook):
                        for l, blk in blocks_at(n, hook):
                            if l and blk == 0:
                                prepare_preg(l)
                            if starts_run(l, blk):
                                split_scale(l, blk)
                            split_lo(l, blk)
                            if blk + 1 < NB and not starts_run(l, blk + 1):
                                split_scale(l, blk + 1)

                    def b_wait(step):
                        wait(dve, v_b, j, step)

                    def b_done(ins):
                        ins.then_inc(v_b.sem, 1)

                    def mask_max(half):
                        wait(dve, t_b, j, f"sc{half}")
                        first = isinstance(j, int) and j % NT == 0
                        r2 = slice(2 * half, 2 * half + 2)
                        for g in range(2):
                            ins = dve.tensor_tensor(s4[:, g, r2, :], SC[g][:].rearrange("p (r k) -> p r k", r=2),
                                                    band[:, 0 if first else 1, :].unsqueeze(1).broadcast_to([P, 2, 2 * P]),
                                                    ALU.add)
                        b_done(ins)
                        b_wait(f"mask{half}")
                        heads = [t[:].rearrange("p (g r) -> p g r", g=2)[:, :, r2] for t in (row_max, neg_max, sinks)]
                        wait(dve, v_b, j - 1, "sinkd")
                        b_done(dve.tensor_reduce(heads[0], s4[:, :, r2, :], AX.X, ALU.max))
                        b_wait(f"max{half}")
                        b_done(dve.tensor_tensor(heads[0], heads[0], heads[2], ALU.max))
                        b_wait(f"neg{half}")
                        b_done(dve.tensor_scalar(heads[1], heads[0], -1.0, None, ALU.mult))

                    if i == 1 and a:
                        dve.wait_ge(gmw_t, layer + 1)
                        wait(dve, t_b, layer * NT - 1, "gm")
                        dve.tensor_tensor(gm_wT[:], TR[0][:].rearrange("p (h t) -> p h t", h=GH),
                                          causal[:].unsqueeze(1).broadcast_to([P, GH, P]), ALU.mult).then_inc(gmw_ready, 1)
                    if b:
                        wait(dve, a_a, j, "c5")
                        dve.wait_ge(rope_loaded, 16 * (j + 1))
                        wait(dve, t_b, j - 1, "pt1b")
                        wait(dve, v_b, j - 1, "yc")
                        qk = pj[:, C_SQ:C_SQ + 640].rearrange("p (m d) -> p m d", d=HEAD // 2)
                        for half, dst in ((0, xc), (1, xs)):
                            b_done(dve.tensor_tensor(dst.rearrange("p (m d) -> p m d", d=HEAD // 2), qk,
                                                     rope[:, 32 * half:32 * half + 32].unsqueeze(1).broadcast_to([P, 20, 32]),
                                                     ALU.mult))
                        b_wait("xs")
                        qc = xc[:, 0:512].rearrange("p (g r e d) -> p g r e d", g=2, r=4, e=2)
                        qs = xs[:, 0:512].rearrange("p (g r e d) -> p g r e d", g=2, r=4, e=2)
                        qo = roped[:, 0:512].rearrange("p (r g e d) -> p g r e d", r=4, g=2, e=2)
                        kc, ks, ko = (halves(t[:, 512:640], 2) for t in (xc, xs, roped))
                        b_done(dve.tensor_tensor(qo[:, :, :, 0, :], qc[:, :, :, 0, :], qs[:, :, :, 1, :], ALU.subtract))
                        b_done(dve.tensor_tensor(qo[:, :, :, 1, :], qc[:, :, :, 1, :], qs[:, :, :, 0, :], ALU.add))
                        b_done(dve.tensor_tensor(ko[:, :, 0, :], kc[:, :, 0, :], ks[:, :, 1, :], ALU.subtract))
                        b_done(dve.tensor_tensor(ko[:, :, 1, :], kc[:, :, 1, :], ks[:, :, 0, :], ALU.add))
                    if c:
                        for half in range(2):
                            wait(dve, t_b, k, "pv1")
                            wait(dve, a_c, k, f"hi{half}")
                            dve.tensor_tensor(y_lo[:, 4 * half:4 * half + 4, :], TR[1 - half][:].rearrange("p (k t) -> p k t", k=4),
                                              y_hi[:, 4 * half:4 * half + 4, :], ALU.subtract).then_inc(v_c.sem, 1)
                        wait(dve, v_b, k, "yun")
                        wait(dve, a_c, k - 1, "ev1")
                        if isinstance(k, int) and k % NT == 0:
                            wait(dve, v_w, k // NT * NB + NB - 1, "lo3")
                        dve.tensor_scalar(fac[:], unscale_out[:], y_unscale[:, 0:1], None, ALU.mult).then_inc(v_c.sem, 1)
                    if b:
                        dve.wait_ge(params, 16 * N_PARAMS * (layer_of(j, layer) + 1))
                        wait(dve, a_b, j, "silu_a")
                        b_done(dve.tensor_tensor(y[:, 0:GM], y[:, 0:GM], pj[:, C_U:C_U + GM], ALU.mult))
                        wait(dve, a_b, j, "silu_b")
                        y_gla = y[:, GM:GM + GLA].rearrange("p (h d) -> p h d", h=GH)
                        b_done(dve.tensor_tensor(y_gla, y_gla, norm_g[:].unsqueeze(1).broadcast_to([P, GH, HEAD]), ALU.mult))
                    splits(1)
                    if b:
                        wait(dve, a_b, j, "abs")
                        wait(dve, v_b, j - 1, "cum")
                        b_done(dve.tensor_scalar(gate_m[:], GL[:, 0:P], gate_b[:, 0:1], 0.0, ALU.add, ALU.min))
                        b_wait("min")
                        wait(dve, a_b, j, "ln")
                        b_done(dve.tensor_tensor(gate_m[:], gate_m[:], gate_a[:], ALU.subtract))
                        b_wait("la")
                        wait(dve, a_b, j - 1, "kdec")
                        b_done(dve.tensor_tensor_scan(cum[:], one[:, 0:1].broadcast_to([P, P]), gate_m[:], 0.0,
                                                      ALU.mult, ALU.add))
                        b_wait("cum")
                        dve.tensor_scalar(ref_p[:, 0:NSUB], cum[:, SUB // 2 - 1::SUB], 1.0 / GATE_TAU, None, ALU.mult)
                        b_done(dve.tensor_scalar(ref_p[:, NSUB:NSUB + 1], cum[:, P - 1:P], 1.0 / GATE_TAU, None, ALU.mult))
                        b_wait("refs")
                        b_done(dve.tensor_scalar(ref_n[:], ref_p[:, 0:NSUB], -1.0, None, ALU.mult))
                        wait(dve, t_b, j, "gm")
                        wait(dve, v_b, j - 1, "yb")
                        mix4 = mix[:].rearrange("p (h d) -> p h d", h=GH)
                        mx4 = MX[:, 0:GM].rearrange("p (h d) -> p h d", h=GH)
                        b_done(dve.tensor_tensor(mix4, mx4, gm_bias[:].unsqueeze(2).broadcast_to([P, GH, HEAD]), ALU.add))
                        b_wait("sv")
                        b_done(dve.tensor_tensor(y[:, 0:GM], y[:, 0:GM], mix[:], ALU.mult))
                        wait(dve, a_b, j, "kref")
                        b_done(dve.tensor_tensor(k_ref[:], k_ref[:], g_qk[:, 1, :].unsqueeze(1).broadcast_to([P, NSUB, P]),
                                                 ALU.mult))
                        wait(dve, a_b, j, "qref")
                        b_done(dve.scalar_tensor_tensor(q_ref[:], g_qk[:, 0, :], float(GK) ** -0.5, q_ref[:],
                                                        ALU.mult, ALU.mult))
                        b_wait("qref")
                        wait(dve, t_b, j - 1, "o")
                        b_done(dve.tensor_tensor(
                            q_bd[:].rearrange("p (i h t) -> p i h t", i=NSUB, h=GH),
                            q_ref[:].rearrange("p (i t) -> p i t", i=NSUB).unsqueeze(2).broadcast_to([P, NSUB, GH, SUB]),
                            head_mask[:].unsqueeze(1).unsqueeze(3).broadcast_to([P, NSUB, GH, SUB]), ALU.mult))
                        wait(dve, a_b, j, "decay")
                        wait(dve, v_b, j - 1, "state")
                        b_done(dve.tensor_copy(tile_decay[:], decay[:, P - 1:P]))
                        b_wait("dlast")
                        b_done(dve.scalar_tensor_tensor(q_dec[:], g_qk[:, 0, :], float(GK) ** -0.5, decay[:],
                                                        ALU.mult, ALU.mult))
                        wait(dve, a_b, j, "kdec")
                        b_done(dve.tensor_tensor(k_dec[:], k_dec[:], g_qk[:, 1, :], ALU.mult))
                        wait(dve, t_b, j, "at")
                        b_done(dve.tensor_tensor(
                            a_mask.rearrange("p h (i t) -> p i h t", i=NSUB),
                            GL[:].rearrange("p (i h t) -> p i h t", i=NSUB, h=GH),
                            causal[:].rearrange("p (i t) -> p i t", i=NSUB).unsqueeze(2).broadcast_to([P, NSUB, GH, SUB]),
                            ALU.mult))
                    splits(2)
                    if b:
                        mask_max(0)
                    if c:
                        wait(dve, a_c, k, "ev1")
                        for h in range(2):
                            ins = dve.bn_stats(o_stats[:, h, :], ot[:, h * 512:(h + 1) * 512])
                        ins.then_inc(v_c.sem, 1)
                        wait(dve, v_c, k, "stats")
                        before_aggregate(dve)
                        dve.bn_aggr(o_mv[:], o_stats[:]).then_inc(v_c.sem, 1)
                        wait(dve, v_c, k, "aggr")
                        dve.scalar_tensor_tensor(o_mv[:, 1:2], o_mv[:, 0:1], o_mv[:, 0:1], o_mv[:, 1:2],
                                                 ALU.mult, ALU.add).then_inc(v_c.sem, 1)
                        wait(dve, v_c, k, "msq")
                        dve.tensor_scalar(o_mv[:, 0:1], o_mv[:, 1:2], EPS, None, ALU.add).then_inc(v_c.sem, 1)
                    if b:
                        mask_max(1)
                        b_wait("negm1")
                        wait(dve, v_b, j - 1, "den")
                        b_done(dve.tensor_tensor(sink_e[:], sinks[:], neg_max[:], ALU.add))
                    if c:
                        dve.wait_ge(postg_loaded, 16 * (layer_of(k, layer) + 1))
                        wait(dve, p_c, k, "pow")
                        dve.scalar_tensor_tensor(ot[:], ot[:], out_r[:, 0:1], postg[:], ALU.mult, ALU.mult).then_inc(v_c.sem, 1)
                        wait(dve, v_c, k, "post")
                        dve.wait_ge(res_loaded, 16 * (k + 1))
                        dve.tensor_tensor(ot[:], ot[:], res[:], ALU.add).then_inc(v_c.sem, 1)
                    if a:
                        wait(dve, a_a, n, "c1")
                        wait(dve, v_l, n - 1, "norm")
                        dve.bn_stats(v_stats[:], pj[:, C_V:C_V + GM]).then_inc(v_l.sem, 1)
                        wait(dve, v_l, n, "stats")
                        before_aggregate(dve)
                        dve.bn_aggr(v_mv[:], v_stats[:]).then_inc(v_l.sem, 1)
                        wait(dve, v_l, n, "aggr")
                        wait(dve, p_l, n - 1, "pow")
                        dve.tensor_scalar(v_mv[:, 1:2], v_mv[:, 1:2], EPS, None, ALU.add).then_inc(v_l.sem, 1)
                    splits(3)
                    if a:
                        dve.wait_ge(params, 16 * N_PARAMS * (layer + 1))
                        wait(dve, p_l, n, "pow")
                        dve.tensor_scalar(pj[:, C_V:C_V + GM], pj[:, C_V:C_V + GM], v_mv[:, 0:1], v_r[:, 0:1],
                                          ALU.subtract, ALU.mult).then_inc(v_l.sem, 1)
                        wait(dve, v_l, n, "norm")
                        dve.tensor_tensor(pj[:, C_V:C_V + GM], pj[:, C_V:C_V + GM], ln_g[:], ALU.mult).then_inc(v_l.sem, 1)
                        wait(dve, v_l, n, "gain")
                        dve.tensor_tensor(pj[:, C_V:C_V + GM], pj[:, C_V:C_V + GM], ln_b[:], ALU.add).then_inc(v_l.sem, 1)
                    if b:
                        wait(dve, a_b, j, "sq")
                        b_done(dve.tensor_tensor(update.rearrange("p (h d) -> p h d", h=GH),
                                                 MX[:, GLA:2 * GLA].rearrange("p (h d) -> p h d", h=GH),
                                                 head_mask[:].unsqueeze(2).broadcast_to([P, GH, HEAD]), ALU.mult))
                        b_wait("um")
                        b_done(dve.scalar_tensor_tensor(state[:], state[:], tile_decay[:, 0:1], update, ALU.mult, ALU.add))
                        wait(dve, a_b, j, "sq")
                        b_done(dve.tensor_reduce(o_sum[:], mix4, AX.X, ALU.add))
                        b_wait("ored")
                        b_done(dve.tensor_scalar(o_sum[:], o_sum[:], 1.0 / HEAD, EPS, ALU.mult, ALU.add))
                        wait(dve, p_b, j, "o_pow")
                        b_done(dve.tensor_tensor(mix4, mx4, o_r[:].unsqueeze(2).broadcast_to([P, GH, HEAD]), ALU.mult))
                        b_wait("o1")
                        b_done(dve.tensor_tensor(y[:, GM:GM + GLA], y[:, GM:GM + GLA], mix[:], ALU.mult))
                        wait(dve, t_b, j, "pt0b")
                        wait(dve, t_c, k, "out1")
                        b_done(dve.tensor_copy(pt4[:, 1, :, :], TR[1][:].rearrange("p (c q) -> p c q", c=4)))
                    splits(4)
                    if x:
                        x_stats_of(n + 1)
                    if b:
                        wait(dve, t_b, j, "pt1b")
                        b_done(dve.tensor_copy(pt4[:, 1, :, :], TR[1][:].rearrange("p (c q) -> p c q", c=4)))
                        wait(dve, a_b, j, "sink")
                        b_done(dve.tensor_tensor(denom[:], row_sum[:], sink_e[:], ALU.add))
                        b_wait("den")
                        b_done(dve.reciprocal(denom[:], denom[:]))
                    splits(5)
                    if x:
                        x_lo(n + 1)
                    if b:
                        wait(dve, t_b, j, "pv1")
                        b_wait("recip")
                        b_done(dve.tensor_tensor(att.rearrange("p (h d) -> p h d", h=8), GL[:].rearrange("p (h d) -> p h d", h=8),
                                                 denom[:].unsqueeze(2).broadcast_to([P, 8, HEAD]), ALU.mult))
                        b_wait("att")
                        wait(dve, a_b, j, "silu_c")
                        b_done(dve.tensor_tensor(y[:, GM + GLA:], y[:, GM + GLA:], att, ALU.mult))
                        b_wait("yc")
                        b_done(dve.tensor_reduce(y_max[:], y[:], AX.X, ALU.max, apply_absolute_value=True))
                        b_wait("ymax")
                        b_done(dve.tensor_scalar(y_max[:], y_max[:], TINY, None, ALU.max))
                        b_wait("yguard")
                        bits = y_max[:].bitcast(U32)
                        b_done(dve.tensor_scalar(bits, bits, EXP_BITS, None, ALU.bitwise_and))
                        b_wait("ybits")
                        wait(dve, a_b, j - 1, "yscale")
                        b_done(dve.reciprocal(y_scale[:], y_max[:]))
                        b_wait("yrecip")
                        b_done(dve.tensor_scalar(y_scale[:], y_scale[:], TOP, None, ALU.mult))
                        wait(dve, v_c, j - 1, "fac")
                        b_done(dve.tensor_scalar(y_unscale[:], y_max[:], 1.0 / TOP, None, ALU.mult))

                    splits(6)

            run_pipeline(dve, iteration)

        @block.gpsimd
        def _(pool):
            own = sem("pool_constants")
            pool.memset(ident[:], 0.0)
            pool.memset(causal[:], 1.0)
            pool.memset(pool_one[:], 1.0)
            pool.memset(band[:], 0.0)
            pool.memset(head_mask[:], 1.0)
            pool.memset(k_ref[:], 0.0)
            pool.memset(neg_half[:], -0.5).then_inc(own, 1)
            pool.wait_ge(own, 1)
            pool.affine_select(out=ident[:], in_=ident[:], compare_op=ALU.not_equal, fill=1.0, base=0,
                               pattern=[[-1, P]], channel_multiplier=1)
            pool.affine_select(out=causal[:], in_=causal[:], compare_op=ALU.is_ge, fill=0.0, base=0,
                               pattern=[[1, P]], channel_multiplier=-1)
            for v in range(2):
                pool.affine_select(out=band[:, v, P:], in_=band[:, v, P:], compare_op=ALU.is_ge, fill=NEG, base=0,
                                   pattern=[[-1, P]], channel_multiplier=1)
            pool.affine_select(out=band[:, 1, 0:P], in_=band[:, 1, 0:P], compare_op=ALU.is_gt, fill=NEG, base=0,
                               pattern=[[1, P]], channel_multiplier=-1)
            pool.memset(band[:, 0, 0:P], NEG)
            pool.affine_select(out=head_mask[:], in_=head_mask[:], compare_op=ALU.is_ge, fill=0.0, base=0,
                               pattern=[[-GK, GH]], channel_multiplier=1).then_inc(own, 1)
            pool.wait_ge(own, 2)
            pool.affine_select(out=head_mask[:], in_=head_mask[:], compare_op=ALU.is_ge, fill=0.0, base=GK - 1,
                               pattern=[[GK, GH]], channel_multiplier=-1).then_inc(const_ready, 1)
            pool.wait_ge(const_ready, 1)

            def x_pow(n):
                wait(pool, v_x, n, "eps")
                wait(pool, a_x, n - 1, "scale")
                pool.tensor_tensor(x_r[:], x_mv[:, 0:1], neg_half[:, 0:1], ALU.pow).then_inc(p_x.sem, 1)

            def block_bound(layer, b):
                n = layer * NB + b
                side = slice(n % 2, n % 2 + 1)
                wait(pool, a_m, n, "sum")
                pool.wait_ge(preg_ready, layer + 1)
                pool.tensor_tensor(part_bound[:, side], part_sum[:, side], (preg_top if b < N_WIN else pool_one)[:, 0:1],
                                   ALU.mult).then_inc(p_w.sem, 1)
                wait(pool, p_w, n, "gain")
                wait(pool, v_w, n - 2, "guard")
                pool.partition_all_reduce(bound[:, side], part_bound[:, side], P, ABSMAX).then_inc(p_w.sem, 1)

            x_pow(0)
            for blk in range(N_FIRST + 1):
                block_bound(0, blk)

            def iteration(n, layer, a, b, c, x):
                j, k = n - 1, n - 2
                i = n % NT if isinstance(n, int) else None

                def splits(hook):
                    for l, blk in blocks_at(n, hook):
                        if starts_run(l, blk):
                            block_bound(l, blk)
                        if blk + 1 < NB and not starts_run(l, blk + 1):
                            block_bound(l, blk + 1)

                if i == 1 and a:
                    wait(pool, t_b, j - 1, "pv1")
                    wait(pool, p_b, j - 1, "vcopy")
                    wait(pool, v_b, j - 1, "state")
                    pool.memset(kT[:, 0, :], 0.0)
                    pool.memset(vv[:, 0, :], 0.0)
                    pool.memset(state[:], 0.0).then_inc(layer_state, 1)
                splits(1)
                splits(2)
                if c:
                    wait(pool, v_c, k, "eps")
                    wait(pool, v_c, k - 1, "post")
                    pool.tensor_tensor(out_r[:], o_mv[:, 0:1], neg_half[:, 0:1], ALU.pow).then_inc(p_c.sem, 1)
                if a:
                    wait(pool, v_l, n, "eps")
                    wait(pool, v_l, n - 1, "norm")
                    pool.tensor_tensor(v_r[:], v_mv[:, 1:2], neg_half[:, 0:1], ALU.pow).then_inc(p_l.sem, 1)
                splits(3)
                if b:
                    wait(pool, v_b, j, "oeps")
                    pool.tensor_tensor(o_r[:], o_sum[:], neg_half[:], ALU.pow).then_inc(p_b.sem, 1)
                    wait(pool, t_b, j, "sc1")
                    pool.tensor_tensor(kT[:, 0, :], kT[:, 1, :], pool_one[:, 0:1].broadcast_to([P, P]),
                                       ALU.mult).then_inc(p_b.sem, 1)
                splits(4)
                if x:
                    x_pow(n + 1)
                splits(5)
                if b:
                    wait(pool, t_b, j, "pv1")
                    pool.tensor_tensor(vv[:, 0, :], vv[:, 1, :], pool_one[:, 0:1].broadcast_to([P, P]),
                                       ALU.mult).then_inc(p_b.sem, 1)
                splits(6)

            run_pipeline(pool, iteration)


_INS = ["x", "positions", "pre_g", "w_in", "gm_ln_g", "gm_ln_b", "gm_ws", "gm_bs", "gla_wg2", "gla_bg",
        "gla_norm_g", "swa_sinks", "w_out", "post_g"]


def kernel(**inputs):
    import concourse.bacc as _bacc
    from concourse.bass_utils import run_bass_kernel_spmd as _run

    nc = _bacc.Bacc("TRN2", target_bir_lowering=False, num_devices=1)
    arrays = {n: np.ascontiguousarray(inputs[n]) for n in _INS}
    arrays["x"] = arrays["x"].reshape(SEQ, D_MODEL)
    arrays["inv_freq"] = (ROPE_THETA ** (-np.arange(HEAD // 2) * 2.0 / HEAD)).astype(np.float32).reshape(1, -1)
    aps = [nc.dram_tensor("in_" + n, a.shape, mybir.dt.from_np(a.dtype), kind="ExternalInput").ap()
           for n, a in arrays.items()]
    out = nc.dram_tensor("out_y", (SEQ, D_MODEL), F32, kind="ExternalOutput").ap()
    hybrid_trunk(nc, *aps, out)
    r = _run(nc, [{"in_" + n: a for n, a in arrays.items()}], core_ids=[0])
    return r.results[0]["out_y"].reshape(1, SEQ, D_MODEL)
```

```python
from contextlib import ExitStack

import numpy as np

import concourse.bass as bass
from concourse import mybir

F32 = mybir.dt.float32
F16 = mybir.dt.float16
BF16 = mybir.dt.bfloat16
I32 = mybir.dt.int32
U32 = mybir.dt.uint32
ALU = mybir.AluOpType
ACT = mybir.ActivationFunctionType
AX = mybir.AxisListType
ABSMAX = bass.bass_isa.ReduceOp.max

P = 128
D_MODEL, SEQ, DEPTH = 1024, 2048, 2
NT = SEQ // P
KC = D_MODEL // P
HEAD = 64
EPS = 1e-6
GM, GLA, SWA = 256, 256, 512
GH, GK = 4, 32
GATE_TAU = 16.0
NSUB, SUB = 4, 32
ROPE_THETA = 10000.0

C_U, C_V, C_Z = 0, 256, 512
C_GQ, C_GK, C_GV, C_GL, C_GZ = 768, 896, 1024, 1280, 1296
C_SQ, C_SK, C_SV, C_SZ = 1552, 2064, 2192, 2320
D_IN = 2832
RANK = C_GZ - C_GL
N_CHUNK = 6
CH = D_IN // N_CHUNK
WG = CH // 2
N_WIN = D_IN // WG
OG = 256
N_WOUT = D_MODEL // OG
RAW_W = max(WG, OG)
HI_ACT = 6

H_SCALE = 2.0 ** 10
P_SCALE = 2.0 ** 15
TOP = 2.0 ** 14
NEG = -1.0e30
TINY = 1.0e-30
EXP_BITS = 0x7F800000
ROUND = 12582912.0
TWO_PI_HI, TWO_PI_LO = 6.28125, 0.0019353071795864769
PI_SAFE = 3.1415925


class Stage:

    def __init__(self, sem, steps):
        self.sem = sem
        self.steps = steps.split()
        assert len(set(self.steps)) == len(self.steps)

    def after(self, n, step):
        assert not isinstance(n, int) or n >= 0
        return n * len(self.steps) + (self.steps.index(step) + 1)


def began(n):
    return not isinstance(n, int) or n >= 0


def hybrid_trunk(nc, x, positions, pre_g, w_in, gm_ln_g, gm_ln_b, gm_ws, gm_bs, gla_wg2, gla_bg,
                 gla_norm_g, swa_sinks, w_out, post_g, inv_freq, out):
    with ExitStack() as ctx:
        def sb(name, shape, dt=F32):
            return ctx.enter_context(nc.sbuf_tensor(name, shape, dt))

        def bank(name):
            return ctx.enter_context(nc.psum_tensor(name, [P, 512], F32))

        def sem(name):
            return ctx.enter_context(nc.semaphore(name))

        rope_dram = nc.dram_tensor("rope_tables", (NT, P, HEAD), F32, kind="Internal").ap()

        columns = sb("columns", [P, 200])
        used = [0]

        def col(n, *shape):
            at = used[0]
            used[0] += n
            ap = columns[:, at:at + n]
            return ap if not shape else ap.rearrange("p (a b) -> p a b", a=shape[0])

        w_hi = sb("w_hi", [P, KC, D_IN], F16)
        w_lo = sb("w_lo", [P, KC, D_IN], F16)
        wo_hi = sb("wo_hi", [P, KC, D_MODEL], F16)
        wo_lo = sb("wo_lo", [P, KC, D_MODEL], F16)
        raw = sb("raw", [P, 2, KC, RAW_W])
        part_sum = col(2)
        part_bound = col(2)
        bound = col(2)
        wpow = col(2)
        wscale = col(2 * KC, 2)
        unscale_in = col(N_WIN)
        unscale_out = col(N_WOUT)
        att_pow = col(1)
        qk_scale = col(1)
        score_unscale = col(1)
        v_scale = col(1)
        preg = col(KC)
        preg_top = col(1)
        postg = sb("postg", [P, D_MODEL])
        ln_g = sb("ln_g", [P, GM])
        ln_b = sb("ln_b", [P, GM])
        gm_wT = sb("gm_wT", [P, GH, P])
        gm_bias = col(GH)
        wg2 = sb("wg2", [RANK, P])
        gate_b = col(1)
        norm_g = sb("norm_g", [P, HEAD])
        sinks = col(8)
        ident = sb("ident", [P, P])
        ident16 = sb("ident16", [P, P], F16)
        causal = sb("causal", [P, P])
        band = sb("band", [P, 3 * P])
        head_mask = col(GH)
        one = col(1)
        unused = col(1)
        pool_one = col(1)
        neg_half = col(GH)
        xt = sb("xt", [P, D_MODEL])
        h_hi = sb("h_hi", [P, KC, P], F16)
        h_lo = sb("h_lo", [P, KC, P], F16)
        x_stats = col(2 * 6, 2)
        x_mv = col(2)
        x_r = col(1)
        pj = sb("pj", [P, D_IN])
        y = sb("y", [P, D_MODEL])
        s_buf = sb("s_buf", [P, 8 * 2 * P])
        pt = sb("pt", [P, 2 * 4 * P])
        qT = sb("qT", [P, 8, P], F16)
        kT = sb("kT", [P, 3, 2, P], F16)
        vv = sb("vv", [P, 2, 2, P], F16)
        rope = sb("rope", [P, HEAD])
        row_max = col(8)
        neg_max = col(8)
        row_sum = col(8)
        sink_e = col(8)
        denom = col(8)
        g_v = sb("g_v", [P, GLA])
        g_qk = sb("g_qk", [P, 2, P])
        g_low = sb("g_low", [RANK, P])
        gate_a = sb("gate_a", [P, P])
        gate_m = sb("gate_m", [P, P])
        cum = sb("cum", [P, P])
        ref_p = col(NSUB + 1)
        ref_n = col(NSUB)
        k_ref = sb("k_ref", [P, NSUB, P])
        q_ref = gate_m
        q_bd = sb("q_bd", [P, NSUB * GH * SUB])
        decay = sb("decay", [P, P])
        q_dec = decay
        tile_decay = col(1)
        k_dec = sb("k_dec", [P, P])
        k_decN = gate_a
        state = sb("state", [P, GLA])
        update = q_bd[:, 0:GLA]
        mix = sb("mix", [P, GLA])
        o_sum = col(GH)
        o_r = col(GH)
        v_stats = col(6)
        v_mv = col(2)
        v_r = col(1)
        y_max = col(1)
        y_scale = col(1)
        y_unscale = col(1)
        y_parts = pt[:].bitcast(F16).rearrange("p (s k t) -> p s k t", s=2, k=KC)
        y_hi, y_lo = y_parts[:, 0], y_parts[:, 1]
        fac = col(N_WOUT)
        ot = sb("ot", [P, D_MODEL])
        res = sb("res", [P, D_MODEL])
        o_stats = col(2 * 6, 2)
        o_mv = col(2)
        out_r = col(1)

        PJ = [bank("PJ0"), bank("PJ1")]
        TR = [bank("TR0"), bank("TR1")]
        SC = [bank("SC0"), bank("SC1")]
        MX = bank("MX")
        GL = bank("GL")

        s4 = s_buf[:].rearrange("p (g r k) -> p g r k", g=2, r=4)
        xc, xs = s_buf[:, 0:640], s_buf[:, 640:1280]
        roped = s_buf[:, 1280:1920]
        qk_parts = s_buf[:, 0:704].bitcast(F16).rearrange("p (b c) -> p b c", b=11)
        att = s_buf[:, 0:512]
        p_parts = pt[:].bitcast(F16).rearrange("p (s g c q) -> p s g c q", s=2, g=2, c=4)
        a_mask = q_bd[:].rearrange("p (h t) -> p h t", h=GH)

        rope_ang, rope_turns = ot[:, 0:512], ot[:, 512:1024]
        rope_args = res[:, 0:512], res[:, 512:1024]
        rope_pos = y[:, 0:2 * NT].rearrange("p (e t) -> p e t", e=2)
        rope_freq = y[:, 2 * NT:2 * NT + HEAD // 2]

        def halves(ap, n):
            return ap.rearrange("p (n e d) -> p n e d", n=n, e=2)

        params = sem("params_loaded")
        preg_loaded = sem("preg_loaded")
        postg_loaded = sem("postg_loaded")
        gmw_loaded = sem("gm_weights_loaded")
        raw_loaded = [sem(f"raw{i}_loaded") for i in range(3)]
        x_loaded = sem("x_loaded")
        rope_loaded = sem("rope_loaded")
        rope_stored = sem("rope_stored")
        res_loaded = sem("res_loaded")
        out_stored = sem("out_stored")
        const_ready = sem("const_ready")
        pos_loaded = sem("pos_loaded")
        table_v = sem("rope_table_vector_steps")
        one_ready = sem("one_ready")
        table_a = sem("rope_table_sines")
        layer_state = sem("layer_state_cleared")
        gmw_t = sem("gm_weights_transposed")
        gmw_ready = sem("gm_weights_ready")
        preg_ready = sem("preg_ready")

        NB = N_WIN + N_WOUT
        a_m = Stage(sem("a_m"), "sum")
        v_s = Stage(sem("v_s"), "guard bits recip unscale mult")
        v_w = Stage(sem("v_w"), "hi lo0 lo1 lo2 lo3")
        a_w = Stage(sem("a_w"), "hi0 hi1 hi2")
        p_w = Stage(sem("p_w"), "gain all")

        t_x = Stage(sem("t_x"), "x0 x1")
        a_x = Stage(sem("a_x"), "scale hi0 hi1")
        v_x = Stage(sem("v_x"), "stats aggr msq eps lo0 lo1")
        p_x = Stage(sem("p_x"), "pow")

        t_a = Stage(sem("t_a"), "c0 c1 c2 c3 c4 c5")
        a_a = Stage(sem("a_a"), "c0 c1 c2 c3 c4 c5")

        t_b = Stage(sem("t_b"), "gm gla logit ropeq ropek sc0 at kd sc1 o u pt0a pt0b pv0 pt1a pt1b pv1")
        a_b = Stage(sem("a_b"), "qk low gv vv silu_a silu_b silu_c abs exp ln qT kT kref qref decay kdec kdn"
                                " exp0 sq exp1 sink hi0a hi0b hi1a hi1b yscale")
        v_l = Stage(sem("v_l"), "stats aggr eps norm gain bias")
        p_l = Stage(sem("p_l"), "pow")
        v_b = Stage(sem("v_b"), "xc xs rq1 rq2 rk1 rk2 qhi khi qlo klo vlo gate_u gate_g"
                                " min la cum refs refn sv ya kref qref qbd dlast qdec kdec am"
                                " mask0 max0 neg0 negm0 mask1 max1 neg1 negm1 kcopy sinkd lo0a lo0b um state ored oeps o1 yb"
                                " lo1a lo1b den sden recip att vcopy yc ymax yguard ybits yrecip yscale yun")
        p_b = Stage(sem("p_b"), "o_pow")
        v_k = Stage(sem("v_k"), "pow qk a u v")

        t_c = Stage(sem("t_c"), "y0 y1 out0 out1")
        a_c = Stage(sem("a_c"), "hi0 hi1 ev0 ev1")
        v_c = Stage(sem("v_c"), "lo0 lo1 fac stats aggr msq eps post add")
        p_c = Stage(sem("p_c"), "pow")

        N_PARAMS = 7

        def layer_of(n, layer):
            return n // NT if isinstance(n, int) else layer

        def run_pipeline(engine, iteration):
            for layer in range(DEPTH):
                base, last = layer * NT, layer == DEPTH - 1
                first = 3
                assert (NT - 1 - first) % 2 == 0
                for i in range(first):
                    n = base + i
                    iteration(n, layer, a=True, b=n >= 1, c=n >= 2, x=True)
                with engine.Fori(0, (NT - 1 - first) // 2) as pair:
                    for step in range(2):
                        iteration(pair * 2 + (base + first + step), layer, a=True, b=True, c=True, x=True)
                iteration(base + NT - 1, layer, a=True, b=True, c=True, x=not last)
            end = DEPTH * NT
            iteration(end, DEPTH - 1, a=False, b=True, c=True, x=False)
            iteration(end + 1, DEPTH - 1, a=False, b=False, c=True, x=False)

        N_FIRST = 4
        SPLITS = {(0, 0): {0: [4, 5], 1: [6], 2: [7], 3: [8, 9], 4: [10, 11], 5: [12], 6: [13]},
                  (0, 1): {5: [14], 6: [15]}}
        for l in range(1, DEPTH):
            SPLITS.update({(l - 1, NT - 1): {1: [0], 2: [1], 3: [2, 3], 4: [4], 5: [5]},
                           (l, 0): {0: [6], 1: [7], 2: [8], 3: [9], 4: [10, 11]},
                           (l, 1): {3: [12], 4: [13], 5: [14], 6: [15]}})

        def blocks_at(n, hook):
            if not isinstance(n, int):
                return []
            layer, i = divmod(n, NT)
            return [(layer + (i == NT - 1), b) for b in SPLITS.get((layer, i), {}).get(hook, [])]

        staging = [raw[:, 0], raw[:, 1], s_buf[:].rearrange("p (k c) -> p k c", k=KC)]
        THREE = N_WIN
        assert THREE % 6 == 0

        def buffer_of(n):
            return n % 3 if n < THREE else n % 2

        def buffer_before(n):
            return n - 3 if n < THREE + 2 else n - 2

        def wait_raw(engine, n):
            count = n // 3 + 1 if n < THREE else THREE // 3 + (n - THREE) // 2 + 1
            engine.wait_ge(raw_loaded[buffer_of(n)], 2 * 16 * count)

        def loads_after(layer, b):
            n = layer * NB + b
            return [m - layer * NB for m in range(n + 2, n + 4)
                    if m < (layer + 1) * NB and buffer_before(m) == n]

        def sums_after(layer, b):
            if layer == 0:
                return [b + 2] if b < THREE else [] if b == THREE or b == NB - 1 else [b + 1]
            return [b + 1] if b + 1 < NB and not starts_run(layer, b + 1) else []

        def starts_run(layer, b):
            return b == 0 or (b == N_WIN and layer > 0)

        def before_aggregate(dve):
            dve.memset(unused[:], 0.0)

        block = ctx.enter_context(nc.Block())

        @block.sync
        def _(sp):
            def rows(t):
                return bass.ts(t, P)

            x_rows = x

            def load_positions():
                sp.dma_start(rope_pos[:, 0, :].bitcast(I32), positions.rearrange("b (t p) -> p (b t)", p=P),
                             allow_slow_non_contiguous=True).then_inc(pos_loaded, 16)
                sp.dma_start(rope_freq, inv_freq.broadcast_to([P, HEAD // 2])).then_inc(pos_loaded, 16)

            def store_rope_tables():
                sp.wait_ge(table_a, 2)
                sp.dma_start(rope_dram.rearrange("t p c -> p t c"),
                             pt[:].rearrange("p (t c) -> p t c", t=NT)).then_inc(rope_stored, 16)

            def load_block(layer, b):
                n = layer * NB + b
                w, src = ((WG, w_in[layer][:, b * WG:(b + 1) * WG]) if b < N_WIN else
                          (OG, w_out[layer][:, (b - N_WIN) * OG:(b - N_WIN + 1) * OG]))
                for half in range(2):
                    if began(buffer_before(n)):
                        sp.wait_ge(v_w.sem, v_w.after(buffer_before(n), f"lo{2 * half + 1}"))
                        sp.wait_ge(a_w.sem, a_w.after(buffer_before(n), f"hi{1 + half}"))
                    sp.dma_start(staging[buffer_of(n)][:, 4 * half:4 * half + 4, 0:w],
                                 src[512 * half:512 * half + 512].rearrange("(k p) c -> p k c", p=P)
                                 ).then_inc(raw_loaded[buffer_of(n)], 16)

            def load_x(n, layer):
                if began(n - 1):
                    sp.wait_ge(t_x.sem, t_x.after(n - 1, "x1"))
                layer = layer_of(n, layer)
                t = n - layer * NT
                if layer:
                    sp.wait_ge(out_stored, 16 * (t + 1))
                sp.dma_start(xt[:], (out if layer else x_rows)[rows(t), :]).then_inc(x_loaded, 16)

            def load_preg(layer):
                if layer:
                    sp.wait_ge(v_s.sem, v_s.after(layer * NB - 1, "mult"))
                    sp.wait_ge(p_w.sem, p_w.after(layer * NB - 1, "gain"))
                sp.dma_start(preg[:], pre_g[layer].rearrange("(k p) -> p k", p=P),
                             allow_slow_non_contiguous=True).then_inc(preg_loaded, 16)

            def load_params(layer):
                if layer:
                    sp.wait_ge(v_b.sem, v_b.after(layer * NT - 1, "sinkd"))
                    sp.wait_ge(a_b.sem, a_b.after(layer * NT - 1, "abs"))
                    sp.wait_ge(t_b.sem, t_b.after(layer * NT - 1, "logit"))
                sp.dma_start(ln_g[:], gm_ln_g[layer:layer + 1].broadcast_to([P, GM])).then_inc(params, 16)
                sp.dma_start(ln_b[:], gm_ln_b[layer:layer + 1].broadcast_to([P, GM])).then_inc(params, 16)
                sp.dma_start(gm_bias[:], gm_bs[layer].rearrange("h t -> t h"),
                             allow_slow_non_contiguous=True).then_inc(params, 16)
                sp.dma_start(wg2[:], gla_wg2[layer]).then_inc(params, 16)
                sp.dma_start(gate_b[:], gla_bg[layer].rearrange("(c o) -> c o", o=1),
                             allow_slow_non_contiguous=True).then_inc(params, 16)
                sp.dma_start(norm_g[:], gla_norm_g[layer:layer + 1].broadcast_to([P, HEAD])).then_inc(params, 16)
                sp.dma_start(sinks[:], swa_sinks[layer:layer + 1].broadcast_to([P, 8])).then_inc(params, 16)

            def load_gm_weights(layer):
                if layer:
                    sp.wait_ge(v_b.sem, v_b.after(layer * NT - 1, "state"))
                sp.dma_start(q_bd[:].rearrange("p (h c) -> p h c", h=GH),
                             gm_ws[layer].rearrange("h t c -> t h c")).then_inc(gmw_loaded, 16)

            def load_postg(layer):
                if layer:
                    sp.wait_ge(v_c.sem, v_c.after(layer * NT - 1, "post"))
                sp.dma_start(postg[:], post_g[layer:layer + 1].broadcast_to([P, D_MODEL])).then_inc(postg_loaded, 16)

            def iteration(n, layer, a, b, c, x):
                i = n % NT if isinstance(n, int) else None
                if x:
                    load_x(n + 1, layer)
                if b:
                    j = n - 1
                    t = j - layer_of(j, layer) * NT
                    if began(j - 1):
                        sp.wait_ge(v_b.sem, v_b.after(j - 1, "xs"))
                    if isinstance(j, int) and j == 0:
                        sp.wait_ge(rope_stored, 16)
                    sp.dma_start(rope[:], rope_dram[t] if isinstance(t, int) else
                                 rope_dram[bass.ds(t, 1)].rearrange("o p c -> (o p) c")).then_inc(rope_loaded, 16)
                if c:
                    k = n - 2
                    lk = layer_of(k, layer)
                    k_rows = rows(k - lk * NT)
                    if began(k - 1):
                        sp.wait_ge(v_c.sem, v_c.after(k - 1, "add"))
                    sp.dma_start(res[:], (out if lk else x_rows)[k_rows, :]).then_inc(res_loaded, 16)
                new_layer = i == NT - 1 and layer + 1 < DEPTH
                if new_layer:
                    load_preg(layer + 1)
                    load_block(layer + 1, 0)
                    load_block(layer + 1, 1)

                def blocks(*hooks):
                    for hook in hooks:
                        for l, blk in blocks_at(n, hook):
                            for nxt in loads_after(l, blk):
                                load_block(l, nxt)

                blocks(0)
                if isinstance(n, int) and n == 0:
                    store_rope_tables()
                blocks(1, 2)
                if c:
                    sp.wait_ge(v_c.sem, v_c.after(k, "add"))
                    sp.dma_start(out[k_rows, :], ot[:]).then_inc(out_stored, 16)
                if i == 0 and layer and n < NT * DEPTH:
                    load_params(layer)
                if i == 1 and layer and n < NT * DEPTH:
                    load_postg(layer)
                blocks(3)
                if i == 0 and layer and n < NT * DEPTH:
                    load_gm_weights(layer)
                blocks(4, 5, 6)

            load_positions()
            load_x(0, 0)
            load_preg(0)
            load_block(0, 0)
            load_block(0, 1)
            for b in range(2, N_FIRST + 3):
                load_block(0, b)
            load_params(0)
            load_gm_weights(0)
            load_postg(0)
            run_pipeline(sp, iteration)
            sp.wait_ge(out_stored, 16 * NT * DEPTH)

        @block.tensor
        def _(pe):
            pe.wait_ge(const_ready, 1)

            def transpose_x(n):
                pe.wait_ge(a_x.sem, a_x.after(n, "scale"))
                for half in range(2):
                    for q in range(4):
                        k = 4 * half + q
                        mm = pe.transpose(TR[half][:, q * P:(q + 1) * P], xt[:, k * P:(k + 1) * P], ident[:])
                    mm.then_inc(t_x.sem, 1)

            def chunk(n, c):
                if c == 0:
                    pe.wait_ge(a_x.sem, a_x.after(n, "hi1"))
                    pe.wait_ge(v_x.sem, v_x.after(n, "lo1"))
                for k in range(KC):
                    for part, (h, w) in enumerate(((h_hi, w_hi), (h_hi, w_lo), (h_lo, w_hi))):
                        mm = pe.matmul(PJ[c % 2][:, 0:CH], h[:, k, :], w[:, k, c * CH:(c + 1) * CH],
                                       start=(k == 0 and part == 0), stop=(k == KC - 1 and part == 2))
                mm.then_inc(t_a.sem, 1)

            def out_half(n, half):
                for k in range(KC):
                    for part, (h, w) in enumerate(((y_hi, wo_hi), (y_hi, wo_lo), (y_lo, wo_hi))):
                        mm = pe.matmul(PJ[half][:, :], h[:, k, :], w[:, k, half * 512:(half + 1) * 512],
                                       start=(k == 0 and part == 0), stop=(k == KC - 1 and part == 2))
                mm.then_inc(t_c.sem, 1)

            def scores(half):
                for r in range(2 * half, 2 * half + 2):
                    for g in range(2):
                        rows = slice(g * HEAD, (g + 1) * HEAD)
                        out_cols = SC[g][:, (r % 2) * 2 * P:(r % 2 + 1) * 2 * P]
                        pe.matmul(out_cols, qT[:, 2 * r + g, :], kT[:, g, :, :], start=True, stop=False)
                        mm = pe.matmul(out_cols, qT[rows, 2 * r + g, :], kT[rows, 2, :, :], start=False, stop=True)
                mm.then_inc(t_b.sem, 1)

            def prob_transposes(half):
                for g in range(2):
                    for c in range(4):
                        r, blk = 2 * half + c // 2, c % 2
                        mm = pe.transpose(TR[g][:, c * P:(c + 1) * P], s4[:, g, r, blk * P:(blk + 1) * P], ident[:])
                    mm.then_inc(t_b.sem, 1)

            def attend(half):
                for g in range(2):
                    for r2 in range(2):
                        head = 4 * g + 2 * half + r2
                        for blk in range(2):
                            for p_part, v_part in ((0, 0), (0, 1), (1, 0)):
                                mm = pe.matmul(GL[:, head * HEAD:(head + 1) * HEAD],
                                               p_parts[:, p_part, g, 2 * r2 + blk, :],
                                               vv[:, v_part, blk, g * HEAD:(g + 1) * HEAD],
                                               start=(blk == 0 and p_part == v_part == 0),
                                               stop=(blk == 1 and p_part == 1))
                mm.then_inc(t_b.sem, 1)

            transpose_x(0)

            def iteration(n, layer, a, b, c, x):
                j, k = n - 1, n - 2
                i = n % NT if isinstance(n, int) else None

                def wait_block(blk):
                    if i == 0:
                        pe.wait_ge(a_w.sem, a_w.after(layer * NB + blk, "hi2"))
                        pe.wait_ge(v_w.sem, v_w.after(layer * NB + blk, "lo3"))

                def wait_out_block(blk):
                    if isinstance(k, int) and k % NT == 0:
                        pe.wait_ge(a_w.sem, a_w.after(k // NT * NB + blk, "hi2"))
                        pe.wait_ge(v_w.sem, v_w.after(k // NT * NB + blk, "lo3"))

                if b:
                    pe.wait_ge(v_l.sem, v_l.after(j, "bias"))
                    if began(j - 1):
                        pe.wait_ge(v_b.sem, v_b.after(j - 1, "um"))
                        pe.wait_ge(v_b.sem, v_b.after(j - 1, "o1"))
                    pe.wait_ge(gmw_ready, layer_of(j, layer) + 1)
                    pe.wait_ge(params, 16 * N_PARAMS * (layer_of(j, layer) + 1))
                    for h in range(GH):
                        mm = pe.matmul(MX[:, h * HEAD:(h + 1) * HEAD], gm_wT[:, h, :],
                                       pj[:, C_V + h * HEAD:C_V + (h + 1) * HEAD], start=True, stop=True)
                    mm.then_inc(t_b.sem, 1)
                    pe.wait_ge(a_a.sem, a_a.after(j, "c5"))
                    pe.wait_ge(v_x.sem, v_x.after(j + 1 if a else j, "lo0"))
                    pe.wait_ge(a_x.sem, a_x.after(j + 1 if a else j, "hi0"))
                    pe.transpose(TR[0][:, 0:P], pj[:, C_GQ:C_GQ + P], ident[:])
                    pe.transpose(TR[0][:, P:2 * P], pj[:, C_GK:C_GK + P], ident[:])
                    pe.transpose(TR[0][0:RANK, 2 * P:3 * P], pj[:, C_GL:C_GL + RANK], ident[:]).then_inc(t_b.sem, 1)
                if a:
                    if began(n - 1):
                        pe.wait_ge(a_a.sem, a_a.after(n - 1, "c4"))
                    wait_block(0)
                    wait_block(1)
                    chunk(n, 0)
                if c:
                    pe.wait_ge(a_b.sem, a_b.after(k, "yscale"))
                    if a:
                        pe.wait_ge(v_x.sem, v_x.after(n, "lo1"))
                        pe.wait_ge(a_x.sem, a_x.after(n, "hi1"))
                    pe.wait_ge(v_b.sem, v_b.after(k, "lo1b"))
                    pe.wait_ge(a_b.sem, a_b.after(k, "hi1b"))
                    for q in range(4):
                        mm = pe.transpose(TR[1][:, q * P:(q + 1) * P], y[:, q * P:(q + 1) * P], ident[:])
                    mm.then_inc(t_c.sem, 1)
                    if b:
                        pe.wait_ge(a_b.sem, a_b.after(j, "low"))
                    for q in range(4):
                        mm = pe.transpose(TR[0][:, q * P:(q + 1) * P], y[:, (q + 4) * P:(q + 5) * P], ident[:])
                    mm.then_inc(t_c.sem, 1)
                if b:
                    pe.wait_ge(a_b.sem, a_b.after(j, "low"))
                    if began(j - 1):
                        pe.wait_ge(v_b.sem, v_b.after(j - 1, "att"))
                    pe.matmul(GL[:, 0:P], wg2[:, :], g_low[:, :], start=True, stop=True).then_inc(t_b.sem, 1)
                if a:
                    if began(n - 1):
                        pe.wait_ge(a_a.sem, a_a.after(n - 1, "c5"))
                    wait_block(2)
                    wait_block(3)
                    chunk(n, 1)
                if b:
                    pe.wait_ge(v_b.sem, v_b.after(j, "klo"))
                    if c:
                        pe.wait_ge(a_c.sem, a_c.after(k, "hi0"))
                        pe.wait_ge(v_c.sem, v_c.after(k, "lo0"))
                    for h in range(8):
                        mm = pe.transpose(TR[1][:].bitcast(F16)[:, h * P:(h + 1) * P], qk_parts[:, h, :], ident16[:])
                    mm.then_inc(t_b.sem, 1)
                    if c:
                        pe.wait_ge(a_c.sem, a_c.after(k, "hi1"))
                        pe.wait_ge(v_c.sem, v_c.after(k, "lo1"))
                    for h in range(3):
                        mm = pe.transpose(TR[0][:].bitcast(F16)[:, h * P:(h + 1) * P], qk_parts[:, 8 + h, :], ident16[:])
                    mm.then_inc(t_b.sem, 1)
                if c:
                    pe.wait_ge(a_c.sem, a_c.after(k, "hi1"))
                    pe.wait_ge(v_c.sem, v_c.after(k, "lo1"))
                    if began(k - 1):
                        pe.wait_ge(a_c.sem, a_c.after(k - 1, "ev0"))
                    if a:
                        pe.wait_ge(a_a.sem, a_a.after(n, "c0"))
                    wait_out_block(N_WIN + 1)
                    out_half(k, 0)
                if b:
                    pe.wait_ge(a_b.sem, a_b.after(j, "kT"))
                    if began(j - 1):
                        pe.wait_ge(v_b.sem, v_b.after(j - 1, "mask1"))
                    pe.wait_ge(layer_state, layer_of(j, layer) + 1)
                    if began(j - 1):
                        pe.wait_ge(v_b.sem, v_b.after(j - 1, "kcopy"))
                    scores(0)
                if c:
                    if began(k - 1):
                        pe.wait_ge(a_c.sem, a_c.after(k - 1, "ev1"))
                    if a:
                        pe.wait_ge(a_a.sem, a_a.after(n, "c1"))
                    wait_out_block(N_WIN + 3)
                    out_half(k, 1)
                if b:
                    pe.wait_ge(v_b.sem, v_b.after(j, "kdec"))
                    for sub in range(NSUB):
                        cols = slice(sub * P, (sub + 1) * P)
                        mm = pe.matmul(GL[:, cols], k_ref[:, sub, :], q_bd[:, cols],
                                       start=True, stop=True)
                    mm.then_inc(t_b.sem, 1)
                    pe.wait_ge(a_b.sem, a_b.after(j, "kT"))
                    pe.transpose(TR[0][:, 0:P], k_dec[:], ident[:]).then_inc(t_b.sem, 1)
                if a:
                    pe.wait_ge(a_a.sem, a_a.after(n, "c0"))
                    if c:
                        pe.wait_ge(a_c.sem, a_c.after(k, "ev0"))
                    wait_block(4)
                    wait_block(5)
                    chunk(n, 2)
                if b:
                    pe.wait_ge(v_b.sem, v_b.after(j, "mask0"))
                    scores(1)
                    pe.wait_ge(v_b.sem, v_b.after(j, "am"))
                    pe.wait_ge(v_b.sem, v_b.after(j, "sv"))
                    if began(j - 1):
                        pe.wait_ge(v_b.sem, v_b.after(j - 1, "state"))
                    pe.wait_ge(a_b.sem, a_b.after(j, "gv"))
                    pe.matmul(MX[:, 0:GLA], q_dec[:], state[:], start=True, stop=False, skip_group_check=True)
                    for h in range(GH):
                        mm = pe.matmul(MX[:, h * HEAD:(h + 1) * HEAD], a_mask[:, h, :],
                                       g_v[:, h * HEAD:(h + 1) * HEAD], start=False, stop=(h == GH - 1),
                                       skip_group_check=True)
                    mm.then_inc(t_b.sem, 1)
                    pe.wait_ge(a_b.sem, a_b.after(j, "kdn"))
                    pe.matmul(MX[:, GLA:2 * GLA], k_decN[:], g_v[:], start=True, stop=True,
                              skip_group_check=True).then_inc(t_b.sem, 1)
                    pe.wait_ge(a_b.sem, a_b.after(j, "exp0"))
                    pe.wait_ge(a_b.sem, a_b.after(j, "kdn"))
                    pe.wait_ge(a_b.sem, a_b.after(j, "qT"))
                    prob_transposes(0)
                if a:
                    pe.wait_ge(a_a.sem, a_a.after(n, "c1"))
                    if c:
                        pe.wait_ge(a_c.sem, a_c.after(k, "ev1"))
                    wait_block(6)
                    wait_block(7)
                    chunk(n, 3)
                if a:
                    pe.wait_ge(a_a.sem, a_a.after(n, "c2"))
                    wait_block(8)
                    wait_block(9)
                    chunk(n, 4)
                if b:
                    pe.wait_ge(a_b.sem, a_b.after(j, "hi0b"))
                    pe.wait_ge(v_b.sem, v_b.after(j, "lo0b"))
                    pe.wait_ge(v_b.sem, v_b.after(j, "vlo"))
                    pe.wait_ge(v_b.sem, v_b.after(j, "am"))
                    if began(j - 1):
                        pe.wait_ge(v_b.sem, v_b.after(j - 1, "vcopy"))
                    attend(0)
                    pe.wait_ge(a_b.sem, a_b.after(j, "exp1"))
                    prob_transposes(1)
                if i == 0 and a:
                    pe.wait_ge(gmw_loaded, 16 * (layer + 1))
                    if b:
                        pe.wait_ge(v_b.sem, v_b.after(j, "um"))
                        pe.wait_ge(v_b.sem, v_b.after(j, "o1"))
                    for h in range(GH):
                        mm = pe.transpose(MX[:, h * P:(h + 1) * P], q_bd[:, h * P:(h + 1) * P], ident[:])
                    mm.then_inc(gmw_t, 1)
                if a:
                    pe.wait_ge(a_a.sem, a_a.after(n, "c3"))
                    wait_block(10)
                    wait_block(11)
                    chunk(n, 5)
                if x:
                    if b:
                        pe.wait_ge(a_b.sem, a_b.after(j, "hi1b"))
                        pe.wait_ge(v_b.sem, v_b.after(j, "lo1b"))
                    transpose_x(n + 1)
                if b:
                    pe.wait_ge(a_b.sem, a_b.after(j, "hi1b"))
                    pe.wait_ge(v_b.sem, v_b.after(j, "lo1b"))
                    attend(1)

            run_pipeline(pe, iteration)

        @block.scalar
        def _(act):
            copy = ACT.Copy
            def rope_sines():
                for half in range(2):
                    act.wait_ge(table_v, 14)
                    act.activation(pt[:].rearrange("p (t e d) -> p t e d", t=NT, e=2)[:, :, half, :],
                                   rope_args[half].rearrange("p (t d) -> p t d", t=NT), ACT.Sin).then_inc(table_a, 1)

            def x_scale(n):
                act.wait_ge(p_x.sem, p_x.after(n, "pow"))
                act.activation(xt[:], xt[:], copy, scale=x_r[:, 0:1]).then_inc(a_x.sem, 1)

            def x_hi(n):
                if began(n - 1):
                    act.wait_ge(t_a.sem, t_a.after(n - 1, "c5"))
                for half in range(2):
                    act.wait_ge(t_x.sem, t_x.after(n, f"x{half}"))
                    act.activation(h_hi[:, 4 * half:4 * half + 4, :], TR[half][:].rearrange("p (k t) -> p k t", k=4),
                                   copy).then_inc(a_x.sem, 1)

            def block_sum(layer, b):
                n = layer * NB + b
                wait_raw(act, n)
                if began(n - 2):
                    act.wait_ge(p_w.sem, p_w.after(n - 2, "all"))
                if b < N_WIN:
                    if layer:
                        act.wait_ge(t_a.sem, t_a.after(layer * NT - 1, f"c{b // 2}"))
                    w, room = WG, w_lo[:, :, b * WG:(b + 1) * WG]
                else:
                    if layer:
                        act.wait_ge(t_c.sem, t_c.after(layer * NT - 1, "out1"))
                    w, room = OG, wo_lo[:, :, (b - N_WIN) * OG:(b - N_WIN + 1) * OG]
                act.activation(room.bitcast(BF16), staging[buffer_of(n)][:, :, 0:w], ACT.Abs,
                               accum_out=part_sum[:, n % 2:n % 2 + 1]).then_inc(a_m.sem, 1)

            def split_hi(layer, b):
                n = layer * NB + b
                act.wait_ge(v_s.sem, v_s.after(n, "mult"))
                if b < N_WIN:
                    if layer:
                        act.wait_ge(t_a.sem, t_a.after(layer * NT - 1, f"c{b // 2}"))
                else:
                    if layer:
                        act.wait_ge(t_c.sem, t_c.after(layer * NT - 1, "out1"))
                w, dst = (WG, w_hi[:, :, b * WG:(b + 1) * WG]) if b < N_WIN else \
                         (OG, wo_hi[:, :, (b - N_WIN) * OG:(b - N_WIN + 1) * OG])
                for k in range(HI_ACT):
                    ins = act.activation(dst[:, k, :], staging[buffer_of(n)][:, k, 0:w], copy, scale=wscale[:, n % 2, k:k + 1])
                    if k % 2:
                        ins.then_inc(a_w.sem, 1)

            block_sum(0, 0)
            x_scale(0)
            x_hi(0)
            block_sum(0, 1)
            for blk in range(N_FIRST):
                split_hi(0, blk)
                block_sum(0, blk + 2)
            rope_sines()

            def iteration(n, layer, a, b, c, x):
                j, k = n - 1, n - 2

                def splits(hook):
                    for l, blk in blocks_at(n, hook):
                        if starts_run(l, blk):
                            block_sum(l, blk)
                        split_hi(l, blk)
                        for nxt in sums_after(l, blk):
                            block_sum(l, nxt)

                def evac(chunk):
                    act.wait_ge(t_a.sem, t_a.after(n, f"c{chunk}"))
                    for g in range(2 * chunk, 2 * chunk + 2):
                        ins = act.activation(pj[:, g * WG:(g + 1) * WG], PJ[chunk % 2][:, (g % 2) * WG:(g % 2 + 1) * WG],
                                             copy, scale=unscale_in[:, g:g + 1])
                    ins.then_inc(a_a.sem, 1)

                def p_hi(g):
                    act.activation(p_parts[:, 0, g], TR[g][:].rearrange("p (c q) -> p c q", c=4), copy,
                                   scale=P_SCALE).then_inc(a_b.sem, 1)

                def probs(half):
                    act.wait_ge(v_b.sem, v_b.after(j, f"negm{half}"))
                    for g in range(2):
                        for r in range(2 * half, 2 * half + 2):
                            head = 4 * g + r
                            ins = act.activation(s4[:, g, r, :], s4[:, g, r, :], ACT.Exp,
                                                 bias=neg_max[:, head:head + 1],
                                                 accum_out=row_sum[:, head:head + 1])
                    ins.then_inc(a_b.sem, 1)

                if b:
                    act.wait_ge(t_b.sem, t_b.after(j, "gla"))
                    if began(j - 1):
                        act.wait_ge(v_b.sem, v_b.after(j - 1, "kdec"))
                    act.activation(g_qk[:], TR[0][:, 0:2 * P].rearrange("p (e t) -> p e t", e=2), copy).then_inc(a_b.sem, 1)
                    if began(j - 1):
                        act.wait_ge(t_b.sem, t_b.after(j - 1, "logit"))
                    act.activation(g_low[:], TR[0][0:RANK, 2 * P:3 * P], copy).then_inc(a_b.sem, 1)
                    if began(j - 1):
                        act.wait_ge(t_b.sem, t_b.after(j - 1, "u"))
                    act.activation(g_v[:], pj[:, C_GV:C_GV + GLA], copy).then_inc(a_b.sem, 1)
                    if began(j - 1):
                        act.wait_ge(t_b.sem, t_b.after(j - 1, "pv1"))
                        act.wait_ge(v_b.sem, v_b.after(j - 1, "vcopy"))
                    act.wait_ge(v_k.sem, v_k.after(layer_of(j, layer), "v"))
                    act.activation(vv[:, 0, 1, :], pj[:, C_SV:C_SV + P], copy, scale=v_scale[:, 0:1]).then_inc(a_b.sem, 1)
                if c:
                    act.wait_ge(t_b.sem, t_b.after(k, "pv1"))
                    for half in range(2):
                        act.wait_ge(t_c.sem, t_c.after(k, f"y{half}"))
                        act.activation(y_hi[:, 4 * half:4 * half + 4, :],
                                       TR[1 - half][:].rearrange("p (k t) -> p k t", k=4), copy).then_inc(a_c.sem, 1)
                if b:
                    if began(j - 1):
                        act.wait_ge(t_c.sem, t_c.after(j - 1, "y1"))
                    if not c:
                        if began(j - 1):
                            act.wait_ge(a_b.sem, a_b.after(j - 1, "yscale"))
                    act.activation(y[:, 0:GM], pj[:, C_Z:C_Z + GM], ACT.Silu).then_inc(a_b.sem, 1)
                    act.activation(y[:, GM:GM + GLA], pj[:, C_GZ:C_GZ + GLA], ACT.Silu).then_inc(a_b.sem, 1)
                    act.activation(y[:, GM + GLA:], pj[:, C_SZ:C_SZ + SWA], ACT.Silu).then_inc(a_b.sem, 1)
                if a:
                    if b:
                        act.wait_ge(v_b.sem, v_b.after(j, "gate_u"))
                        act.wait_ge(t_b.sem, t_b.after(j, "gm"))
                    evac(0)
                if b:
                    act.wait_ge(t_b.sem, t_b.after(j, "logit"))
                    if began(j - 1):
                        act.wait_ge(v_b.sem, v_b.after(j - 1, "la"))
                    act.wait_ge(params, 16 * N_PARAMS * (layer_of(j, layer) + 1))
                    act.activation(gate_a[:], GL[:, 0:P], ACT.Abs, bias=gate_b[:, 0:1]).then_inc(a_b.sem, 1)
                    act.wait_ge(a_b.sem, a_b.after(j, "abs"))
                    act.activation(gate_a[:], gate_a[:], ACT.Exp, scale=-1.0).then_inc(a_b.sem, 1)
                    act.wait_ge(a_b.sem, a_b.after(j, "exp"))
                    act.activation(gate_a[:], gate_a[:], ACT.Ln, bias=one[:, 0:1]).then_inc(a_b.sem, 1)
                splits(0)
                if a:
                    evac(1)
                if b:
                    act.wait_ge(t_b.sem, t_b.after(j, "ropeq"))
                    if began(j - 1):
                        act.wait_ge(t_b.sem, t_b.after(j - 1, "sc1"))
                    act.activation(qT[:], TR[1][:].bitcast(F16).rearrange("p (h t) -> p h t", h=8), copy).then_inc(a_b.sem, 1)
                    act.wait_ge(t_b.sem, t_b.after(j, "ropek"))
                    if began(j - 1):
                        act.wait_ge(v_b.sem, v_b.after(j - 1, "kcopy"))
                    act.activation(kT[:, :, 1, :], TR[0][:].bitcast(F16)[:, 0:3 * P].rearrange("p (h t) -> p h t", h=3),
                                   copy).then_inc(a_b.sem, 1)
                splits(1)
                if b:
                    act.wait_ge(v_b.sem, v_b.after(j, "refn"))
                    if began(j - 1):
                        act.wait_ge(t_b.sem, t_b.after(j - 1, "at"))
                    for i in range(NSUB):
                        m = (i + 1) * SUB
                        ins = act.activation(k_ref[:, i, 0:m], cum[:, 0:m], ACT.Exp, scale=-1.0 / GATE_TAU,
                                             bias=ref_p[:, i:i + 1])
                    ins.then_inc(a_b.sem, 1)
                    if began(j - 1):
                        act.wait_ge(v_b.sem, v_b.after(j - 1, "qbd"))
                    for i in range(NSUB):
                        cols = slice(i * SUB, (i + 1) * SUB)
                        ins = act.activation(q_ref[:, cols], cum[:, cols], ACT.Exp, scale=1.0 / GATE_TAU,
                                             bias=ref_n[:, i:i + 1])
                    ins.then_inc(a_b.sem, 1)
                    if began(j - 1):
                        act.wait_ge(v_b.sem, v_b.after(j - 1, "state"))
                    act.activation(decay[:], cum[:], ACT.Exp, scale=1.0 / GATE_TAU).then_inc(a_b.sem, 1)
                    if began(j - 1):
                        act.wait_ge(t_b.sem, t_b.after(j - 1, "kd"))
                    act.activation(k_dec[:], cum[:], ACT.Exp, scale=-1.0 / GATE_TAU,
                                   bias=ref_p[:, NSUB:NSUB + 1]).then_inc(a_b.sem, 1)
                if c:
                    act.wait_ge(v_c.sem, v_c.after(k, "fac"))
                    if began(k - 1):
                        act.wait_ge(v_c.sem, v_c.after(k - 1, "add"))
                    if not (isinstance(k, int) and k == 0):
                        act.wait_ge(out_stored, k * 16)
                    for half in range(2):
                        act.wait_ge(t_c.sem, t_c.after(k, f"out{half}"))
                        for g in range(2 * half, 2 * half + 2):
                            ins = act.activation(ot[:, g * OG:(g + 1) * OG], PJ[half][:, (g % 2) * OG:(g % 2 + 1) * OG],
                                                 copy, scale=fac[:, g:g + 1])
                        ins.then_inc(a_c.sem, 1)
                if b:
                    act.wait_ge(t_b.sem, t_b.after(j, "kd"))
                    if began(j - 1):
                        act.wait_ge(t_b.sem, t_b.after(j - 1, "u"))
                    act.activation(k_decN[:], TR[0][:, 0:P], copy).then_inc(a_b.sem, 1)
                splits(2)
                if b:
                    probs(0)
                if a:
                    evac(2)
                if b:
                    act.wait_ge(t_b.sem, t_b.after(j, "u"))
                    act.wait_ge(v_b.sem, v_b.after(j, "ya"))
                    act.activation(mix[:], MX[:, 0:GLA], ACT.Square).then_inc(a_b.sem, 1)
                    probs(1)
                    act.wait_ge(v_b.sem, v_b.after(j, "sinkd"))
                    act.activation(sink_e[:], sink_e[:], ACT.Exp).then_inc(a_b.sem, 1)
                if b:
                    act.wait_ge(t_b.sem, t_b.after(j, "pt0a"))
                    if began(j - 1):
                        act.wait_ge(t_b.sem, t_b.after(j - 1, "pv1"))
                    if c:
                        act.wait_ge(t_c.sem, t_c.after(k, "out1"))
                    p_hi(0)
                    act.wait_ge(t_b.sem, t_b.after(j, "pt0b"))
                    p_hi(1)
                splits(3)
                if a:
                    if b:
                        act.wait_ge(v_b.sem, v_b.after(j, "xs"))
                    evac(3)
                splits(4)
                if a:
                    evac(4)
                if b:
                    act.wait_ge(t_b.sem, t_b.after(j, "pt1a"))
                    p_hi(0)
                    act.wait_ge(t_b.sem, t_b.after(j, "pt1b"))
                    p_hi(1)
                splits(5)
                if x:
                    x_scale(n + 1)
                if a:
                    evac(5)
                if x:
                    x_hi(n + 1)
                if b:
                    act.wait_ge(v_b.sem, v_b.after(j, "yscale"))
                    act.activation(y[:], y[:], copy, scale=y_scale[:, 0:1]).then_inc(a_b.sem, 1)
                splits(6)

            run_pipeline(act, iteration)

        @block.vector
        def _(dve):
            tsteps = [0]

            def table(ins):
                tsteps[0] += 1
                ins.then_inc(table_v, 1)
                dve.wait_ge(table_v, tsteps[0])

            def rope_angles():
                dve.wait_ge(pos_loaded, 32)
                table(dve.tensor_copy(rope_pos[:, 1, :], rope_pos[:, 0, :].bitcast(I32)))
                table(dve.tensor_tensor(rope_ang.rearrange("p (t d) -> p t d", t=NT),
                                        rope_pos[:, 1, :].unsqueeze(2).broadcast_to([P, NT, HEAD // 2]),
                                        rope_freq.unsqueeze(1).broadcast_to([P, NT, HEAD // 2]), ALU.mult))

            def rope_arguments(half):
                arg, turns, quarter = rope_args[half], rope_turns, (0.25, 0.0)[half]
                table(dve.tensor_scalar(turns, rope_ang, 1.0 / (2.0 * np.pi), quarter, ALU.mult, ALU.add))
                table(dve.tensor_scalar(turns, turns, ROUND, ROUND, ALU.add, ALU.subtract))
                table(dve.scalar_tensor_tensor(arg, turns, -TWO_PI_HI, rope_ang, ALU.mult, ALU.add))
                table(dve.scalar_tensor_tensor(arg, turns, -TWO_PI_LO, arg, ALU.mult, ALU.add))
                table(dve.tensor_scalar(arg, arg, quarter * 2.0 * np.pi, PI_SAFE, ALU.add, ALU.min))
                table(dve.tensor_scalar(arg, arg, -PI_SAFE, None, ALU.max))

            dve.memset(one[:], 1.0).then_inc(one_ready, 1)
            dve.wait_ge(one_ready, 1)
            dve.wait_ge(const_ready, 1)

            def x_stats_of(n):
                dve.wait_ge(x_loaded, 16 * (n + 1))
                for h in range(2):
                    ins = dve.bn_stats(x_stats[:, h, :], xt[:, h * 512:(h + 1) * 512])
                ins.then_inc(v_x.sem, 1)
                dve.wait_ge(v_x.sem, v_x.after(n, "stats"))
                before_aggregate(dve)
                dve.bn_aggr(x_mv[:], x_stats[:]).then_inc(v_x.sem, 1)
                dve.wait_ge(v_x.sem, v_x.after(n, "aggr"))
                dve.scalar_tensor_tensor(x_mv[:, 1:2], x_mv[:, 0:1], x_mv[:, 0:1], x_mv[:, 1:2],
                                         ALU.mult, ALU.add).then_inc(v_x.sem, 1)
                dve.wait_ge(v_x.sem, v_x.after(n, "msq"))
                if began(n - 1):
                    dve.wait_ge(a_x.sem, a_x.after(n - 1, "scale"))
                dve.tensor_scalar(x_mv[:, 0:1], x_mv[:, 1:2], EPS, H_SCALE ** -2, ALU.add, ALU.mult).then_inc(v_x.sem, 1)

            def x_lo(n):
                if began(n - 1):
                    dve.wait_ge(t_a.sem, t_a.after(n - 1, "c5"))
                for half in range(2):
                    dve.wait_ge(a_x.sem, a_x.after(n, f"hi{half}"))
                    dve.tensor_tensor(h_lo[:, 4 * half:4 * half + 4, :], TR[half][:].rearrange("p (k t) -> p k t", k=4),
                                      h_hi[:, 4 * half:4 * half + 4, :], ALU.subtract).then_inc(v_x.sem, 1)

            def split_scale(layer, b):
                n = layer * NB + b
                power, inverse = wpow[:, 0:1], wpow[:, 1:2]
                if began(n - 1):
                    dve.wait_ge(v_s.sem, v_s.after(n - 1, "mult"))
                dve.wait_ge(p_w.sem, p_w.after(n, "all"))
                dve.tensor_scalar(power, bound[:, n % 2:n % 2 + 1], TINY, None, ALU.max).then_inc(v_s.sem, 1)
                dve.wait_ge(v_s.sem, v_s.after(n, "guard"))
                dve.tensor_scalar(power.bitcast(U32), power.bitcast(U32), EXP_BITS, None, ALU.bitwise_and).then_inc(v_s.sem, 1)
                dve.wait_ge(v_s.sem, v_s.after(n, "bits"))
                dve.reciprocal(inverse, power).then_inc(v_s.sem, 1)
                if b < N_WIN:
                    if layer:
                        dve.wait_ge(a_a.sem, a_a.after(layer * NT - 1, f"c{b // 2}"))
                    dve.tensor_scalar(unscale_in[:, b:b + 1], power, 1.0 / (TOP * H_SCALE), None,
                                      ALU.mult).then_inc(v_s.sem, 1)
                else:
                    if layer:
                        dve.wait_ge(v_c.sem, v_c.after(layer * NT - 1, "fac"))
                    dve.tensor_scalar(unscale_out[:, b - N_WIN:b - N_WIN + 1], power, 1.0 / TOP, None,
                                      ALU.mult).then_inc(v_s.sem, 1)
                dve.wait_ge(v_s.sem, v_s.after(n, "recip"))
                if began(n - 2):
                    dve.wait_ge(v_w.sem, v_w.after(n - 2, "lo3"))
                    dve.wait_ge(a_w.sem, a_w.after(n - 2, "hi2"))
                gain = preg[:] if b < N_WIN else one[:, 0:1].broadcast_to([P, KC])
                dve.tensor_scalar(wscale[:, n % 2, :], gain, inverse, TOP, ALU.mult, ALU.mult).then_inc(v_s.sem, 1)

            def split_lo(layer, b):
                n = layer * NB + b
                w, hi, lo, at = (WG, w_hi, w_lo, b * WG) if b < N_WIN else (OG, wo_hi, wo_lo, (b - N_WIN) * OG)
                dve.wait_ge(v_s.sem, v_s.after(n, "mult"))
                if b < N_WIN:
                    if layer:
                        dve.wait_ge(t_a.sem, t_a.after(layer * NT - 1, f"c{b // 2}"))
                else:
                    if layer:
                        dve.wait_ge(t_c.sem, t_c.after(layer * NT - 1, "out1"))
                for k in range(HI_ACT, KC):
                    ins = dve.tensor_scalar(hi[:, k, at:at + w], staging[buffer_of(n)][:, k, 0:w],
                                            wscale[:, n % 2, k:k + 1], None, ALU.mult)
                ins.then_inc(v_w.sem, 1)
                for k in range(KC):
                    if k == HI_ACT:
                        dve.wait_ge(v_w.sem, v_w.after(n, "hi"))
                    elif k % 2 == 0 and k < HI_ACT:
                        dve.wait_ge(a_w.sem, a_w.after(n, f"hi{k // 2}"))
                    ins = dve.scalar_tensor_tensor(lo[:, k, at:at + w], staging[buffer_of(n)][:, k, 0:w], wscale[:, n % 2, k:k + 1],
                                                   hi[:, k, at:at + w], ALU.mult, ALU.subtract)
                    if k % 2:
                        ins.then_inc(v_w.sem, 1)

            def attention_scales(layer):
                blocks = slice(C_SQ // WG, (C_SV + P - 1) // WG + 1)
                v_block = C_SV // WG
                assert (C_SV + P - 1) // WG == v_block
                if layer:
                    dve.wait_ge(v_b.sem, v_b.after(layer * NT - 1, "vcopy"))
                dve.wait_ge(v_s.sem, v_s.after(layer * NB + N_WIN - 1, "mult"))
                dve.tensor_reduce(att_pow[:], unscale_in[:, blocks], AX.X, ALU.max).then_inc(v_k.sem, 1)
                to_16 = 16.0 / (TOP * H_SCALE)
                dve.wait_ge(v_k.sem, v_k.after(layer, "pow"))
                dve.reciprocal(qk_scale[:], att_pow[:]).then_inc(v_k.sem, 1)
                dve.tensor_scalar(score_unscale[:], att_pow[:], to_16 ** -1, None, ALU.mult).then_inc(v_k.sem, 1)
                dve.reciprocal(v_scale[:], unscale_in[:, v_block:v_block + 1])
                dve.wait_ge(v_k.sem, v_k.after(layer, "a"))
                dve.scalar_tensor_tensor(score_unscale[:], score_unscale[:], float(HEAD) ** -0.5, score_unscale[:],
                                         ALU.mult, ALU.mult).then_inc(v_k.sem, 1)
                dve.wait_ge(v_k.sem, v_k.after(layer, "u"))
                for scale in (qk_scale, v_scale):
                    ins = dve.tensor_scalar(scale[:], scale[:], to_16, None, ALU.mult)
                ins.then_inc(v_k.sem, 1)
                dve.wait_ge(v_k.sem, v_k.after(layer, "v"))

            def prepare_preg(layer):
                dve.wait_ge(preg_loaded, 16 * (layer + 1))
                if layer:
                    dve.wait_ge(p_w.sem, p_w.after(layer * NB - 1, "gain"))
                dve.tensor_reduce(preg_top[:], preg[:], AX.X, ALU.max, apply_absolute_value=True).then_inc(preg_ready, 1)

            rope_angles()
            rope_arguments(0)
            prepare_preg(0)
            x_stats_of(0)
            x_lo(0)
            split_scale(0, 0)
            for blk in range(N_FIRST):
                split_scale(0, blk + 1)
                split_lo(0, blk)
                if blk == 1:
                    rope_arguments(1)

            def iteration(n, layer, a, b, c, x):
                j, k = n - 1, n - 2
                i = n % NT if isinstance(n, int) else None

                def splits(hook):
                    for l, blk in blocks_at(n, hook):
                        if l and blk == 0:
                            prepare_preg(l)
                        if starts_run(l, blk):
                            split_scale(l, blk)
                        ahead = l == 0 and blk <= THREE
                        follows = blk + 1 < NB and not starts_run(l, blk + 1)
                        if follows and ahead:
                            split_scale(l, blk + 1)
                        split_lo(l, blk)
                        if follows and not ahead:
                            split_scale(l, blk + 1)

                def p_lo(g):
                    dve.scalar_tensor_tensor(p_parts[:, 1, g], TR[g][:].rearrange("p (c q) -> p c q", c=4), P_SCALE,
                                             p_parts[:, 0, g], ALU.mult, ALU.subtract).then_inc(v_b.sem, 1)

                def mask_max(half):
                    dve.wait_ge(t_b.sem, t_b.after(j, f"sc{half}"))
                    first = isinstance(j, int) and j % NT == 0
                    r2 = slice(2 * half, 2 * half + 2)
                    pieces = ((0, P, 0), (P, 2 * P, 2 * P)) if first else ((0, 2 * P, P),)
                    for g in range(2):
                        for lo, hi, at in pieces:
                            ins = dve.scalar_tensor_tensor(
                                s4[:, g, r2, lo:hi], SC[g][:].rearrange("p (r k) -> p r k", r=2)[:, :, lo:hi],
                                score_unscale[:, 0:1], band[:, at:at + hi - lo].unsqueeze(1).broadcast_to([P, 2, hi - lo]),
                                ALU.mult, ALU.add)
                    ins.then_inc(v_b.sem, 1)
                    dve.wait_ge(v_b.sem, v_b.after(j, f"mask{half}"))
                    heads = [t[:].rearrange("p (g r) -> p g r", g=2)[:, :, r2] for t in (row_max, neg_max, sinks)]
                    if began(j - 1):
                        dve.wait_ge(v_b.sem, v_b.after(j - 1, "sinkd"))
                    dve.tensor_reduce(heads[0], s4[:, :, r2, :], AX.X, ALU.max).then_inc(v_b.sem, 1)
                    dve.wait_ge(v_b.sem, v_b.after(j, f"max{half}"))
                    dve.tensor_tensor(heads[0], heads[0], heads[2], ALU.max).then_inc(v_b.sem, 1)
                    dve.wait_ge(v_b.sem, v_b.after(j, f"neg{half}"))
                    dve.tensor_scalar(heads[1], heads[0], -1.0, None, ALU.mult).then_inc(v_b.sem, 1)

                if i == 1 and n < NT * DEPTH:
                    attention_scales(layer)
                if b:
                    dve.wait_ge(a_a.sem, a_a.after(j, "c5"))
                    dve.wait_ge(rope_loaded, 16 * (j + 1))
                    if began(j - 1):
                        dve.wait_ge(t_b.sem, t_b.after(j - 1, "pt1b"))
                        dve.wait_ge(v_b.sem, v_b.after(j - 1, "yc"))
                    qk = pj[:, C_SQ:C_SQ + 640].rearrange("p (m d) -> p m d", d=HEAD // 2)
                    for half, dst in ((0, xc), (1, xs)):
                        dve.scalar_tensor_tensor(dst.rearrange("p (m d) -> p m d", d=HEAD // 2), qk, qk_scale[:, 0:1],
                                                 rope[:, 32 * half:32 * half + 32].unsqueeze(1).broadcast_to([P, 20, 32]),
                                                 ALU.mult, ALU.mult).then_inc(v_b.sem, 1)
                    dve.wait_ge(v_b.sem, v_b.after(j, "xs"))
                    qc = xc[:, 0:512].rearrange("p (g r e d) -> p g r e d", g=2, r=4, e=2)
                    qs = xs[:, 0:512].rearrange("p (g r e d) -> p g r e d", g=2, r=4, e=2)
                    qo = roped[:, 0:512].rearrange("p (r g e d) -> p g r e d", r=4, g=2, e=2)
                    kc, ks, ko = (halves(t[:, 512:640], 2) for t in (xc, xs, roped))
                    dve.tensor_tensor(qo[:, :, :, 0, :], qc[:, :, :, 0, :], qs[:, :, :, 1, :], ALU.subtract).then_inc(v_b.sem, 1)
                    dve.tensor_tensor(qo[:, :, :, 1, :], qc[:, :, :, 1, :], qs[:, :, :, 0, :], ALU.add).then_inc(v_b.sem, 1)
                    dve.tensor_tensor(ko[:, :, 0, :], kc[:, :, 0, :], ks[:, :, 1, :], ALU.subtract).then_inc(v_b.sem, 1)
                    dve.tensor_tensor(ko[:, :, 1, :], kc[:, :, 1, :], ks[:, :, 0, :], ALU.add).then_inc(v_b.sem, 1)
                    q_roped = roped[:, 0:512].rearrange("p (r g d) -> p r g d", r=4, g=2)
                    k_roped = roped[:, 512:640].rearrange("p (g d) -> p g d", g=2)
                    q_parts = qk_parts[:, 0:8, :].rearrange("p (r g) (s d) -> p r (g s) d", g=2, s=2)
                    k_high = qk_parts[:, 8:10, :].rearrange("p g (s d) -> p g s d", s=2)
                    k_low = qk_parts[:, 10, :].rearrange("p (g d) -> p g d", g=2)
                    dve.wait_ge(v_b.sem, v_b.after(j, "rk2"))
                    dve.tensor_copy(q_parts[:, :, 0::3, :], q_roped).then_inc(v_b.sem, 1)
                    dve.tensor_copy(k_high, k_roped.unsqueeze(2).broadcast_to([P, 2, 2, HEAD])).then_inc(v_b.sem, 1)
                    dve.wait_ge(v_b.sem, v_b.after(j, "khi"))
                    dve.tensor_tensor(q_parts[:, :, 1:3, :], q_roped, q_parts[:, :, 0::3, :],
                                      ALU.subtract).then_inc(v_b.sem, 1)
                    dve.tensor_tensor(k_low, k_roped, k_high[:, :, 0, :], ALU.subtract).then_inc(v_b.sem, 1)
                    dve.wait_ge(a_b.sem, a_b.after(j, "vv"))
                    dve.scalar_tensor_tensor(vv[:, 1, 1, :], pj[:, C_SV:C_SV + P], v_scale[:, 0:1], vv[:, 0, 1, :],
                                             ALU.mult, ALU.subtract).then_inc(v_b.sem, 1)
                if c:
                    for half in range(2):
                        dve.wait_ge(t_b.sem, t_b.after(k, "pv1"))
                        dve.wait_ge(a_c.sem, a_c.after(k, f"hi{half}"))
                        dve.tensor_tensor(y_lo[:, 4 * half:4 * half + 4, :], TR[1 - half][:].rearrange("p (k t) -> p k t", k=4),
                                          y_hi[:, 4 * half:4 * half + 4, :], ALU.subtract).then_inc(v_c.sem, 1)
                    dve.wait_ge(v_b.sem, v_b.after(k, "yun"))
                    if began(k - 1):
                        dve.wait_ge(a_c.sem, a_c.after(k - 1, "ev1"))
                    if isinstance(k, int) and k % NT == 0:
                        dve.wait_ge(v_w.sem, v_w.after(k // NT * NB + NB - 1, "lo3"))
                    dve.tensor_scalar(fac[:], unscale_out[:], y_unscale[:, 0:1], None, ALU.mult).then_inc(v_c.sem, 1)
                if b:
                    dve.wait_ge(params, 16 * N_PARAMS * (layer_of(j, layer) + 1))
                    dve.wait_ge(a_b.sem, a_b.after(j, "silu_a"))
                    dve.tensor_tensor(y[:, 0:GM], y[:, 0:GM], pj[:, C_U:C_U + GM], ALU.mult).then_inc(v_b.sem, 1)
                    dve.wait_ge(a_b.sem, a_b.after(j, "silu_b"))
                    y_gla = y[:, GM:GM + GLA].rearrange("p (h d) -> p h d", h=GH)
                    dve.tensor_tensor(y_gla, y_gla, norm_g[:].unsqueeze(1).broadcast_to([P, GH, HEAD]), ALU.mult).then_inc(v_b.sem, 1)
                splits(0)
                splits(1)
                if b:
                    dve.wait_ge(a_b.sem, a_b.after(j, "abs"))
                    if began(j - 1):
                        dve.wait_ge(v_b.sem, v_b.after(j - 1, "cum"))
                    dve.tensor_scalar(gate_m[:], GL[:, 0:P], gate_b[:, 0:1], 0.0, ALU.add, ALU.min).then_inc(v_b.sem, 1)
                    dve.wait_ge(v_b.sem, v_b.after(j, "min"))
                    dve.wait_ge(a_b.sem, a_b.after(j, "ln"))
                    dve.tensor_tensor(gate_m[:], gate_m[:], gate_a[:], ALU.subtract).then_inc(v_b.sem, 1)
                    dve.wait_ge(v_b.sem, v_b.after(j, "la"))
                    if began(j - 1):
                        dve.wait_ge(a_b.sem, a_b.after(j - 1, "kdec"))
                    dve.tensor_tensor_scan(cum[:], one[:, 0:1].broadcast_to([P, P]), gate_m[:], 0.0,
                                           ALU.mult, ALU.add).then_inc(v_b.sem, 1)
                    dve.wait_ge(v_b.sem, v_b.after(j, "cum"))
                    dve.tensor_scalar(ref_p[:, 0:NSUB], cum[:, SUB // 2 - 1::SUB], 1.0 / GATE_TAU, None, ALU.mult)
                    dve.tensor_scalar(ref_p[:, NSUB:NSUB + 1], cum[:, P - 1:P], 1.0 / GATE_TAU, None, ALU.mult).then_inc(v_b.sem, 1)
                    dve.wait_ge(v_b.sem, v_b.after(j, "refs"))
                    dve.tensor_scalar(ref_n[:], ref_p[:, 0:NSUB], -1.0, None, ALU.mult).then_inc(v_b.sem, 1)
                    dve.wait_ge(t_b.sem, t_b.after(j, "gm"))
                    if began(j - 1):
                        dve.wait_ge(v_b.sem, v_b.after(j - 1, "yb"))
                    mix4 = mix[:].rearrange("p (h d) -> p h d", h=GH)
                    mx4 = MX[:, 0:GM].rearrange("p (h d) -> p h d", h=GH)
                    dve.tensor_tensor(mix4, mx4, gm_bias[:].unsqueeze(2).broadcast_to([P, GH, HEAD]), ALU.add).then_inc(v_b.sem, 1)
                    dve.wait_ge(v_b.sem, v_b.after(j, "sv"))
                    dve.tensor_tensor(y[:, 0:GM], y[:, 0:GM], mix[:], ALU.mult).then_inc(v_b.sem, 1)
                    dve.wait_ge(a_b.sem, a_b.after(j, "kref"))
                    dve.tensor_tensor(k_ref[:], k_ref[:], g_qk[:, 1, :].unsqueeze(1).broadcast_to([P, NSUB, P]),
                                      ALU.mult).then_inc(v_b.sem, 1)
                    dve.wait_ge(a_b.sem, a_b.after(j, "qref"))
                    dve.scalar_tensor_tensor(q_ref[:], g_qk[:, 0, :], float(GK) ** -0.5, q_ref[:],
                                             ALU.mult, ALU.mult).then_inc(v_b.sem, 1)
                    dve.wait_ge(v_b.sem, v_b.after(j, "qref"))
                    if began(j - 1):
                        dve.wait_ge(t_b.sem, t_b.after(j - 1, "o"))
                    dve.tensor_tensor(
                        q_bd[:].rearrange("p (i h t) -> p i h t", i=NSUB, h=GH),
                        q_ref[:].rearrange("p (i t) -> p i t", i=NSUB).unsqueeze(2).broadcast_to([P, NSUB, GH, SUB]),
                        head_mask[:].unsqueeze(1).unsqueeze(3).broadcast_to([P, NSUB, GH, SUB]), ALU.mult).then_inc(v_b.sem, 1)
                    dve.wait_ge(a_b.sem, a_b.after(j, "decay"))
                    if began(j - 1):
                        dve.wait_ge(v_b.sem, v_b.after(j - 1, "state"))
                    dve.tensor_copy(tile_decay[:], decay[:, P - 1:P]).then_inc(v_b.sem, 1)
                    dve.wait_ge(v_b.sem, v_b.after(j, "dlast"))
                    dve.scalar_tensor_tensor(q_dec[:], g_qk[:, 0, :], float(GK) ** -0.5, decay[:],
                                             ALU.mult, ALU.mult).then_inc(v_b.sem, 1)
                    dve.wait_ge(a_b.sem, a_b.after(j, "kdec"))
                    dve.tensor_tensor(k_dec[:], k_dec[:], g_qk[:, 1, :], ALU.mult).then_inc(v_b.sem, 1)
                    dve.wait_ge(t_b.sem, t_b.after(j, "at"))
                    dve.tensor_tensor(
                        a_mask.rearrange("p h (i t) -> p i h t", i=NSUB),
                        GL[:].rearrange("p (i h t) -> p i h t", i=NSUB, h=GH),
                        causal[:].rearrange("p (i t) -> p i t", i=NSUB).unsqueeze(2).broadcast_to([P, NSUB, GH, SUB]),
                        ALU.mult).then_inc(v_b.sem, 1)
                splits(2)
                if b:
                    mask_max(0)
                if c:
                    dve.wait_ge(a_c.sem, a_c.after(k, "ev1"))
                    for h in range(2):
                        ins = dve.bn_stats(o_stats[:, h, :], ot[:, h * 512:(h + 1) * 512])
                    ins.then_inc(v_c.sem, 1)
                    dve.wait_ge(v_c.sem, v_c.after(k, "stats"))
                    before_aggregate(dve)
                    dve.bn_aggr(o_mv[:], o_stats[:]).then_inc(v_c.sem, 1)
                    dve.wait_ge(v_c.sem, v_c.after(k, "aggr"))
                    dve.scalar_tensor_tensor(o_mv[:, 1:2], o_mv[:, 0:1], o_mv[:, 0:1], o_mv[:, 1:2],
                                             ALU.mult, ALU.add).then_inc(v_c.sem, 1)
                    dve.wait_ge(v_c.sem, v_c.after(k, "msq"))
                    dve.tensor_scalar(o_mv[:, 0:1], o_mv[:, 1:2], EPS, None, ALU.add).then_inc(v_c.sem, 1)
                if b:
                    mask_max(1)
                    dve.tensor_copy(kT[:, :, 0, :], kT[:, :, 1, :]).then_inc(v_b.sem, 1)
                    dve.wait_ge(v_b.sem, v_b.after(j, "negm1"))
                    if began(j - 1):
                        dve.wait_ge(v_b.sem, v_b.after(j - 1, "den"))
                    dve.tensor_tensor(sink_e[:], sinks[:], neg_max[:], ALU.add).then_inc(v_b.sem, 1)
                if c:
                    dve.wait_ge(postg_loaded, 16 * (layer_of(k, layer) + 1))
                    dve.wait_ge(p_c.sem, p_c.after(k, "pow"))
                    dve.scalar_tensor_tensor(ot[:], ot[:], out_r[:, 0:1], postg[:], ALU.mult, ALU.mult).then_inc(v_c.sem, 1)
                    dve.wait_ge(v_c.sem, v_c.after(k, "post"))
                    dve.wait_ge(res_loaded, 16 * (k + 1))
                    dve.tensor_tensor(ot[:], ot[:], res[:], ALU.add).then_inc(v_c.sem, 1)
                if b:
                    if c:
                        dve.wait_ge(t_c.sem, t_c.after(k, "out1"))
                    for g in range(2):
                        dve.wait_ge(a_b.sem, a_b.after(j, "hi0" + "ab"[g]))
                        p_lo(g)
                if a:
                    dve.wait_ge(a_a.sem, a_a.after(n, "c1"))
                    if began(n - 1):
                        dve.wait_ge(v_l.sem, v_l.after(n - 1, "norm"))
                    dve.bn_stats(v_stats[:], pj[:, C_V:C_V + GM]).then_inc(v_l.sem, 1)
                    dve.wait_ge(v_l.sem, v_l.after(n, "stats"))
                    before_aggregate(dve)
                    dve.bn_aggr(v_mv[:], v_stats[:]).then_inc(v_l.sem, 1)
                    dve.wait_ge(v_l.sem, v_l.after(n, "aggr"))
                    if began(n - 1):
                        dve.wait_ge(p_l.sem, p_l.after(n - 1, "pow"))
                    dve.tensor_scalar(v_mv[:, 1:2], v_mv[:, 1:2], EPS, None, ALU.add).then_inc(v_l.sem, 1)
                splits(3)
                if a:
                    dve.wait_ge(params, 16 * N_PARAMS * (layer + 1))
                    dve.wait_ge(p_l.sem, p_l.after(n, "pow"))
                    dve.tensor_scalar(pj[:, C_V:C_V + GM], pj[:, C_V:C_V + GM], v_mv[:, 0:1], v_r[:, 0:1],
                                      ALU.subtract, ALU.mult).then_inc(v_l.sem, 1)
                    dve.wait_ge(v_l.sem, v_l.after(n, "norm"))
                    dve.tensor_tensor(pj[:, C_V:C_V + GM], pj[:, C_V:C_V + GM], ln_g[:], ALU.mult).then_inc(v_l.sem, 1)
                    dve.wait_ge(v_l.sem, v_l.after(n, "gain"))
                    dve.tensor_tensor(pj[:, C_V:C_V + GM], pj[:, C_V:C_V + GM], ln_b[:], ALU.add).then_inc(v_l.sem, 1)
                if b:
                    dve.wait_ge(a_b.sem, a_b.after(j, "sq"))
                    dve.tensor_tensor(update.rearrange("p (h d) -> p h d", h=GH),
                                      MX[:, GLA:2 * GLA].rearrange("p (h d) -> p h d", h=GH),
                                      head_mask[:].unsqueeze(2).broadcast_to([P, GH, HEAD]), ALU.mult).then_inc(v_b.sem, 1)
                    dve.wait_ge(v_b.sem, v_b.after(j, "um"))
                    dve.scalar_tensor_tensor(state[:], state[:], tile_decay[:, 0:1], update, ALU.mult, ALU.add).then_inc(v_b.sem, 1)
                    dve.wait_ge(a_b.sem, a_b.after(j, "sq"))
                    dve.tensor_reduce(o_sum[:], mix4, AX.X, ALU.add).then_inc(v_b.sem, 1)
                    dve.wait_ge(v_b.sem, v_b.after(j, "ored"))
                    dve.tensor_scalar(o_sum[:], o_sum[:], 1.0 / HEAD, EPS, ALU.mult, ALU.add).then_inc(v_b.sem, 1)
                    dve.wait_ge(p_b.sem, p_b.after(j, "o_pow"))
                    dve.tensor_tensor(mix4, mx4, o_r[:].unsqueeze(2).broadcast_to([P, GH, HEAD]), ALU.mult).then_inc(v_b.sem, 1)
                    dve.wait_ge(v_b.sem, v_b.after(j, "o1"))
                    dve.tensor_tensor(y[:, GM:GM + GLA], y[:, GM:GM + GLA], mix[:], ALU.mult).then_inc(v_b.sem, 1)
                splits(4)
                if x:
                    x_stats_of(n + 1)
                if b:
                    for g in range(2):
                        dve.wait_ge(a_b.sem, a_b.after(j, "hi1" + "ab"[g]))
                        p_lo(g)
                    dve.wait_ge(a_b.sem, a_b.after(j, "sink"))
                    dve.tensor_tensor(denom[:], row_sum[:], sink_e[:], ALU.add).then_inc(v_b.sem, 1)
                    dve.wait_ge(v_b.sem, v_b.after(j, "den"))
                    dve.tensor_scalar(denom[:], denom[:], v_scale[:, 0:1], P_SCALE, ALU.mult, ALU.mult).then_inc(v_b.sem, 1)
                    dve.wait_ge(v_b.sem, v_b.after(j, "sden"))
                    dve.reciprocal(denom[:], denom[:]).then_inc(v_b.sem, 1)
                splits(5)
                if i == 0 and a:
                    dve.wait_ge(gmw_t, layer + 1)
                    if layer:
                        dve.wait_ge(t_b.sem, t_b.after(layer * NT - 1, "gm"))
                    dve.tensor_tensor(gm_wT[:], MX[:].rearrange("p (h t) -> p h t", h=GH),
                                      causal[:].unsqueeze(1).broadcast_to([P, GH, P]), ALU.mult).then_inc(gmw_ready, 1)
                if x:
                    x_lo(n + 1)
                if b:
                    dve.wait_ge(t_b.sem, t_b.after(j, "pv1"))
                    dve.wait_ge(v_b.sem, v_b.after(j, "recip"))
                    dve.tensor_tensor(att.rearrange("p (h d) -> p h d", h=8), GL[:].rearrange("p (h d) -> p h d", h=8),
                                      denom[:].unsqueeze(2).broadcast_to([P, 8, HEAD]), ALU.mult).then_inc(v_b.sem, 1)
                    dve.tensor_copy(vv[:, :, 0, :], vv[:, :, 1, :]).then_inc(v_b.sem, 1)
                    dve.wait_ge(v_b.sem, v_b.after(j, "att"))
                    dve.wait_ge(a_b.sem, a_b.after(j, "silu_c"))
                    dve.tensor_tensor(y[:, GM + GLA:], y[:, GM + GLA:], att, ALU.mult).then_inc(v_b.sem, 1)
                    dve.wait_ge(v_b.sem, v_b.after(j, "yc"))
                    dve.tensor_reduce(y_max[:], y[:], AX.X, ALU.max, apply_absolute_value=True).then_inc(v_b.sem, 1)
                    dve.wait_ge(v_b.sem, v_b.after(j, "ymax"))
                    dve.tensor_scalar(y_max[:], y_max[:], TINY, None, ALU.max).then_inc(v_b.sem, 1)
                    dve.wait_ge(v_b.sem, v_b.after(j, "yguard"))
                    bits = y_max[:].bitcast(U32)
                    dve.tensor_scalar(bits, bits, EXP_BITS, None, ALU.bitwise_and).then_inc(v_b.sem, 1)
                    dve.wait_ge(v_b.sem, v_b.after(j, "ybits"))
                    if began(j - 1):
                        dve.wait_ge(a_b.sem, a_b.after(j - 1, "yscale"))
                    dve.reciprocal(y_scale[:], y_max[:]).then_inc(v_b.sem, 1)
                    dve.wait_ge(v_b.sem, v_b.after(j, "yrecip"))
                    dve.tensor_scalar(y_scale[:], y_scale[:], TOP, None, ALU.mult).then_inc(v_b.sem, 1)
                    if began(j - 1):
                        dve.wait_ge(v_c.sem, v_c.after(j - 1, "fac"))
                    dve.tensor_scalar(y_unscale[:], y_max[:], 1.0 / TOP, None, ALU.mult).then_inc(v_b.sem, 1)

                splits(6)

            run_pipeline(dve, iteration)

        @block.gpsimd
        def _(pool):
            own = sem("pool_constants")
            pool.memset(ident[:], 0.0)
            pool.memset(causal[:], 1.0)
            pool.memset(pool_one[:], 1.0)
            pool.memset(band[:], 0.0)
            pool.memset(head_mask[:], 1.0)
            pool.memset(k_ref[:], 0.0)
            pool.memset(neg_half[:], -0.5).then_inc(own, 1)
            pool.wait_ge(own, 1)
            pool.affine_select(out=ident[:], in_=ident[:], compare_op=ALU.not_equal, fill=1.0, base=0,
                               pattern=[[-1, P]], channel_multiplier=1)
            pool.affine_select(out=causal[:], in_=causal[:], compare_op=ALU.is_ge, fill=0.0, base=0,
                               pattern=[[1, P]], channel_multiplier=-1)
            pool.affine_select(out=band[:, P:2 * P], in_=band[:, P:2 * P], compare_op=ALU.is_gt, fill=NEG, base=0,
                               pattern=[[1, P]], channel_multiplier=-1)
            pool.affine_select(out=band[:, 2 * P:], in_=band[:, 2 * P:], compare_op=ALU.is_ge, fill=NEG, base=0,
                               pattern=[[-1, P]], channel_multiplier=1)
            pool.memset(band[:, 0:P], NEG)
            pool.affine_select(out=head_mask[:], in_=head_mask[:], compare_op=ALU.is_ge, fill=0.0, base=0,
                               pattern=[[-GK, GH]], channel_multiplier=1).then_inc(own, 1)
            pool.wait_ge(own, 2)
            pool.affine_select(out=head_mask[:], in_=head_mask[:], compare_op=ALU.is_ge, fill=0.0, base=GK - 1,
                               pattern=[[GK, GH]], channel_multiplier=-1)
            pool.tensor_copy(ident16[:], ident[:]).then_inc(const_ready, 1)
            pool.wait_ge(const_ready, 1)

            def x_pow(n):
                pool.wait_ge(v_x.sem, v_x.after(n, "eps"))
                if began(n - 1):
                    pool.wait_ge(a_x.sem, a_x.after(n - 1, "scale"))
                pool.tensor_tensor(x_r[:], x_mv[:, 0:1], neg_half[:, 0:1], ALU.pow).then_inc(p_x.sem, 1)

            def block_bound(layer, b):
                n = layer * NB + b
                side = slice(n % 2, n % 2 + 1)
                pool.wait_ge(a_m.sem, a_m.after(n, "sum"))
                pool.wait_ge(preg_ready, layer + 1)
                pool.tensor_tensor(part_bound[:, side], part_sum[:, side], (preg_top if b < N_WIN else pool_one)[:, 0:1],
                                   ALU.mult).then_inc(p_w.sem, 1)
                pool.wait_ge(p_w.sem, p_w.after(n, "gain"))
                if began(n - 2):
                    pool.wait_ge(v_s.sem, v_s.after(n - 2, "guard"))
                pool.partition_all_reduce(bound[:, side], part_bound[:, side], P, ABSMAX).then_inc(p_w.sem, 1)

            x_pow(0)
            for blk in range(N_FIRST + 2):
                block_bound(0, blk)

            def iteration(n, layer, a, b, c, x):
                j, k = n - 1, n - 2
                i = n % NT if isinstance(n, int) else None

                def splits(hook):
                    for l, blk in blocks_at(n, hook):
                        if starts_run(l, blk):
                            block_bound(l, blk)
                        for nxt in sums_after(l, blk):
                            block_bound(l, nxt)

                if i == 1 and a:
                    if began(j - 1):
                        pool.wait_ge(t_b.sem, t_b.after(j - 1, "pv1"))
                        pool.wait_ge(v_b.sem, v_b.after(j - 1, "vcopy"))
                        pool.wait_ge(v_b.sem, v_b.after(j - 1, "state"))
                    pool.memset(kT[:, :, 0, :], 0.0)
                    pool.memset(vv[:, :, 0, :], 0.0)
                    pool.memset(state[:], 0.0).then_inc(layer_state, 1)
                splits(0)
                splits(1)
                splits(2)
                if c:
                    pool.wait_ge(v_c.sem, v_c.after(k, "eps"))
                    if began(k - 1):
                        pool.wait_ge(v_c.sem, v_c.after(k - 1, "post"))
                    pool.tensor_tensor(out_r[:], o_mv[:, 0:1], neg_half[:, 0:1], ALU.pow).then_inc(p_c.sem, 1)
                if a:
                    pool.wait_ge(v_l.sem, v_l.after(n, "eps"))
                    if began(n - 1):
                        pool.wait_ge(v_l.sem, v_l.after(n - 1, "norm"))
                    pool.tensor_tensor(v_r[:], v_mv[:, 1:2], neg_half[:, 0:1], ALU.pow).then_inc(p_l.sem, 1)
                splits(3)
                if b:
                    pool.wait_ge(v_b.sem, v_b.after(j, "oeps"))
                    pool.tensor_tensor(o_r[:], o_sum[:], neg_half[:], ALU.pow).then_inc(p_b.sem, 1)
                splits(4)
                if x:
                    x_pow(n + 1)
                splits(5)
                splits(6)

            run_pipeline(pool, iteration)


_INS = ["x", "positions", "pre_g", "w_in", "gm_ln_g", "gm_ln_b", "gm_ws", "gm_bs", "gla_wg2", "gla_bg",
        "gla_norm_g", "swa_sinks", "w_out", "post_g"]


def kernel(**inputs):
    import concourse.bacc as _bacc
    from concourse.bass_utils import run_bass_kernel_spmd as _run

    nc = _bacc.Bacc("TRN2", target_bir_lowering=False, num_devices=1)
    arrays = {n: np.ascontiguousarray(inputs[n]) for n in _INS}
    arrays["x"] = arrays["x"].reshape(SEQ, D_MODEL)
    arrays["inv_freq"] = (ROPE_THETA ** (-np.arange(HEAD // 2) * 2.0 / HEAD)).astype(np.float32).reshape(1, -1)
    aps = [nc.dram_tensor("in_" + n, a.shape, mybir.dt.from_np(a.dtype), kind="ExternalInput").ap()
           for n, a in arrays.items()]
    out = nc.dram_tensor("out_y", (SEQ, D_MODEL), F32, kind="ExternalOutput").ap()
    hybrid_trunk(nc, *aps, out)
    r = _run(nc, [{"in_" + n: a for n, a in arrays.items()}], core_ids=[0])
    return r.results[0]["out_y"].reshape(1, SEQ, D_MODEL)
```
